# Optimizing a Trainium2 kernel written in Bass

```python
import numpy as np
import jax, jax.numpy as jnp
from jax import lax

D_MODEL = 1024
BATCH = 1
SEQ = 256
DEPTH = 2

HEAD_DIM = 64
N_A_LAYERS = DEPTH // 2
N_B_LAYERS = DEPTH - N_A_LAYERS
MEM_LEN = 256
MEM_HEADS = 4
MEM_W = MEM_HEADS * HEAD_DIM
CONV_W = D_MODEL - MEM_W
CONV_K = 31
NSA_HEADS = (D_MODEL - MEM_W) // HEAD_DIM
NSA_W = NSA_HEADS * HEAD_DIM
NSA_KV_GROUPS = 2
HEADS_PER_GROUP = NSA_HEADS // NSA_KV_GROUPS
CMP_L = 32
CMP_STRIDE = 16
CMP_HID = 256
SEL_L = 64
N_SEL = 16
WIN = 512
Q_BLOCK = 128
D_FF = 4 * D_MODEL
KV_W = 6 * NSA_KV_GROUPS * HEAD_DIM
A_IN_W = 2 * CONV_W + MEM_W
B_IN_W = NSA_W + MEM_W + 3 * NSA_HEADS


def rms_norm(x, g, eps=1e-6):
    xf = x.astype(jnp.float32)
    y = xf * lax.rsqrt(jnp.mean(xf * xf, axis=-1, keepdims=True) + eps)
    return (y * g.astype(jnp.float32)).astype(x.dtype)

def layer_norm(x, g, b, eps=1e-5):
    xf = x.astype(jnp.float32)
    mu = jnp.mean(xf, axis=-1, keepdims=True)
    var = jnp.mean(jnp.square(xf - mu), axis=-1, keepdims=True)
    y = (xf - mu) * lax.rsqrt(var + eps)
    return (y * g.astype(jnp.float32) + b.astype(jnp.float32)).astype(x.dtype)

def masked_softmax(s, mask):
    s = jnp.where(mask, s.astype(jnp.float32), -jnp.inf)
    m = jnp.max(s, axis=-1, keepdims=True)
    m = jnp.where(jnp.isfinite(m), m, 0.0)
    e = jnp.exp(s - m)
    return e / jnp.maximum(jnp.sum(e, axis=-1, keepdims=True), 1e-30)

def selection_map(n_cmp, n_sb):
    cs = np.arange(n_cmp)[:, None] * CMP_STRIDE
    ss = np.arange(n_sb)[None, :] * SEL_L
    ov = np.minimum(cs + CMP_L, ss + SEL_L) - np.maximum(cs, ss)
    return (np.clip(ov, 0, None) / CMP_STRIDE).astype(np.float32)

def squared_relu_mlp(h, w_in, w_out):
    return jnp.square(jax.nn.relu(h @ w_in)) @ w_out

def memory_attention(q, mk, mv):
    B, S = q.shape[:2]
    s = jnp.einsum('bshd,bmhd->bhsm', q, mk) * HEAD_DIM ** -0.5
    p = jax.nn.softmax(s.astype(jnp.float32), axis=-1)
    return jnp.einsum('bhsm,bmhd->bshd', p.astype(mv.dtype), mv).reshape(B, S, MEM_W)

def conformer_conv(u, dw, dw_b, ln_g, ln_b):
    a, gate = jnp.split(u, 2, axis=-1)
    v = a * jax.nn.sigmoid(gate)
    v = lax.conv_general_dilated(v, dw[:, None, :], window_strides=(1,),
                                 padding=[(CONV_K - 1, 0)],
                                 dimension_numbers=('NWC', 'WIO', 'NWC'),
                                 feature_group_count=CONV_W) + dw_b
    return jax.nn.silu(layer_norm(v, ln_g, ln_b))

def shared_nsa_kv(h, kv_norm_g, w_kv, k_norm_g, pe_k, pe_v, w1_k, w2_k, w1_v, w2_v):
    B, S = h.shape[:2]
    G, HD = NSA_KV_GROUPS, HEAD_DIM
    kv = (rms_norm(h, kv_norm_g) @ w_kv).reshape(B, S, 6, G, HD)
    k_c, v_c, k_s, v_s, k_w, v_w = (kv[:, :, i] for i in range(6))
    n_cmp = (S - CMP_L) // CMP_STRIDE + 1
    idx = np.arange(n_cmp)[:, None] * CMP_STRIDE + np.arange(CMP_L)[None, :]

    def compress(t, pe, w1, w2):
        blk = t[:, idx] + pe[:, None, :]
        blk = blk.transpose(0, 1, 3, 2, 4).reshape(B, n_cmp, G, CMP_L * HD)
        return jax.nn.gelu(blk @ w1) @ w2

    k_cmp = rms_norm(compress(k_c, pe_k, w1_k, w2_k), k_norm_g[0])
    v_cmp = compress(v_c, pe_v, w1_v, w2_v)
    n_sb = S // SEL_L
    k_blk = rms_norm(k_s, k_norm_g[1]).reshape(B, n_sb, SEL_L, G, HD).transpose(0, 3, 1, 2, 4)
    v_blk = v_s.reshape(B, n_sb, SEL_L, G, HD).transpose(0, 3, 1, 2, 4)
    pad = ((0, 0), (WIN, 0), (0, 0), (0, 0))
    k_win = jnp.pad(rms_norm(k_w, k_norm_g[2]), pad)
    v_win = jnp.pad(v_w, pad)
    return k_cmp, v_cmp, k_blk, v_blk, k_win, v_win

def nsa_attention(q, gates, k_cmp, v_cmp, k_blk, v_blk, k_win, v_win):
    B, S = q.shape[:2]
    G, HG, HD = NSA_KV_GROUPS, HEADS_PER_GROUP, HEAD_DIM
    n_qb = S // Q_BLOCK
    n_cmp = k_cmp.shape[1]
    n_sb = k_blk.shape[2]
    n_sel = min(N_SEL, n_sb)
    scale = HD ** -0.5
    cmp_end = jnp.asarray(np.arange(n_cmp) * CMP_STRIDE + CMP_L - 1)
    sel_map = jnp.asarray(selection_map(n_cmp, n_sb))
    blk_ids = jnp.arange(n_sb)
    b_ix = jnp.arange(B)[:, None, None, None]
    g_ix = jnp.arange(G)[None, None, :, None]
    qs = q.reshape(B, n_qb, Q_BLOCK, G, HG, HD).transpose(1, 0, 2, 3, 4, 5)
    gs = gates.reshape(B, n_qb, Q_BLOCK, G, HG, 3).transpose(1, 0, 2, 3, 4, 5)

    def block(args):
        c, qb, gb = args
        t = c * Q_BLOCK + jnp.arange(Q_BLOCK)
        s = jnp.einsum('bqghd,bngd->bqghn', qb, k_cmp) * scale
        p_cmp = masked_softmax(s, (cmp_end[None, :] <= t[:, None])[None, :, None, None, :])
        o_cmp = jnp.einsum('bqghn,bngd->bqghd', p_cmp.astype(v_cmp.dtype), v_cmp)
        imp = jnp.einsum('bqgn,nj->bqgj', jnp.sum(p_cmp, axis=3), sel_map)
        tb = (t // SEL_L)[:, None]
        valid = (blk_ids[None, :] <= tb)[None, :, None, :]
        forced = ((blk_ids[None, :] == 0) | (blk_ids[None, :] == tb)
                  | (blk_ids[None, :] == tb - 1))[None, :, None, :]
        score = jnp.where(forced, jnp.inf, jnp.where(valid, imp, -jnp.inf))
        top_val, top_idx = lax.top_k(score, n_sel)
        kg = k_blk[b_ix, g_ix, top_idx]
        vg = v_blk[b_ix, g_ix, top_idx]
        pos = top_idx[..., None] * SEL_L + jnp.arange(SEL_L)
        smask = (top_val > -jnp.inf)[..., None] & (pos <= t[None, :, None, None, None])
        s = jnp.einsum('bqghd,bqgnkd->bqghnk', qb, kg) * scale
        n_tok = n_sel * SEL_L
        p = masked_softmax(s.reshape(B, Q_BLOCK, G, HG, n_tok),
                           smask.reshape(B, Q_BLOCK, G, 1, n_tok))
        o_slc = jnp.einsum('bqghm,bqgmd->bqghd', p.astype(vg.dtype),
                           vg.reshape(B, Q_BLOCK, G, n_tok, HD))
        kw = lax.dynamic_slice_in_dim(k_win, c * Q_BLOCK, Q_BLOCK + WIN, axis=1)
        vw = lax.dynamic_slice_in_dim(v_win, c * Q_BLOCK, Q_BLOCK + WIN, axis=1)
        kp = c * Q_BLOCK - WIN + jnp.arange(Q_BLOCK + WIN)
        wmask = (kp[None, :] <= t[:, None]) & (kp[None, :] > t[:, None] - WIN) & (kp[None, :] >= 0)
        s = jnp.einsum('bqghd,bkgd->bqghk', qb, kw) * scale
        p = masked_softmax(s, wmask[None, :, None, None, :])
        o_win = jnp.einsum('bqghk,bkgd->bqghd', p.astype(vw.dtype), vw)
        o = o_cmp * gb[..., 0:1] + o_slc * gb[..., 1:2] + o_win * gb[..., 2:3]
        return o.reshape(B, Q_BLOCK, NSA_W)

    out = lax.map(block, (jnp.arange(n_qb), qs, gs))
    return out.transpose(1, 0, 2, 3).reshape(B, S, NSA_W)

def first_inputs(seed: int = 0) -> dict:
    key = jax.random.key(seed)
    ks = iter(jax.random.split(key, 32))

    def w(shape, fan_in):
        return jax.random.normal(next(ks), shape, jnp.float32) * fan_in ** -0.5

    def gain(shape):
        return 1.0 + 0.1 * jax.random.normal(next(ks), shape, jnp.float32)

    def bias(shape):
        return 0.01 * jax.random.normal(next(ks), shape, jnp.float32)

    return {
        'x': jax.random.normal(next(ks), (BATCH, SEQ, D_MODEL), jnp.float32),
        'mem': jax.random.normal(next(ks), (BATCH, MEM_LEN, D_MODEL), jnp.float32),
        'norm_mix_g': gain((DEPTH, D_MODEL)),
        'norm_mlp_g': gain((DEPTH, D_MODEL)),
        'mem_norm_g': gain((D_MODEL,)),
        'w_mem_kv': w((DEPTH, D_MODEL, 2 * MEM_W), D_MODEL),
        'mem_q_norm_g': gain((DEPTH, HEAD_DIM)),
        'mem_k_norm_g': gain((DEPTH, HEAD_DIM)),
        'w_out': w((DEPTH, D_MODEL, D_MODEL), D_MODEL),
        'w_mlp_in': w((DEPTH, D_MODEL, D_FF), D_MODEL),
        'w_mlp_out': w((DEPTH, D_FF, D_MODEL), D_FF),
        'a_w_in': w((N_A_LAYERS, D_MODEL, A_IN_W), D_MODEL),
        'a_b_glu': bias((N_A_LAYERS, 2 * CONV_W)),
        'a_dw': w((N_A_LAYERS, CONV_K, CONV_W), CONV_K),
        'a_dw_b': bias((N_A_LAYERS, CONV_W)),
        'a_ln_g': gain((N_A_LAYERS, CONV_W)),
        'a_ln_b': bias((N_A_LAYERS, CONV_W)),
        'b_w_in': w((N_B_LAYERS, D_MODEL, B_IN_W), D_MODEL),
        'b_gate_b': bias((N_B_LAYERS, 3 * NSA_HEADS)),
        'b_q_norm_g': gain((N_B_LAYERS, HEAD_DIM)),
        'kv_norm_g': gain((D_MODEL,)),
        'w_kv': w((D_MODEL, KV_W), D_MODEL),
        'k_norm_g': gain((3, HEAD_DIM)),
        'cmp_pe_k': 0.1 * jax.random.normal(next(ks), (CMP_L, HEAD_DIM), jnp.float32),
        'cmp_pe_v': 0.1 * jax.random.normal(next(ks), (CMP_L, HEAD_DIM), jnp.float32),
        'cmp_w1_k': w((CMP_L * HEAD_DIM, CMP_HID), CMP_L * HEAD_DIM),
        'cmp_w2_k': w((CMP_HID, HEAD_DIM), CMP_HID),
        'cmp_w1_v': w((CMP_L * HEAD_DIM, CMP_HID), CMP_L * HEAD_DIM),
        'cmp_w2_v': w((CMP_HID, HEAD_DIM), CMP_HID),
    }

def first_block(x, mem, norm_mix_g, norm_mlp_g, mem_norm_g, w_mem_kv, mem_q_norm_g, mem_k_norm_g,
              w_out, w_mlp_in, w_mlp_out, a_w_in, a_b_glu, a_dw, a_dw_b, a_ln_g, a_ln_b,
              b_w_in, b_gate_b, b_q_norm_g, kv_norm_g, w_kv, k_norm_g, cmp_pe_k, cmp_pe_v,
              cmp_w1_k, cmp_w2_k, cmp_w1_v, cmp_w2_v):
    B, S = x.shape[:2]
    mem_n = rms_norm(mem, mem_norm_g)
    shared = None
    for l in range(DEPTH):
        mkv = (mem_n @ w_mem_kv[l]).reshape(B, MEM_LEN, 2, MEM_HEADS, HEAD_DIM)
        mk = rms_norm(mkv[:, :, 0], mem_k_norm_g[l])
        mv = mkv[:, :, 1]
        h = rms_norm(x, norm_mix_g[l])
        if l == N_A_LAYERS:
            shared = shared_nsa_kv(x, kv_norm_g, w_kv, k_norm_g, cmp_pe_k, cmp_pe_v,
                                   cmp_w1_k, cmp_w2_k, cmp_w1_v, cmp_w2_v)
        if l < N_A_LAYERS:
            i = l
            u = h @ a_w_in[i]
            conv_out = conformer_conv(u[..., :2 * CONV_W] + a_b_glu[i], a_dw[i], a_dw_b[i],
                                      a_ln_g[i], a_ln_b[i])
            qm = rms_norm(u[..., 2 * CONV_W:].reshape(B, S, MEM_HEADS, HEAD_DIM), mem_q_norm_g[l])
            mix = jnp.concatenate([conv_out, memory_attention(qm, mk, mv)], axis=-1)
        else:
            i = l - N_A_LAYERS
            u = h @ b_w_in[i]
            q = rms_norm(u[..., :NSA_W].reshape(B, S, NSA_HEADS, HEAD_DIM), b_q_norm_g[i])
            qm = rms_norm(u[..., NSA_W:NSA_W + MEM_W].reshape(B, S, MEM_HEADS, HEAD_DIM),
                          mem_q_norm_g[l])
            gates = jax.nn.sigmoid(u[..., NSA_W + MEM_W:] + b_gate_b[i]).reshape(B, S, NSA_HEADS, 3)
            nsa_out = nsa_attention(q, gates, *shared)
            mix = jnp.concatenate([nsa_out, memory_attention(qm, mk, mv)], axis=-1)
        x = x + mix @ w_out[l]
        x = x + squared_relu_mlp(rms_norm(x, norm_mlp_g[l]), w_mlp_in[l], w_mlp_out[l])
    return x


DEPTH_2 = 1

SB_HEADS = 8
SB_HEAD_DIM = 64
MLA_HEADS = 8
QK_NOPE_DIM = 64
QK_ROPE_DIM = 32
V_HEAD_DIM = 64
Q_LORA_RANK = 256
KV_LORA_RANK = 128
SB_WIDTH = SB_HEADS * SB_HEAD_DIM
MLA_WIDTH = MLA_HEADS * V_HEAD_DIM
D_MIX = SB_WIDTH + MLA_WIDTH
IN_COLS = 3 * SB_WIDTH + Q_LORA_RANK + KV_LORA_RANK + QK_ROPE_DIM
D_FF_2 = 2816
CONV_WIDTH = 3
PLE_DIM = 256
ROPE_THETA = 10000.0
NORM_EPS = 1e-6
MAX_POS_OFFSET = 4096


def rms_norm_2(x, gain):
    xf = x.astype(jnp.float32)
    y = xf * lax.rsqrt(jnp.mean(xf * xf, axis=-1, keepdims=True) + NORM_EPS)
    return (y * gain.astype(jnp.float32)).astype(x.dtype)

def rope_tables(positions, dtype):
    inv_freq = 1.0 / (ROPE_THETA ** (jnp.arange(0, QK_ROPE_DIM, 2, dtype=jnp.float32) / QK_ROPE_DIM))
    ang = positions.astype(jnp.float32)[..., None] * inv_freq
    return jnp.cos(ang).astype(dtype), jnp.sin(ang).astype(dtype)

def apply_rope(x, cos, sin):
    x1, x2 = jnp.split(x, 2, axis=-1)
    return jnp.concatenate([x1 * cos - x2 * sin, x2 * cos + x1 * sin], axis=-1)

def stick_breaking_attention(q, k, v):
    seq = q.shape[1]
    scale = SB_HEAD_DIM ** -0.5
    outs = []
    for start in range(0, seq, Q_BLOCK):
        end = start + Q_BLOCK
        z = jnp.einsum('bqhd,bkhd->bhqk', q[:, start:end], k[:, :end]).astype(jnp.float32) * scale
        t_idx = start + jnp.arange(Q_BLOCK)[:, None]
        s_idx = jnp.arange(end)[None, :]
        strict = s_idx < t_idx
        log_keep = jnp.where(strict, -jax.nn.softplus(z), 0.0)
        log_keep_after = lax.cumsum(log_keep, axis=3, reverse=True) - log_keep
        weights = jnp.where(strict, jnp.exp(jax.nn.log_sigmoid(z) + log_keep_after), 0.0)
        outs.append(jnp.einsum('bhqk,bkhd->bqhd', weights.astype(v.dtype), v[:, :end]))
    return jnp.concatenate(outs, axis=1)

def mla_attention(q_nope, q_rope, k_nope, k_rope, v):
    seq = q_nope.shape[1]
    scale = (QK_NOPE_DIM + QK_ROPE_DIM) ** -0.5
    outs = []
    for start in range(0, seq, Q_BLOCK):
        end = start + Q_BLOCK
        s = (jnp.einsum('bqhd,bkhd->bhqk', q_nope[:, start:end], k_nope[:, :end])
             + jnp.einsum('bqhd,bkd->bhqk', q_rope[:, start:end], k_rope[:, :end]))
        s = s.astype(jnp.float32) * scale
        causal = jnp.arange(end)[None, :] <= (start + jnp.arange(Q_BLOCK)[:, None])
        probs = jax.nn.softmax(jnp.where(causal, s, -jnp.inf), axis=-1)
        outs.append(jnp.einsum('bhqk,bkhd->bqhd', probs.astype(v.dtype), v[:, :end]))
    return jnp.concatenate(outs, axis=1)

def causal_depthwise_conv(u, w, b):
    c = u.shape[-1]
    y = lax.conv_general_dilated(u, w[:, None, :].astype(u.dtype), window_strides=(1,),
                                 padding=[(CONV_WIDTH - 1, 0)],
                                 dimension_numbers=('NWC', 'WIO', 'NWC'),
                                 feature_group_count=c)
    return y + b.astype(u.dtype)

def second_inputs(seed: int = 0) -> dict:
    key = jax.random.key(seed)
    ks = jax.random.split(key, 24)
    f32 = jnp.float32

    def normal(k, shape, scale):
        return jax.random.normal(k, shape, f32) * scale

    def gain(k, shape):
        return 1.0 + 0.05 * jax.random.normal(k, shape, f32)

    L = DEPTH_2
    x = normal(ks[0], (BATCH, SEQ, D_MODEL), 1.0)
    p = normal(ks[1], (DEPTH_2, BATCH, SEQ, PLE_DIM), 1.0)
    offsets = jax.random.randint(ks[2], (BATCH, 1), 0, MAX_POS_OFFSET, dtype=jnp.int32)
    positions = offsets + jnp.arange(SEQ, dtype=jnp.int32)[None, :]
    return {
        'x': x,
        'p': p,
        'positions': positions,
        'w_in': normal(ks[3], (L, D_MODEL, IN_COLS), D_MODEL ** -0.5),
        'g_pre_mix': gain(ks[4], (L, D_MODEL)),
        'g_q_lat': gain(ks[5], (L, Q_LORA_RANK)),
        'w_q_up': normal(ks[6], (L, Q_LORA_RANK, MLA_HEADS * (QK_NOPE_DIM + QK_ROPE_DIM)), Q_LORA_RANK ** -0.5),
        'g_kv_lat': gain(ks[7], (L, KV_LORA_RANK)),
        'w_kv_up': normal(ks[8], (L, KV_LORA_RANK, MLA_HEADS * (QK_NOPE_DIM + V_HEAD_DIM)), KV_LORA_RANK ** -0.5),
        'g_grp_sb': gain(ks[9], (L, SB_WIDTH)),
        'g_grp_mla': gain(ks[10], (L, MLA_WIDTH)),
        'w_o': normal(ks[11], (L, D_MIX, D_MODEL), D_MIX ** -0.5),
        'g_post_mix': gain(ks[12], (L, D_MODEL)),
        'g_pre_ffn': gain(ks[13], (L, D_MODEL)),
        'w_up': normal(ks[14], (L, D_MODEL, 2 * D_FF_2), D_MODEL ** -0.5),
        'conv_w': normal(ks[15], (L, CONV_WIDTH, 2 * D_FF_2), CONV_WIDTH ** -0.5),
        'conv_b': normal(ks[16], (L, 2 * D_FF_2), 0.01),
        'w_down': normal(ks[17], (L, D_FF_2, D_MODEL), D_FF_2 ** -0.5),
        'g_post_ffn': gain(ks[18], (L, D_MODEL)),
        'w_ple': normal(ks[19], (L, PLE_DIM, D_MODEL), PLE_DIM ** -0.5),
        'g_ple_gate': gain(ks[20], (L, D_MODEL)),
        'w_ple_gate': normal(ks[21], (L, D_MODEL, D_MODEL), D_MODEL ** -0.5),
        'b_ple_gate': normal(ks[22], (L, D_MODEL), 0.01),
        'g_post_ple': gain(ks[23], (L, D_MODEL)),
    }

def second_block(x, p, positions, w_in, g_pre_mix, g_q_lat, w_q_up, g_kv_lat, w_kv_up,
              g_grp_sb, g_grp_mla, w_o, g_post_mix, g_pre_ffn, w_up, conv_w, conv_b,
              w_down, g_post_ffn, w_ple, g_ple_gate, w_ple_gate, b_ple_gate, g_post_ple):
    b, s, _ = x.shape
    cos, sin = rope_tables(positions, x.dtype)
    split_at = [SB_WIDTH, 2 * SB_WIDTH, 3 * SB_WIDTH,
                3 * SB_WIDTH + Q_LORA_RANK, 3 * SB_WIDTH + Q_LORA_RANK + KV_LORA_RANK]
    for i in range(DEPTH_2):
        h = rms_norm_2(x, g_pre_mix[i])
        proj = h @ w_in[i]
        sb_q, sb_k, sb_v, q_lat, kv_lat, k_rope = jnp.split(proj, split_at, axis=-1)

        o_sb = stick_breaking_attention(sb_q.reshape(b, s, SB_HEADS, SB_HEAD_DIM),
                                        sb_k.reshape(b, s, SB_HEADS, SB_HEAD_DIM),
                                        sb_v.reshape(b, s, SB_HEADS, SB_HEAD_DIM)).reshape(b, s, SB_WIDTH)

        q = (rms_norm_2(q_lat, g_q_lat[i]) @ w_q_up[i]).reshape(b, s, MLA_HEADS, QK_NOPE_DIM + QK_ROPE_DIM)
        q_nope, q_rope = jnp.split(q, [QK_NOPE_DIM], axis=-1)
        q_rope = apply_rope(q_rope, cos[:, :, None, :], sin[:, :, None, :])
        kv = (rms_norm_2(kv_lat, g_kv_lat[i]) @ w_kv_up[i]).reshape(b, s, MLA_HEADS, QK_NOPE_DIM + V_HEAD_DIM)
        k_nope, v_mla = jnp.split(kv, [QK_NOPE_DIM], axis=-1)
        k_rope = apply_rope(k_rope, cos, sin)
        o_mla = mla_attention(q_nope, q_rope, k_nope, k_rope, v_mla).reshape(b, s, MLA_WIDTH)

        mix = jnp.concatenate([rms_norm_2(o_sb, g_grp_sb[i]), rms_norm_2(o_mla, g_grp_mla[i])], axis=-1) @ w_o[i]
        x = x + rms_norm_2(mix, g_post_mix[i])

        h = rms_norm_2(x, g_pre_ffn[i])
        u = causal_depthwise_conv(h @ w_up[i], conv_w[i], conv_b[i])
        gate, val = jnp.split(u, 2, axis=-1)
        f = (jax.nn.gelu(gate, approximate=True) * val) @ w_down[i]
        x = x + rms_norm_2(f, g_post_ffn[i])

        e = p[i] @ w_ple[i]
        g = jax.nn.sigmoid(rms_norm_2(x, g_ple_gate[i]) @ w_ple_gate[i] + b_ple_gate[i])
        x = x + rms_norm_2(g * e, g_post_ple[i])
    return x


def setup_inputs(seed=0):
    out = dict(first_inputs(seed))
    for name, value in second_inputs(seed + 1).items():
        if name != "x":
            out[name + "_2"] = value
    return out


def reference(
    x, mem, norm_mix_g, norm_mlp_g, mem_norm_g, w_mem_kv, mem_q_norm_g, mem_k_norm_g, w_out,
    w_mlp_in, w_mlp_out, a_w_in, a_b_glu, a_dw, a_dw_b, a_ln_g, a_ln_b, b_w_in, b_gate_b,
    b_q_norm_g, kv_norm_g, w_kv, k_norm_g, cmp_pe_k, cmp_pe_v, cmp_w1_k, cmp_w2_k, cmp_w1_v,
    cmp_w2_v, p_2, positions_2, w_in_2, g_pre_mix_2, g_q_lat_2, w_q_up_2, g_kv_lat_2, w_kv_up_2,
    g_grp_sb_2, g_grp_mla_2, w_o_2, g_post_mix_2, g_pre_ffn_2, w_up_2, conv_w_2, conv_b_2,
    w_down_2, g_post_ffn_2, w_ple_2, g_ple_gate_2, w_ple_gate_2, b_ple_gate_2, g_post_ple_2,
):
    x = first_block(
        x, mem, norm_mix_g, norm_mlp_g, mem_norm_g, w_mem_kv, mem_q_norm_g, mem_k_norm_g, w_out,
        w_mlp_in, w_mlp_out, a_w_in, a_b_glu, a_dw, a_dw_b, a_ln_g, a_ln_b, b_w_in, b_gate_b,
        b_q_norm_g, kv_norm_g, w_kv, k_norm_g, cmp_pe_k, cmp_pe_v, cmp_w1_k, cmp_w2_k, cmp_w1_v,
        cmp_w2_v,
    )
    return second_block(
        x, p_2, positions_2, w_in_2, g_pre_mix_2, g_q_lat_2, w_q_up_2, g_kv_lat_2, w_kv_up_2,
        g_grp_sb_2, g_grp_mla_2, w_o_2, g_post_mix_2, g_pre_ffn_2, w_up_2, conv_w_2, conv_b_2,
        w_down_2, g_post_ffn_2, w_ple_2, g_ple_gate_2, w_ple_gate_2, b_ple_gate_2, g_post_ple_2,
    )


_drawn_inputs = setup_inputs


def setup_inputs(seed=0):
    import zlib

    import numpy as np

    out = dict(_drawn_inputs(seed))
    spreads = {}
    factors = {'mem_norm_g': 6.416,
     'mem_q_norm_g': 8.0,
     'mem_k_norm_g': 8.0,
     'a_b_glu': 8.0,
     'a_dw_b': 4.307,
     'a_ln_b': 8.0,
     'b_gate_b': 35.692,
     'b_q_norm_g': 6.946,
     'k_norm_g': 7.826,
     'cmp_pe_k': 8.0,
     'cmp_pe_v': 3.367,
     'g_q_lat_2': 8.0,
     'g_kv_lat_2': 3.636,
     'g_grp_sb_2': 12.443,
     'g_grp_mla_2': 11.003,
     'g_post_mix_2': 2.67,
     'conv_b_2': 8.0,
     'g_post_ffn_2': 2.979,
     'g_ple_gate_2': 7.978,
     'b_ple_gate_2': 64.0,
     'g_post_ple_2': 3.126}
    for name, (base, spread) in spreads.items():
        noise = np.random.default_rng([zlib.crc32(name.encode()), seed]).standard_normal(out[name].shape)
        drawn = base * np.exp(spread * noise) if base else spread * noise
        out[name] = __import__('jax').numpy.asarray(drawn.astype(out[name].dtype))
    for name, factor in factors.items():
        out[name] = (out[name] * factor).astype(out[name].dtype)
    return out
```

```python
import math
from contextlib import ExitStack

import numpy as np

import concourse.bass as bass
from concourse import mybir

F32 = mybir.dt.float32
BF16 = mybir.dt.bfloat16
I32 = mybir.dt.int32
ALU = mybir.AluOpType
ACT = mybir.ActivationFunctionType
X_AXIS = mybir.AxisListType.X

SEQ = 256
KD = 8
TT = SEQ // 128
BLOCK_COLS = 2048
RING = 8
NPS = 6
FF_TILES = 32
UP_PAIRS = 22
CONV_TILES = 6
TAPS = 31
PAD = TAPS - 1
QK_SCALE = 64 ** -0.5
MLA_SCALE = 96 ** -0.5
ROUNDER = 1.5 * 2.0 ** 23
SIN_LIMIT = 3.1415925


def pi_parts(value):
    parts = []
    for bits in (8, 8):
        scale = 2.0 ** (bits - math.floor(math.log2(value)))
        parts.append(math.floor(value * scale) / scale)
        value -= parts[-1]
    return parts + [float(np.float32(value))]


def weight_blocks():
    out = []

    def add(name, rows, columns, width=256):
        for c in range(0, columns, width):
            for r in range(0, rows, KD):
                out.append((name, r, min(KD, rows - r), c, min(width, columns - c)))

    add("a_in", KD, 1792)
    add("mem_kv0", KD, 512)
    add("mem_kv1", KD, 512)
    add("out0", KD, 1024)
    add("mlp_in0", KD, 4096)
    add("mlp_out0", FF_TILES, 1024)
    add("kv", KD, 768)
    add("cmp_k", 16, 256)
    add("cmp_v", 16, 256)
    add("b_in", KD, 1024)
    add("gates", KD, 36)
    add("out1", KD, 1024)
    add("mlp_in1", KD, 4096)
    add("mlp_out1", FF_TILES, 1024)
    add("s_in", KD, 1792)
    add("s_lat", KD, 256)
    add("q_up", 2, 768, 768)
    add("kv_up", 1, 1024, 1024)
    add("o", KD, 1024)
    add("ple", 2, 1024, 1024)
    add("up", KD, 5632)
    add("down", UP_PAIRS, 1024)
    add("ple_gate", KD, 1024)
    return out


WEIGHT_BLOCKS = weight_blocks()
NBLOCKS = len(WEIGHT_BLOCKS)
FIRST_BLOCK = {}
for _n, _b in enumerate(WEIGHT_BLOCKS):
    FIRST_BLOCK.setdefault(_b[0], _n)

CONSTS = [
    ("g_mix0", 8), ("g_mix1", 8), ("g_mlp0", 8), ("g_mlp1", 8), ("g_memq0", 1), ("g_memq1", 1), ("g_memk0", 1),
    ("g_memk1", 1), ("g_mem", 8), ("b_glu", 12), ("dw", 186), ("dw_b", 6), ("ln_g", 6), ("ln_b", 6), ("g_kv", 8),
    ("b_gate", 1), ("g_bq", 1), ("g_k", 3), ("pe_k", 32), ("pe_v", 32), ("w2_k", 256), ("w2_v", 128),
    ("g_smix", 8), ("g_qlat", 2), ("g_kvlat", 1), ("g_sb", 4), ("g_mla", 4), ("g_postmix", 8), ("g_ffn", 8),
    ("g_postffn", 8), ("g_plegate", 8), ("b_plegate", 8), ("g_postple", 8), ("conv_b", 44), ("conv_w", 132),
    ("ident", 128), ("ones", 128), ("headsel", 2), ("halfones", 128), ("swap", 96), ("invf", 1), ("eps6", 1),
    ("eps5", 1), ("cbias", 128), ("sbias", 128), ("smask", 384), ("negtri", 128), ("negones", 128),
    ("cmpbias", 32), ("headblock", 6),
]
CONST_AT = {}
NCONST = 0
for _name, _width in CONSTS:
    CONST_AT[_name] = (NCONST, _width)
    NCONST += _width


class Unit:

    def __init__(self, branch, tt, heads, outs, group, first, last):
        self.branch, self.tt, self.heads, self.outs = branch, tt, heads, outs
        self.group, self.first, self.last = group, first, last
        self.keys = SEQ if branch == "mem" else 128 * (tt + 1)


def attention_units(kind):
    units = []

    def group(branch, tt, runs, base):
        for n, heads in enumerate(runs):
            units.append(Unit(branch, tt, heads, [h - base for h in heads], (kind, branch, tt, base),
                              n == 0, n == len(runs) - 1))

    if kind in ("mem0", "mem1"):
        for tt in range(TT):
            group("mem", tt, [(0, 2), (1, 3)], 0)
    elif kind == "nsa":
        for tt in range(TT):
            for base in (0, 6):
                even, odd = tuple(range(base, base + 6, 2)), tuple(range(base + 1, base + 6, 2))
                runs = [even, odd] if tt == 0 else [even[:2], odd[:2], even[2:], odd[2:]]
                for branch in ("slc", "win"):
                    group(branch, tt, runs, base)
    else:
        for tt in range(TT):
            step = 4 if tt == 0 else 2
            group("mla", tt, [tuple(range(h, h + step)) for h in range(0, 8, step)], 0)
    return units


ATTENTIONS = ("mem0", "mem1", "nsa", "mla")
UNITS = {kind: attention_units(kind) for kind in ATTENTIONS}
FIRST_UNIT = {}
_n = 0
for _kind in ATTENTIONS:
    FIRST_UNIT[_kind] = _n
    _n += len(UNITS[_kind])
STAT_COL = {}
_n = 0
for _kind in ATTENTIONS:
    for _u, _unit in enumerate(UNITS[_kind]):
        STAT_COL[_kind, _u] = _n
        _n += len(_unit.heads)
NSTAT = _n


def psum_tiles():
    out = []

    def linear(stage, n, first=0):
        out.extend((stage, t) for t in range(first, first + n))

    def attention(kind):
        n = len(UNITS[kind])
        for w in range(n + 2):
            if w < n:
                out.append((kind, "S", w))
            if 1 <= w <= n:
                out.append((kind, "T", w - 1))

    linear("mem.stat", 1)
    linear("mix0.stat", 1)
    linear("mix0.bc", 1)
    linear("a_in", 4)
    linear("mem.bc", 1)
    linear("a_in", 10, 4)
    linear("qm0.stat", 1)
    linear("mem_kv0", 4)
    linear("qm0.bc", 1)
    linear("mk0.stat", 1)
    linear("mem_kv1", 4)
    linear("mk0.bc", 1)
    linear("mk1.stat", 1)
    linear("mk1.bc", 1)
    attention("mem0")
    linear("mem0.oT", 2)
    linear("ln.mean", 1)
    linear("ln.var", 1)
    linear("out0", 8)
    linear("mlp0.stat", 1)
    linear("mlp0.bc", 1)
    linear("mlp_in0", 32)
    linear("mlp_out0", 8)
    linear("mix1.stat", 1)
    linear("mix1.bc", 1)
    linear("kv", 6)
    linear("ks.stat", 1)
    linear("cmp_k", 2)
    linear("ks.bc", 1)
    linear("cmp_v", 2)
    linear("kc", 1)
    linear("vc", 2)
    linear("b_in", 8)
    linear("kc.norm", 1)
    linear("bq.stat", 1)
    linear("gates", 1)
    linear("bq.bc", 4)
    linear("gatesT", 1)
    attention("mem1")
    linear("mem1.oT", 2)
    for tt in range(TT):
        for g in range(2):
            out += [("cmp.S", 2 * (2 * tt + g) + odd) for odd in range(2)]
    for tt in range(TT):
        for g in range(2):
            out.append(("cmp.T", 2 * tt + g))
    attention("nsa")
    linear("nsa.oT", 4)
    linear("out1", 8)
    linear("mlp1.stat", 1)
    linear("mlp1.bc", 1)
    linear("mlp_in1", 32)
    linear("mlp_out1", 8)
    linear("smix.stat", 1)
    linear("smix.bc", 1)
    linear("s_in", 14)
    linear("s_lat", 2)
    linear("qlat.stat", 1)
    linear("kvlat.stat", 1)
    linear("qlat.bc", 1)
    linear("kvlat.bc", 1)
    linear("krope.swap", 1)
    for w in range(8 + 1):
        if w < 8:
            out.append(("sb.Z", w))
        if w >= 1:
            out.append(("sb.W", w - 1))
    linear("sb.stat", 1)
    linear("q_up", 8)
    linear("q.swap", 4)
    linear("k_up", 8)
    linear("v_up", 2)
    linear("sb.bc", 1)
    attention("mla")
    linear("mla.oT", 2)
    linear("o", 8)
    linear("postmix.stat", 1)
    linear("postmix.bc", 1)
    linear("ple", 8)
    linear("ffn.stat", 1)
    linear("ffn.bc", 1)
    linear("up", 2 * UP_PAIRS)
    linear("down", 8)
    linear("postffn.stat", 1)
    linear("postffn.bc", 1)
    linear("plegate.stat", 1)
    linear("plegate.bc", 1)
    linear("ple_gate", 8)
    linear("postple.stat", 1)
    linear("postple.bc", 1)
    return out


TILE = {name: n for n, name in enumerate(psum_tiles())}


def output_groups():
    out = []
    for kind in ("mem0", "mem1"):
        out += [u.group for u in UNITS[kind] if u.last]
    out += [("cmp", tt, g) for tt in range(TT) for g in range(2)]
    out += [u.group for u in UNITS["nsa"] if u.last]
    out += [("sb", pair) for pair in range(4)]
    out += [u.group for u in UNITS["mla"] if u.last]
    return out


def block_releases():
    rows = {}
    for name, r, kts, _, _ in WEIGHT_BLOCKS:
        rows[name] = max(rows.get(name, 0), r + kts)
    out, partial = [], 0
    last = {"gates": ("gates", 0), "q_up": ("q_up", 7), "kv_up": ("v_up", 1), "ple": ("ple", 7)}
    for name, r, kts, c, width in WEIGHT_BLOCKS:
        if r + kts == rows[name]:
            out.append(("psum_ready", TILE[last.get(name, (name, 2 * (c // 256) + 1))] + 1))
        else:
            partial += 1
            out.append(("weights_used", partial))
    return out


BLOCK_RELEASES = block_releases()
OUT = {name: n for n, name in enumerate(output_groups())}


def build(nc, x_in, mem_in, p_in, pos_in, consts_in, weights_in, out):
    ctx = ExitStack()
    with ctx:
        def sb(name, shape, dt=F32):
            return ctx.enter_context(nc.sbuf_tensor(name, shape, dt))

        semaphores = {}

        def sem(name):
            if name not in semaphores:
                semaphores[name] = ctx.enter_context(nc.semaphore(name.replace(".", "_")))
            return semaphores[name]

        def flatten(t):
            return t[:, :, :].rearrange("p a b -> p (a b)")

        C = sb("consts", [128, NCONST])
        ring = sb("ring", [128, RING, BLOCK_COLS])
        x = sb("x", [128, KD, SEQ])
        xg = sb("xg", [128, KD, SEQ])
        xg2 = sb("xg2", [128, KD, SEQ])
        y = sb("y", [128, KD, SEQ])
        sq = sb("sq", [128, KD, SEQ])
        hidden = sb("hidden", [128, FF_TILES, SEQ])
        mix = sb("mix", [128, KD, SEQ])
        q = sb("q", [128, KD, SEQ])
        probs = sb("probs", [128, 2, 512])
        probsT = sb("probsT", [128, 2, 512])
        otok = sb("otok", [128, TT, 768])
        memk = sb("memk", [128, 2, 2, SEQ])
        memv = sb("memv", [128, 2, TT, 256])
        kd = sb("kd", [128, 2, 2, SEQ])
        vsw = sb("vsw", [128, TT, 256])
        smalls = sb("smalls", [128, 64])
        rc = sb("rc", [128, 64])
        rb = sb("rb", [128, SEQ])
        negmax = sb("negmax", [128, NSTAT])
        rowmax = sb("rowmax", [128, NSTAT])
        rowsum = sb("rowsum", [128, NSTAT])
        rowinv = sb("rowinv", [128, 16])
        tmp = sb("tmp", [128, 2, 512])
        tmp2 = sb("tmp2", [128, 2, 512])
        ident_b = sb("ident_b", [128, 128], BF16)
        cbias_b = sb("cbias_b", [128, 128], BF16)
        sbias_b = sb("sbias_b", [128, 128], BF16)
        gate_tok = sb("gate_tok", [128, TT, 36])

        hid = hidden[:, :, :].rearrange("p a b -> p (a b)")
        glu = hid[:, 0:CONV_TILES * (SEQ + PAD)].rearrange("p (c t) -> p c t", c=CONV_TILES)
        conv = hid[:, 2048:2048 + 1536].rearrange("p (c t) -> p c t", c=CONV_TILES)
        conv2 = hid[:, 4096:4096 + 1536].rearrange("p (c t) -> p c t", c=CONV_TILES)
        tkv = hid[:, 0:544].rearrange("p (a t) -> p a t", a=2)
        windows = hid[:, 1024:2048].rearrange("p (a l n) -> p a l n", a=2, l=16)
        cmph = hid[:, 2048:2176].rearrange("p (a c n) -> p a c n", a=2, c=2)
        cmph6 = hid[:, 2304:2304 + 384].rearrange("p (c g j n) -> p c g j n", c=2, g=2, j=6)
        vbd = hid[:, 3072:3840].rearrange("p (g d) -> p g d", g=2)
        kcmp = hid[:, 3840:3872]
        kraw = hid[:, 3872:3904]
        krms = hid[:, 3904:4000]
        cmps = hid[:, 4096:4096 + 4 * 96].rearrange("p (u n) -> p u n", u=4)
        cmpp = hid[:, 4608:4608 + 4 * 96].rearrange("p (u n) -> p u n", u=4)
        cmppT = hid[:, 5120:5120 + 4 * 128].rearrange("p (u n) -> p u n", u=4)
        gates = hid[:, 5632:5888]
        ksraw = hid[:, 6144:6656].rearrange("p (a t) -> p a t", a=2)
        sbv = hid[:, 0:1024].rearrange("p (a n) -> p a n", a=2)
        qcat = hid[:, 1024:3072].rearrange("p (h t) -> p h t", h=8)
        kcat = hid[:, 3072:5120].rearrange("p (h t) -> p h t", h=8)
        vmla = hid[:, 5120:6144].rearrange("p (a n) -> p a n", a=2)
        lat = hid[:, 6144:6144 + 768].rearrange("p (a t) -> p a t", a=3)
        cosT = hid[:, 6912:7168]
        sinT = hid[:, 7168:7424]
        krope = hid[:, 7424:7680]
        latn = hid[:, 7680:7680 + 512].rearrange("p (a t) -> p a t", a=2)
        kvn = mix[:, 7, :]
        sp = xg2[:, 0:3, :].rearrange("p a b -> p (a b)").rearrange("p (s n) -> p s n", s=2)
        wt = xg2[:, 3:6, :].rearrange("p a b -> p (a b)").rearrange("p (s n) -> p s n", s=2)
        osb = y[:, 0:4, :]
        zt = y[:, 4:7, :].rearrange("p a b -> p (a b)").rearrange("p (s n) -> p s n", s=2)
        padded = flatten(y)[:, 0:4 * (SEQ + 2)].rearrange("p (s t) -> p s t", s=4)
        slots = flatten(tmp).rearrange("p (s t) -> p s t", s=4)
        slots2 = flatten(tmp2).rearrange("p (s t) -> p s t", s=4)
        pT = sb("pT", [128, 2, SEQ])
        pos = sb("pos", [128, SEQ], I32)

        banks = [ctx.enter_context(nc.psum_tensor(f"bank{n}", [128, 512], F32)) for n in range(NPS)]
        obanks = [ctx.enter_context(nc.psum_tensor(f"obank{n}", [128, 512], F32)) for n in range(2)]

        def const(name, a=0, n=None):
            at, width = CONST_AT[name]
            return C[:, at + a:at + (width if n is None else a + n)]

        def bank(*tile):
            return banks[TILE[tile] % NPS]

        def wait_tile(eng, *tile):
            eng.wait_ge(sem("psum_ready"), TILE[tile] + 1)

        def emptied(*tile):
            return sem(f"bank_emptied{TILE[tile] % NPS}")

        def wait_emptied(eng, *tile):
            eng.wait_ge(emptied(*tile), TILE[tile] // NPS + 1)

        def obank(name):
            return obanks[OUT[name] % 2]

        def wait_out(eng, name):
            eng.wait_ge(sem("out_ready"), OUT[name] + 1)

        def out_emptied(name):
            return sem(f"obank_emptied{OUT[name] % 2}")

        def wait_out_emptied(eng, name):
            eng.wait_ge(out_emptied(name), OUT[name] // 2 + 1)

        def flat(ap):
            return ap.rearrange("p a b -> p (a b)")

        def bcast(ap, n):
            return ap.unsqueeze(2).to_broadcast([ap.shape[0], ap.shape[1], n])

        def rows(ap, n):
            return ap.unsqueeze(1).to_broadcast([ap.shape[0], n, ap.shape[1]])

        RC = {"mem": 0, "mix0": 2, "mlp0": 4, "mix1": 6, "mlp1": 8, "smix": 10, "postmix": 12, "ffn": 14,
              "postffn": 16, "plegate": 18, "postple": 20, "qlat": 22, "kvlat": 24, "sb": 26, "mla": 28,
              "qm0": 32, "mk0": 32, "mk1": 32, "ks": 32, "bq": 32}
        HEAD_NORMS = {"qm0": 2, "mk0": 2, "mk1": 2, "ks": 2, "bq": 8}

        block = ctx.enter_context(nc.Block())

        @block.sync
        def _(sp_):
            def load(b):
                _, _, kts, _, width = WEIGHT_BLOCKS[b]
                sp_.dma_start(ring[:, b % RING, 0:kts * width], weights_in[b, :, 0:kts * width])\
                   .then_inc(sem(f"weights_in{b % RING}"), 16)

            for b in range(NBLOCKS):
                if b >= RING:
                    name, count = BLOCK_RELEASES[b - RING]
                    sp_.wait_ge(sem(name), count)
                load(b)
            sp_.wait_ge(sem("result"), KD)
            sp_.dma_start(out, flat(x[:, :, :])).then_inc(sem("stored"), 16)
            sp_.wait_ge(sem("stored"), 16)

        @block.tensor
        def _(pe):
            def take(*tile):
                n = TILE[tile]
                if n >= NPS:
                    pe.wait_ge(sem(f"bank_emptied{n % NPS}"), n // NPS)
                return banks[n % NPS]

            def mm(dst, lhsT, rhs, start=True, stop=True):
                return nc.tensor.matmul(dst, lhsT, rhs, start=start, stop=stop)

            def ready(last):
                last.then_inc(sem("psum_ready"), 1)

            def block_ready(b):
                pe.wait_ge(sem(f"weights_in{b % RING}"), 16 * (b // RING + 1))
                _, _, kts, _, width = WEIGHT_BLOCKS[b]
                return ring[:, b % RING, 0:kts * width].rearrange("p (k c) -> p k c", k=kts), kts

            def linear_pair(stage, t, act, b, nblocks=1):
                k0 = 0
                total = sum(WEIGHT_BLOCKS[b + n][2] for n in range(nblocks))
                dst = None
                for n in range(nblocks):
                    w, kts = block_ready(b + n)
                    if dst is None:
                        dst = [None, None]
                    for c in range(2):
                        if dst[c] is None:
                            dst[c] = take(stage, t + c)
                        for k in range(kts):
                            last = mm(dst[c][0:128, 0:SEQ], w[:, k, 128 * c:128 * c + 128], act[:, k0 + k, :],
                                      k0 + k == 0, k0 + k == total - 1)
                        if k0 + kts == total:
                            ready(last)
                    k0 += kts
                    if k0 < total:
                        last.then_inc(sem("weights_used"), 1)

            def linear_tokens(stage, t, act, b, c0=0, width=256):
                w, kts = block_ready(b)
                for tt in range(TT):
                    dst = take(stage, t + tt)
                    for k in range(kts):
                        last = mm(dst[:, 0:width], act[:, k, 128 * tt:128 * tt + 128], w[:, k, c0:c0 + width],
                                  k == 0, k == kts - 1)
                    ready(last)

            def full_stat(name, nt, src=None, signal=None):
                src = sq if src is None else src
                pe.wait_ge(sem(f"{name}.squares"), nt if signal is None else signal)
                dst = take(f"{name}.stat", 0)
                for tt in range(TT):
                    for k in range(nt):
                        last = mm(dst[:, tt:tt + 1], src[:, k, 128 * tt:128 * tt + 128], const("ones", 0, 1),
                                  k == 0, k == nt - 1)
                ready(last)

            def full_bcast(name):
                pe.wait_ge(sem(f"{name}.rc"), 1)
                dst = take(f"{name}.bc", 0)
                for tt in range(TT):
                    c = RC[name] + tt
                    last = mm(dst[:, 128 * tt:128 * tt + 128], rc[:, c:c + 1].to_broadcast([128, 128]), const("ident"))
                ready(last)

            def head_stat(name):
                nt = HEAD_NORMS[name]
                pe.wait_ge(sem(f"{name}.squares"), 1)
                dst = take(f"{name}.stat", 0)
                for tt in range(TT):
                    for k in range(nt):
                        c = tt * 2 * nt + 2 * k
                        last = mm(dst[:, c:c + 2], sq[:, k, 128 * tt:128 * tt + 128], const("headsel"))
                ready(last)

            def head_bcast(name):
                nt = HEAD_NORMS[name]
                pe.wait_ge(sem(f"{name}.rc"), 1)
                for pair in range(nt // 2):
                    dst = take(f"{name}.bc", pair)
                    for k in (2 * pair, 2 * pair + 1):
                        for tt in range(TT):
                            c = RC[name] + tt * 2 * nt + 2 * k
                            at = (k % 2) * SEQ + 128 * tt
                            for i in range(2):
                                last = mm(dst[64 * i:64 * i + 64, at:at + 128],
                                          rc[:, c + i:c + i + 1].to_broadcast([128, 64]), const("ident"))
                    ready(last)

            def transpose(dst, src):
                k = src.shape[0]
                return nc.tensor.transpose(dst, src, const("ident")[0:k, 0:k])

            def operands(u, h):
                tok = slice(128 * u.tt, 128 * u.tt + 128)
                half = slice(64 * (h % 2), 64 * (h % 2) + 64)
                return tok, half

            def scores(kind, u, n):
                if n == 0 and kind == "nsa":
                    wait_emptied(pe, "kv", 4)
                    wait_emptied(pe, "kv", 5)
                dst = take(kind, "S", n)
                for i, h in enumerate(u.heads):
                    tok, half = operands(u, h)
                    if kind in ("mem0", "mem1"):
                        a = q[half, (6 if kind == "mem1" else 0) + h // 2, tok]
                        b = memk[half, int(kind[3]), h // 2, 0:u.keys]
                    elif kind == "nsa":
                        a = q[half, h // 2, tok]
                        b = kd[half, 0 if u.branch == "slc" else 1, h // 6, 0:u.keys]
                    else:
                        a = qcat[0:96, h, tok]
                        b = kcat[0:96, h, 0:u.keys]
                    masked = u.branch != "mem"
                    last = mm(dst[:, i * u.keys:(i + 1) * u.keys], a, b, True, not masked)
                    if masked:
                        at = i * u.keys + 128 * u.tt
                        last = mm(dst[:, at:at + 128], ident_b[:, :], cbias_b[:, :], False, True)
                ready(last)

            def probs_transposed(kind, u, n):
                slot = (FIRST_UNIT[kind] + n) % 2
                wait_emptied(pe, kind, "S", n)
                dst = take(kind, "T", n)
                for i in range(len(u.heads) * u.keys // 128):
                    last = transpose(dst[:, 128 * i:128 * i + 128], probs[:, slot, 128 * i:128 * i + 128])
                ready(last)

            def outputs(kind, u, n):
                slot = (FIRST_UNIT[kind] + n) % 2
                wait_emptied(pe, kind, "T", n)
                o = OUT[u.group]
                if u.first and o >= 2:
                    pe.wait_ge(out_emptied(u.group), o // 2)
                dst = obank(u.group)
                nk = u.keys // 128
                for i, h in enumerate(u.heads):
                    for k in range(nk):
                        if u.branch == "mem":
                            v = memv[:, int(kind[3]), k, 64 * h:64 * h + 64]
                        elif kind == "nsa":
                            c = (0 if u.branch == "slc" else 128) + 64 * (h // 6)
                            v = vsw[:, k, c:c + 64]
                        else:
                            v = vmla[:, k, 64 * h:64 * h + 64]
                        at = 64 * u.outs[i]
                        c = 128 * (i * nk + k)
                        last = mm(dst[:, at:at + 64], probsT[:, slot, c:c + 128], v, k == 0, k == nk - 1)
                if u.last:
                    last.then_inc(sem("out_ready"), 1)

            def attention(kind):
                units = UNITS[kind]
                for w in range(len(units) + 2):
                    if w < len(units):
                        scores(kind, units[w], w)
                    if 1 <= w <= len(units):
                        probs_transposed(kind, units[w - 1], w - 1)
                    if w >= 2:
                        outputs(kind, units[w - 2], w - 2)

            def blocks_of(name):
                return FIRST_BLOCK[name]

            def linear(stage, act, npairs, nblocks=1, tile0=0, first=0):
                for j in range(first, npairs):
                    linear_pair(stage, tile0 + 2 * j, act, blocks_of(stage) + j * nblocks, nblocks)

            pe.wait_ge(sem("consts_in"), 16)
            full_stat("mem", KD, src=y, signal=1)
            full_stat("mix0", KD, signal=1)
            full_bcast("mix0")
            pe.wait_ge(sem("mix0.xg"), 1)
            linear("a_in", xg, 2)
            full_bcast("mem")
            linear("a_in", xg, 7, first=2)
            head_stat("qm0")
            for l in range(2):
                if l == 0:
                    wait_emptied(pe, "mem.bc", 0)
                linear_pair(f"mem_kv{l}", 0, xg2, blocks_of(f"mem_kv{l}"))
                linear_tokens(f"mem_kv{l}", 2, xg2, blocks_of(f"mem_kv{l}") + 1)
                if l == 0:
                    head_bcast("qm0")
                    head_stat("mk0")
                else:
                    head_bcast("mk0")
                    head_stat("mk1")
            head_bcast("mk1")
            for stage in ("qm0.bc", "mk0.bc", "mk1.bc"):
                wait_emptied(pe, stage, 0)
            for l in range(2):
                for t in (2, 3):
                    wait_emptied(pe, f"mem_kv{l}", t)
            attention("mem0")

            def mem_out_transposed(kind):
                for tt in range(TT):
                    pe.wait_ge(sem(f"{kind}.o"), tt + 1)
                    dst = take(f"{kind}.oT", tt)
                    for i in range(2):
                        last = transpose(dst[:, 128 * i:128 * i + 128], otok[:, tt, 128 * i:128 * i + 128])
                    ready(last)

            mem_out_transposed("mem0")
            pe.wait_ge(sem("conv.done"), CONV_TILES)
            dst = take("ln.mean", 0)
            for c in range(CONV_TILES):
                last = mm(dst[:, 0:SEQ], const("ones"), conv[:, c, :], c == 0, c == CONV_TILES - 1)
            ready(last)
            pe.wait_ge(sem("ln.squares"), 1)
            dst = take("ln.var", 0)
            for c in range(CONV_TILES):
                last = mm(dst[:, 0:SEQ], const("ones"), sq[:, c, :], c == 0, c == CONV_TILES - 1)
            ready(last)
            pe.wait_ge(sem("mix0.mixed"), CONV_TILES)
            wait_emptied(pe, "mem0.oT", 1)
            linear("out0", mix, 4)

            def mlp(l):
                full_stat(f"mlp{l}", KD)
                full_bcast(f"mlp{l}")
                pe.wait_ge(sem(f"mlp{l}.xg"), KD)
                linear(f"mlp_in{l}", xg, FF_TILES // 2)
                pe.wait_ge(sem(f"mlp{l}.hidden"), FF_TILES)
                linear(f"mlp_out{l}", hidden, KD // 2, FF_TILES // KD)

            mlp(0)
            full_stat("mix1", KD)
            full_bcast("mix1")
            pe.wait_ge(sem("kv.xg"), KD)
            linear("kv", xg2, 2)
            linear_tokens("kv", 4, xg2, blocks_of("kv") + 2)
            head_stat("ks")

            def compress(n, a):
                pe.wait_ge(sem(f"windows_{n}"), 1)
                b = blocks_of(f"cmp_{n}")
                dst = [take(f"cmp_{n}", c) for c in range(2)]
                for half in range(2):
                    w, kts = block_ready(b + half)
                    for c in range(2):
                        for k in range(kts):
                            last = mm(dst[c][:, 0:32], w[:, k, 128 * c:128 * c + 128], windows[:, a, 8 * half + k, :],
                                      half + k == 0, half == 1 and k == kts - 1)
                        if half == 1:
                            ready(last)
                    if half == 0:
                        last.then_inc(sem("weights_used"), 1)

            compress("k", 0)
            head_bcast("ks")
            compress("v", 1)
            wait_emptied(pe, "cmp_k", 1)
            dst = take("kc", 0)
            w2k = const("w2_k").rearrange("p (k c) -> p k c", k=2)
            for k in range(2):
                last = mm(dst[:, 0:32], w2k[:, k, :], cmph[:, 0, k, :], k == 0, k == 1)
            ready(last)
            pe.wait_ge(sem("cmph6"), 1)
            w2v = const("w2_v").rearrange("p (k c) -> p k c", k=2)
            for g in range(2):
                dst = take("vc", g)
                for k in range(2):
                    last = mm(dst[0:96, 0:64], cmph6[:, k, g, :, :].rearrange("p j n -> p (j n)"), w2v[:, k, :], k == 0, k == 1)
                ready(last)
            pe.wait_ge(sem("mix1.xg"), KD)
            linear("b_in", xg, 4)
            pe.wait_ge(sem("kc.squares"), 1)
            dst = take("kc.norm", 0)
            ready(mm(dst[:, 0:32], const("halfones"), krms[:, 0:32]))
            head_stat("bq")
            b = blocks_of("gates")
            w, kts = block_ready(b)
            dst = take("gates", 0)
            for k in range(kts):
                last = mm(dst[0:36, 0:SEQ], w[:, k, 0:36], xg[:, k, :], k == 0, k == kts - 1)
            ready(last)
            head_bcast("bq")
            pe.wait_ge(sem("gates.sigmoid"), 1)
            dst = take("gatesT", 0)
            for tt in range(TT):
                last = transpose(dst[:, 36 * tt:36 * tt + 36], gates[0:36, 128 * tt:128 * tt + 128])
            ready(last)
            for pair in range(4):
                wait_emptied(pe, "bq.bc", pair)
            attention("mem1")
            mem_out_transposed("mem1")
            pe.wait_ge(sem("kcmp"), 1)
            for n in range(4):
                tt, g = n // 2, n % 2
                for odd in range(2):
                    dst = take("cmp.S", 2 * n + odd)
                    half = slice(64 * odd, 64 * odd + 64)
                    for i in range(3):
                        last = mm(dst[:, 16 * i:16 * i + 16], q[half, 3 * g + i, 128 * tt:128 * tt + 128],
                                  kcmp[half, 16 * g:16 * g + 16])
                    ready(last)
            for n in range(4):
                pe.wait_ge(sem("cmp.probs"), 1)
                ready(transpose(take("cmp.T", n)[0:96, 0:128], cmpp[:, n, :]))
            for g in range(2):
                wait_emptied(pe, "vc", g)
            for n in range(4):
                tt, g = n // 2, n % 2
                wait_emptied(pe, "cmp.T", n)
                o = OUT["cmp", tt, g]
                if o >= 2:
                    pe.wait_ge(out_emptied(("cmp", tt, g)), o // 2)
                mm(obank(("cmp", tt, g))[:, 0:384], cmppT[0:96, n, :], vbd[0:96, g, :]).then_inc(sem("out_ready"), 1)
            wait_emptied(pe, "ks.bc", 0)
            attention("nsa")
            for n in range(4):
                tt, g = n // 2, n % 2
                pe.wait_ge(sem("nsa.o"), n + 1)
                dst = take("nsa.oT", n)
                for i in range(3):
                    c = 384 * g + 128 * i
                    last = transpose(dst[:, 128 * i:128 * i + 128], otok[:, tt, c:c + 128])
                ready(last)
            for n in range(4):
                wait_emptied(pe, "nsa.oT", n)
            for tt in range(TT):
                wait_emptied(pe, "mem1.oT", tt)
            linear("out1", mix, 4)
            mlp(1)
            full_stat("smix", KD)
            full_bcast("smix")
            pe.wait_ge(sem("smix.xg"), KD)
            linear("s_in", xg, 4)
            for j in range(2):
                linear_tokens("s_in", 8 + 2 * j, xg, blocks_of("s_in") + 4 + j)
            linear("s_in", xg, 7, first=6)
            b = blocks_of("s_lat")
            w, kts = block_ready(b)
            for c, m in ((0, 128), (1, 96)):
                dst = take("s_lat", c)
                for k in range(kts):
                    last = mm(dst[0:m, 0:SEQ], w[:, k, 128 * c:128 * c + m], xg[:, k, :], k == 0, k == kts - 1)
                ready(last)
            full_stat("qlat", 2, signal=1)
            full_stat("kvlat", 1, src=sq[:, 2:3, :], signal=1)
            full_bcast("qlat")
            full_bcast("kvlat")
            wait_emptied(pe, "s_lat", 1)
            dst = take("krope.swap", 0)
            ready(mm(dst[0:96, 0:SEQ], const("swap")[64:96, :], krope[64:96, :]))

            def z_products(dst, h, stop):
                half = slice(64 * (h % 2), 64 * (h % 2) + 64)
                kk, qq = q[half, 4 + h // 2, :], q[half, h // 2, :]
                mm(dst[:, 0:256], kk[:, 0:128], qq[:, 0:256], True, stop)
                return kk, qq

            def sb_scores(h):
                dst = take("sb.Z", h)
                kk, qq = z_products(dst, h, True)
                ready(mm(dst[:, 256:384], kk[:, 128:256], qq[:, 128:256]))

            def sb_weights(h):
                pe.wait_ge(sem("sb.log_keep"), h + 1)
                dst = take("sb.W", h)
                L = sp[:, h % 2, :]
                kk, qq = z_products(dst, h, False)
                mm(dst[:, 0:256], const("negtri"), L[:, 0:256], False, False)
                mm(dst[:, 128:256], const("negones"), L[:, 256:384], False, False)
                mm(dst[:, 0:128], ident_b[:, :], sbias_b[:, :], False, True)
                mm(dst[:, 256:384], kk[:, 128:256], qq[:, 128:256], True, False)
                mm(dst[:, 256:384], const("negtri"), L[:, 256:384], False, False)
                ready(mm(dst[:, 256:384], ident_b[:, :], sbias_b[:, :], False, True))

            def sb_outputs(h):
                wait_emptied(pe, "sb.W", h)
                o = OUT["sb", h // 2]
                if h % 2 == 0 and o >= 2:
                    pe.wait_ge(out_emptied(("sb", h // 2)), o // 2)
                dst = obank(("sb", h // 2))[64 * (h % 2):64 * (h % 2) + 64, :]
                W = wt[:, h % 2, :]
                mm(dst[:, 0:256], sbv[:, 0, 64 * h:64 * h + 64], W[:, 0:256], True, False)
                last = mm(dst[:, 128:256], sbv[:, 1, 64 * h:64 * h + 64], W[:, 256:384], False, True)
                if h % 2:
                    last.then_inc(sem("out_ready"), 1)

            wait_emptied(pe, "s_in", 11)
            for w_ in range(10):
                if w_ < 8:
                    sb_scores(w_)
                if 1 <= w_ <= 8:
                    sb_weights(w_ - 1)
                if w_ >= 2:
                    sb_outputs(w_ - 2)
            full_stat("sb", 4)
            wait_emptied(pe, "qlat.bc", 0)
            b = blocks_of("q_up")
            w, kts = block_ready(b)
            for h in range(8):
                dst = take("q_up", h)
                for k in range(2):
                    last = mm(dst[0:96, 0:SEQ], w[:, k, 96 * h:96 * h + 96], latn[:, k, :], k == 0, k == 1)
                ready(last)
            for j in range(4):
                wait_emptied(pe, "q_up", 2 * j)
                wait_emptied(pe, "q_up", 2 * j + 1)
                dst = take("q.swap", j)
                for i in range(2):
                    last = mm(dst[0:96, SEQ * i:SEQ * i + SEQ], const("swap")[64:96, :], qcat[64:96, 2 * j + i, :])
                ready(last)
            wait_emptied(pe, "kvlat.bc", 0)
            b = blocks_of("kv_up")
            w, kts = block_ready(b)
            for h in range(8):
                ready(mm(take("k_up", h)[0:64, 0:SEQ], w[:, 0, 128 * h:128 * h + 64], kvn))
            wv = w[:, 0, :].rearrange("p (h c) -> p h c", h=8)[:, :, 64:128]
            for tt in range(TT):
                ready(mm(take("v_up", tt)[:, :].rearrange("p (h c) -> p h c", h=8), kvn[:, 128 * tt:128 * tt + 128], wv))
            full_bcast("sb")
            pe.wait_ge(sem("qcat"), 4)
            pe.wait_ge(sem("kcat"), 1)
            wait_emptied(pe, "k_up", 7)
            wait_emptied(pe, "v_up", 0)
            wait_emptied(pe, "v_up", 1)
            attention("mla")
            for tt in range(TT):
                pe.wait_ge(sem("mla.o"), tt + 1)
                dst = take("mla.oT", tt)
                for i in range(4):
                    last = transpose(dst[:, 128 * i:128 * i + 128], otok[:, tt, 128 * i:128 * i + 128])
                ready(last)
            wait_emptied(pe, "sb.bc", 0)
            wait_emptied(pe, "mla.oT", 0)
            wait_emptied(pe, "mla.oT", 1)
            linear("o", mix, 4)
            full_stat("postmix", KD)
            full_bcast("postmix")
            b = blocks_of("ple")
            w, kts = block_ready(b)
            for t in range(KD):
                dst = take("ple", t)
                for k in range(2):
                    last = mm(dst[:, 0:SEQ], w[:, k, 128 * t:128 * t + 128], pT[:, k, :], k == 0, k == 1)
                ready(last)
            full_stat("ffn", KD)
            full_bcast("ffn")
            pe.wait_ge(sem("ffn.xg"), KD)
            linear("up", xg, UP_PAIRS)
            pe.wait_ge(sem("ffn.hidden"), UP_PAIRS)
            linear("down", hidden, 4, 3)
            full_stat("postffn", KD)
            full_bcast("postffn")
            full_stat("plegate", KD)
            full_bcast("plegate")
            pe.wait_ge(sem("plegate.xg"), KD)
            linear("ple_gate", xg, 4)
            full_stat("postple", KD)
            full_bcast("postple")

        @block.scalar
        def _(act):
            own = [0]

            def settle(ins):
                own[0] += 1
                ins.then_inc(sem("scalar_step"), 1)
                act.wait_ge(sem("scalar_step"), own[0])

            def do(dst, src, func, bias=0.0, scale=1.0, **more):
                return nc.scalar.activation(dst, src, func, bias=bias, scale=scale, **more)

            def copy(dst, src, scale=1.0):
                return nc.scalar.activation(dst, src, ACT.Copy, scale=scale)

            def root(name, n, dim):
                wait_tile(act, f"{name}.stat", 0)
                c = RC[name]
                do(smalls[:, c:c + n], bank(f"{name}.stat", 0)[:, 0:n], ACT.Sqrt, const("eps6"), 1.0 / dim)\
                    .then_inc(emptied(f"{name}.stat", 0), 1)

            def keep_bcast(name):
                wait_tile(act, f"{name}.bc", 0)
                copy(rb[:, :], bank(f"{name}.bc", 0)[:, 0:SEQ]).then_inc(emptied(f"{name}.bc", 0), 1)

            def empty(tile, dst, src, func=ACT.Copy):
                wait_tile(act, *tile)
                return copy(dst, src).then_inc(emptied(*tile), 1)

            def squares_of_x(stage, norm):
                for t in range(KD):
                    wait_emptied(act, stage, t)
                    do(sq[:, t, :], x[:, t, :], ACT.Square).then_inc(sem(f"{norm}.squares"), 1)

            def exponentials(kind):
                for n, u in enumerate(UNITS[kind]):
                    slot = (FIRST_UNIT[kind] + n) % 2
                    act.wait_ge(sem("negmax"), FIRST_UNIT[kind] + n + 1)
                    ps = bank(kind, "S", n)
                    for i in range(len(u.heads)):
                        c = STAT_COL[kind, n] + i
                        last = do(probs[:, slot, u.keys * i:u.keys * (i + 1)], ps[:, u.keys * i:u.keys * (i + 1)],
                                  ACT.Exp, negmax[:, c:c + 1], MLA_SCALE if kind == "mla" else QK_SCALE,
                                  accum_out=rowsum[:, c:c + 1])
                    last.then_inc(emptied(kind, "S", n), 1)

            act.dma_start(flat(xg2[:, :, :]), mem_in).then_inc(sem("mem_in"), 16)
            act.dma_start(flat(x[:, :, :]), x_in).then_inc(sem("x_in"), 16)
            act.dma_start(C[:, :], consts_in).then_inc(sem("consts_in"), 16)
            act.dma_start(flat(pT[:, :, :]), p_in).then_inc(sem("p_in"), 16)
            act.dma_start(pos[:, :], pos_in).then_inc(sem("positions_in"), 16)
            act.wait_ge(sem("mem_in"), 16)
            do(flat(y[:, :, :]), flat(xg2[:, :, :]), ACT.Square).then_inc(sem("mem.squares"), 1)
            act.wait_ge(sem("x_in"), 16)
            do(flat(sq[:, :, :]), flat(x[:, :, :]), ACT.Square).then_inc(sem("mix0.squares"), 1)
            act.wait_ge(sem("consts_in"), 16)
            root("mem", 2, 1024)
            root("mix0", 2, 1024)
            keep_bcast("mix0")

            def gate(c):
                act.wait_ge(sem("glu.gate"), c + 1)
                do(tmp[:, c % 2, 256:512], tmp2[:, c % 2, 256:512], ACT.Sigmoid, const("b_glu", 6 + c, 1))\
                    .then_inc(sem("glu.sigmoid"), 1)

            for c in range(CONV_TILES):
                if c >= 2:
                    act.wait_ge(sem("glu.ready"), c - 1)
                for i in range(2):
                    empty(("a_in", 2 * c + i), tmp[:, c % 2, 256 * i:256 * i + 256], bank("a_in", 2 * c + i)[:, 0:SEQ])
                if c >= 1:
                    gate(c - 1)
            gate(CONV_TILES - 1)
            wait_emptied(act, "a_in", 12)
            wait_emptied(act, "a_in", 13)
            do(flat(sq[:, 0:2, :]), flat(y[:, 0:2, :]), ACT.Square).then_inc(sem("qm0.squares"), 1)
            root("qm0", 8, 64)
            for l in range(2):
                for t in range(2):
                    empty((f"mem_kv{l}", t), y[:, 2 + 2 * l + t, :], bank(f"mem_kv{l}", t)[:, 0:SEQ])
                for t in range(2):
                    wait_emptied(act, f"mem_kv{l}", t)
                do(flat(sq[:, 0:2, :]), flat(y[:, 2 + 2 * l:4 + 2 * l, :]), ACT.Square).then_inc(sem(f"mk{l}.squares"), 1)
                for tt in range(TT):
                    empty((f"mem_kv{l}", 2 + tt), memv[:, l, tt, :], bank(f"mem_kv{l}", 2 + tt)[:, 0:256])
                root(f"mk{l}", 8, 64)
            exponentials("mem0")
            act.wait_ge(sem("ln.centered"), CONV_TILES)
            do(flat(sq[:, 0:6, :]), flat(conv2), ACT.Square).then_inc(sem("ln.squares"), 1)
            wait_tile(act, "ln.var", 0)
            do(tmp[:, 0, 0:256], bank("ln.var", 0)[:, 0:SEQ], ACT.Sqrt, const("eps5"), 1.0 / 768)\
                .then_inc(emptied("ln.var", 0), 1)
            for c in range(CONV_TILES):
                act.wait_ge(sem("ln.scaled"), c + 1)
                do(mix[:, c, :], conv2[:, c, :], ACT.Silu, const("ln_b", c, 1), const("ln_g", c, 1))\
                    .then_inc(sem("mix0.mixed"), 1)

            def mlp(l):
                squares_of_x(f"out{l}", f"mlp{l}")
                root(f"mlp{l}", 2, 1024)
                keep_bcast(f"mlp{l}")
                for t in range(FF_TILES):
                    wait_emptied(act, f"mlp_in{l}", t)
                    do(hidden[:, t, :], slots[:, t % 4, :], ACT.Square).then_inc(sem(f"mlp{l}.hidden"), 1)
                norm = ("mix1", "smix")[l]
                squares_of_x(f"mlp_out{l}", norm)
                root(norm, 2, 1024)
                keep_bcast(norm)

            mlp(0)
            for t in range(2):
                wait_emptied(act, "kv", 2 + t)
            do(flat(sq[:, 0:2, :]), flat(ksraw), ACT.Square).then_inc(sem("ks.squares"), 1)
            for t in range(2):
                wait_tile(act, "kv", 4 + t)
                copy(vsw[:, t, :], bank("kv", 4 + t)[:, 0:256], rc[:, RC["mix1"] + t:RC["mix1"] + t + 1])\
                    .then_inc(emptied("kv", 4 + t), 1)
            root("ks", 8, 64)
            for a, n in enumerate("kv"):
                for c in range(2):
                    wait_tile(act, f"cmp_{n}", c)
                    do(cmph[:, a, c, :], bank(f"cmp_{n}", c)[:, 0:32], ACT.Gelu_apprx_tanh)\
                        .then_inc(emptied(f"cmp_{n}", c), 1)
            empty(("kc", 0), kraw, bank("kc", 0)[:, 0:32])
            wait_emptied(act, "kc", 0)
            do(krms[:, 0:32], kraw, ACT.Square).then_inc(sem("kc.squares"), 1)
            for t in range(KD):
                wait_emptied(act, "b_in", t)
                last = do(sq[:, t, :], y[:, t, :], ACT.Square)
            last.then_inc(sem("bq.squares"), 1)
            wait_tile(act, "kc.norm", 0)
            do(krms[:, 32:64], bank("kc.norm", 0)[:, 0:32], ACT.Sqrt, const("eps6"), 1.0 / 64)\
                .then_inc(emptied("kc.norm", 0), 1)
            root("bq", 32, 64)
            wait_emptied(act, "gates", 0)
            do(gates[0:36, :], gates[0:36, :], ACT.Sigmoid, const("b_gate")[0:36, :]).then_inc(sem("gates.sigmoid"), 1)
            exponentials("mem1")
            act.wait_ge(sem("cmp.centered"), 1)
            do(flat(cmpp), flat(cmpp), ACT.Exp).then_inc(sem("cmp.probs"), 1)
            exponentials("nsa")
            mlp(1)
            act.wait_ge(sem("angles"), 1)
            do(sinT, tmp2[:, 0, 0:256], ACT.Sin)
            do(cosT, tmp2[:, 0, 256:512], ACT.Sin).then_inc(sem("rope.tables"), 1)
            for j in range(2):
                for tt in range(TT):
                    tile = ("s_in", 8 + 2 * j + tt)
                    wait_tile(act, *tile)
                    c = RC["smix"] + tt
                    copy(sbv[:, tt, 256 * j:256 * j + 256], bank(*tile)[:, 0:256], rc[:, c:c + 1]).then_inc(emptied(*tile), 1)
            for t in range(2):
                wait_emptied(act, "s_in", 12 + t)
            do(flat(sq[:, 0:2, :]), flat(lat[:, 0:2, :]), ACT.Square).then_inc(sem("qlat.squares"), 1)
            wait_emptied(act, "s_lat", 0)
            do(sq[:, 2, :], lat[:, 2, :], ACT.Square).then_inc(sem("kvlat.squares"), 1)
            root("qlat", 2, 256)
            root("kvlat", 2, 128)
            for w in range(9):
                if w < 8:
                    wait_tile(act, "sb.Z", w)
                    if w >= 2:
                        act.wait_ge(sem("sb.log_keep"), w - 1)
                    zs = zt[:, w % 2, :]
                    settle(do(zs, bank("sb.Z", w)[:, 0:384], ACT.Abs))
                    settle(do(zs, zs, ACT.Exp, scale=-1.0))
                    do(zs, zs, ACT.Ln, 1.0).then_inc(sem("sb.log"), 1)
                if w >= 1:
                    wait_tile(act, "sb.W", w - 1)
                    do(wt[:, (w - 1) % 2, :], bank("sb.W", w - 1)[:, 0:384], ACT.Exp).then_inc(emptied("sb.W", w - 1), 1)
                if w >= 3 and w % 2:
                    pair = (w - 3) // 2
                    wait_out_emptied(act, ("sb", pair))
                    do(sq[:, pair, :], osb[:, pair, :], ACT.Square).then_inc(sem("sb.squares"), 1)
            wait_out_emptied(act, ("sb", 3))
            do(sq[:, 3, :], osb[:, 3, :], ACT.Square).then_inc(sem("sb.squares"), 1)
            root("sb", 2, 512)
            for h in range(8):
                empty(("q_up", h), qcat[0:96, h, :], bank("q_up", h)[0:96, 0:SEQ])
            for h in range(8):
                empty(("k_up", h), kcat[0:64, h, :], bank("k_up", h)[0:64, 0:SEQ])
            exponentials("mla")
            for tt in range(TT):
                c = RC["mla"] + tt
                wait_out_emptied(act, ("mla", "mla", tt, 0))
                settle(do(flat(sq[:, 0:2, :]), otok[:, tt, 0:512], ACT.Square, accum_out=smalls[:, c:c + 1]))
                do(smalls[:, c + 2:c + 3], smalls[:, c:c + 1], ACT.Sqrt, const("eps6"), 1.0 / 512)\
                    .then_inc(sem("mla.root"), 1)

            def raw_outputs(stage, norm):
                for t in range(KD):
                    wait_tile(act, stage, t)
                    ps = bank(stage, t)[:, 0:SEQ]
                    do(sq[:, t, :], ps, ACT.Square).then_inc(sem(f"{norm}.squares"), 1)
                    copy(y[:, t, :], ps).then_inc(emptied(stage, t), 1)
                root(norm, 2, 1024)

            def squares_after(norm, after):
                for t in range(KD):
                    act.wait_ge(sem(f"{after}.x"), t + 1)
                    do(sq[:, t, :], x[:, t, :], ACT.Square).then_inc(sem(f"{norm}.squares"), 1)

            raw_outputs("o", "postmix")
            for t in range(KD):
                empty(("ple", t), xg2[:, t, :], bank("ple", t)[:, 0:SEQ])
            squares_after("ffn", "postmix")
            root("ffn", 2, 1024)
            keep_bcast("ffn")
            for c in range(UP_PAIRS):
                act.wait_ge(sem("ffn.gate"), c + 1)
                do(slots2[:, c % 4, :], slots[:, (2 * c) % 4, :], ACT.Gelu_apprx_tanh).then_inc(sem("ffn.gelu"), 1)
            raw_outputs("down", "postffn")
            squares_after("plegate", "postffn")
            root("plegate", 2, 1024)
            keep_bcast("plegate")
            for t in range(KD + 1):
                if t < KD:
                    wait_emptied(act, "ple_gate", t)
                    do(slots2[:, t % 4, :], slots[:, t % 4, :], ACT.Sigmoid, const("b_plegate", t, 1))\
                        .then_inc(sem("ple.sigmoid"), 1)
                if t >= 1:
                    act.wait_ge(sem("ple.gated"), t)
                    do(sq[:, t - 1, :], y[:, t - 1, :], ACT.Square).then_inc(sem("postple.squares"), 1)
            root("postple", 2, 1024)

        @block.gpsimd
        def _(pool):
            def tt_(dst, a, b, op):
                return nc.gpsimd.tensor_tensor(dst, a, b, op)

            nc.gpsimd.memset(glu[:, :, 0:PAD], 0.0).then_inc(sem("glu.padded"), 1)
            pool.wait_ge(sem("consts_in"), 16)
            nc.gpsimd.tensor_copy(ident_b[:, :], const("ident"))
            nc.gpsimd.tensor_copy(cbias_b[:, :], const("cbias"))
            nc.gpsimd.tensor_copy(sbias_b[:, :], const("sbias")).then_inc(sem("bf16_consts"), 1)
            wait_emptied(pool, "mix0.bc", 0)
            for c in range(CONV_TILES):
                s = c % 2
                wait_emptied(pool, "a_in", 2 * c + 1)
                wait_emptied(pool, "a_in", 2 * c)
                tt_(tmp2[:, s, 256:512], tmp[:, s, 256:512], rb[:, :], ALU.mult).then_inc(sem("glu.gate"), 1)
                tt_(tmp2[:, s, 0:256], tmp[:, s, 0:256], rb[:, :], ALU.mult).then_inc(sem("glu.scaled"), 1)
                pool.wait_ge(sem("glu.scaled"), 2 * c + 1)
                nc.gpsimd.tensor_scalar(tmp2[:, s, 0:256], tmp2[:, s, 0:256], const("b_glu", c, 1), None, ALU.add)\
                    .then_inc(sem("glu.scaled"), 1)
                pool.wait_ge(sem("glu.scaled"), 2 * c + 2)
                pool.wait_ge(sem("glu.sigmoid"), c + 1)
                tt_(glu[:, c, PAD:PAD + SEQ], tmp2[:, s, 0:256], tmp[:, s, 256:512], ALU.mult).then_inc(sem("glu.ready"), 1)
            wait_tile(pool, "mix1.stat", 0)
            nc.gpsimd.memset(tkv[:, :, 256:272], 0.0).then_inc(sem("tkv.padded"), 1)
            pool.wait_ge(sem("krope.rotated"), 1)
            nc.gpsimd.tensor_copy(kcat[64:96, :, :], rows(tmp[64:96, 1, 256:512], 8)).then_inc(sem("kcat"), 1)

        @block.vector
        def _(dve):
            own = [0]

            def step(ins):
                own[0] += 1
                ins.then_inc(sem("vector_step"), 1)

            def settle(ins=None):
                if ins is not None:
                    step(ins)
                dve.wait_ge(sem("vector_step"), own[0])

            def tt_(dst, a, b, op):
                return nc.vector.tensor_tensor(dst, a, b, op)

            def ts(dst, a, s, op, s2=None, op2=None):
                if op2 is None:
                    return nc.vector.tensor_scalar(dst, a, s, None, op)
                return nc.vector.tensor_scalar(dst, a, s, s2, op, op2)

            def stt(dst, a, s, b, op0, op1):
                return nc.vector.scalar_tensor_tensor(out=dst, in0=a, scalar=s, in1=b, op0=op0, op1=op1)

            def invert(name, n):
                wait_emptied(dve, f"{name}.stat", 0)
                c = RC[name]
                nc.vector.reciprocal(rc[:, c:c + n], smalls[:, c:c + n]).then_inc(sem(f"{name}.rc"), 1)

            def scaled(tile, dst, src, factor):
                wait_tile(dve, *tile)
                tt_(dst, src, factor, ALU.mult).then_inc(emptied(*tile), 1)

            def gains(dst_, name, gname, signal):
                for t in range(KD):
                    ts(dst_[:, t, :], x[:, t, :], const(gname, t, 1), ALU.mult).then_inc(sem(signal), 1)

            def residual(stage, inputs):
                for t in range(KD):
                    wait_tile(dve, stage, t)
                    tt_(x[:, t, :], x[:, t, :], bank(stage, t)[:, 0:SEQ], ALU.add).then_inc(emptied(stage, t), 1)
                    wait_emptied(dve, stage, t)
                    for dst_, gname, signal in inputs:
                        ts(dst_[:, t, :], x[:, t, :], const(gname, t, 1), ALU.mult).then_inc(sem(signal), 1)

            def normed_heads(name, srcs, dsts, gs):
                for pair in range(len(srcs) // 2):
                    wait_tile(dve, f"{name}.bc", pair)
                    for k in (2 * pair, 2 * pair + 1):
                        last = stt(dsts[k], srcs[k], gs[k], bank(f"{name}.bc", pair)[:, 256 * (k % 2):256 * (k % 2) + 256],
                                   ALU.mult, ALU.mult)
                    last.then_inc(emptied(f"{name}.bc", pair), 1)

            def heads_of(ap, outs):
                v = ap.rearrange("p (h d) -> p h d", d=64)
                s = outs[1] - outs[0] if len(outs) > 1 else 1
                return v[:, outs[0]:outs[-1] + 1:s, :]

            def attention(kind, finish):
                units = UNITS[kind]
                scale = MLA_SCALE if kind == "mla" else QK_SCALE
                for w in range(len(units) + 2):
                    if w < len(units):
                        u = units[w]
                        nh, c = len(u.heads), STAT_COL[kind, w]
                        wait_tile(dve, kind, "S", w)
                        s = bank(kind, "S", w)[:, 0:nh * u.keys].rearrange("p (h k) -> p h k", h=nh)
                        settle(nc.vector.reduce_max(rowmax[:, c:c + nh], s, X_AXIS))
                        ts(negmax[:, c:c + nh], rowmax[:, c:c + nh], -scale, ALU.mult).then_inc(sem("negmax"), 1)
                    if 1 <= w <= len(units):
                        slot = (FIRST_UNIT[kind] + w - 1) % 2
                        n = len(units[w - 1].heads) * units[w - 1].keys
                        wait_tile(dve, kind, "T", w - 1)
                        nc.vector.tensor_copy(probsT[:, slot, 0:n], bank(kind, "T", w - 1)[:, 0:n])\
                            .then_inc(emptied(kind, "T", w - 1), 1)
                    if w >= 2 and units[w - 2].last:
                        finish(kind, units[w - 2].group)

            def group_units(kind, group):
                return [(n, u) for n, u in enumerate(UNITS[kind]) if u.group == group]

            def inverse_sums(kind, group):
                us = group_units(kind, group)
                c0 = STAT_COL[kind, us[0][0]]
                total = sum(len(u.heads) for _, u in us)
                wait_emptied(dve, kind, "S", us[-1][0])
                settle(nc.vector.reciprocal(rowinv[:, 0:total], rowsum[:, c0:c0 + total]))
                return us

            def finish_plain(kind, group):
                us = inverse_sums(kind, group)
                wait_out(dve, group)
                _, _, tt, _ = group
                ps = obank(group)
                width = 512 if kind == "mla" else 256
                c = 0
                for _, u in us:
                    nh = len(u.heads)
                    last = tt_(heads_of(otok[:, tt, 0:width], u.outs), heads_of(ps[:, 0:width], u.outs),
                               bcast(rowinv[:, c:c + nh], 64), ALU.mult)
                    c += nh
                last.then_inc(out_emptied(group), 1)
                if kind != "mla":
                    own_ready(group, kind)

            def own_ready(group, kind):
                wait_out_emptied(dve, group)
                dve.sem_inc(sem(f"{kind}.o"), 1)

            def finish_gated(kind, group):
                us = inverse_sums(kind, group)
                _, branch, tt, base = group
                b = 1 if branch == "slc" else 2
                gview = gate_tok[:, tt, :].rearrange("p (h b) -> p h b", b=3)
                c = 0
                for _, u in us:
                    nh = len(u.heads)
                    s = u.heads[1] - u.heads[0] if nh > 1 else 1
                    step(tt_(rowinv[:, c:c + nh], rowinv[:, c:c + nh], gview[:, u.heads[0]:u.heads[-1] + 1:s, b], ALU.mult))
                    c += nh
                settle()
                wait_out(dve, group)
                ps = obank(group)
                c = 0
                part = tmp[:, 0, 0:384]
                for _, u in us:
                    nh = len(u.heads)
                    last = tt_(heads_of(part, u.outs), heads_of(ps[:, 0:384], u.outs), bcast(rowinv[:, c:c + nh], 64), ALU.mult)
                    c += nh
                last.then_inc(out_emptied(group), 1)
                wait_out_emptied(dve, group)
                o = otok[:, tt, 64 * base:64 * base + 384]
                ins = tt_(o, o, part, ALU.add)
                if branch == "win":
                    ins.then_inc(sem("nsa.o"), 1)
                else:
                    settle(ins)

            dve.wait_ge(sem("consts_in"), 16)
            dve.wait_ge(sem("x_in"), 16)
            for t in range(KD):
                last = ts(xg[:, t, :], x[:, t, :], const("g_mix0", t, 1), ALU.mult)
            last.then_inc(sem("mix0.xg"), 1)
            invert("mem", 2)
            invert("mix0", 2)
            dve.wait_ge(sem("mem_in"), 16)
            wait_tile(dve, "mem.bc", 0)
            for t in range(KD):
                last = stt(xg2[:, t, :], xg2[:, t, :], const("g_mem", t, 1), bank("mem.bc", 0)[:, 0:SEQ], ALU.mult, ALU.mult)
            last.then_inc(emptied("mem.bc", 0), 1)

            def convolve(c):
                dve.wait_ge(sem("glu.ready"), c + 1)
                if c == 0:
                    dve.wait_ge(sem("glu.padded"), 1)
                sums = (conv[:, c, :], conv2[:, c, :])

                def tap(j):
                    return const("dw", TAPS * c + j, 1)

                step(ts(sums[0], glu[:, c, 0:SEQ], tap(0), ALU.mult, const("dw_b", c, 1), ALU.add))
                step(ts(sums[1], glu[:, c, 1:1 + SEQ], tap(1), ALU.mult))
                for j in range(2, TAPS):
                    dve.wait_ge(sem("vector_step"), own[0] - 1)
                    step(stt(sums[j % 2], glu[:, c, j:j + SEQ], tap(j), sums[j % 2], ALU.mult, ALU.add))
                settle()
                tt_(sums[0], sums[0], sums[1], ALU.add).then_inc(sem("conv.done"), 1)

            for c in range(4):
                convolve(c)
            wait_emptied(dve, "mix0.bc", 0)
            for t in range(2):
                scaled(("a_in", 12 + t), y[:, t, :], bank("a_in", 12 + t)[:, 0:SEQ], rb[:, :])
            convolve(4)
            invert("qm0", 8)
            normed_heads("qm0", [y[:, t, :] for t in range(2)], [q[:, t, :] for t in range(2)], [const("g_memq0")] * 2)
            for l in range(2):
                invert(f"mk{l}", 8)
                normed_heads(f"mk{l}", [y[:, 2 + 2 * l + t, :] for t in range(2)], [memk[:, l, t, :] for t in range(2)],
                             [const(f"g_memk{l}")] * 2)
                if l == 0:
                    convolve(5)
            attention("mem0", finish_plain)

            def mem_out(kind):
                for tt in range(TT):
                    wait_tile(dve, f"{kind}.oT", tt)
                    nc.vector.tensor_copy(mix[:, 6:8, 128 * tt:128 * tt + 128],
                                          bank(f"{kind}.oT", tt)[:, 0:256].rearrange("p (a t) -> p a t", a=2))\
                        .then_inc(emptied(f"{kind}.oT", tt), 1)

            mem_out("mem0")
            dve.wait_ge(sem("conv.done"), CONV_TILES)
            wait_tile(dve, "ln.mean", 0)
            for c in range(CONV_TILES):
                ins = stt(conv2[:, c, :], bank("ln.mean", 0)[:, 0:SEQ], -1.0 / 768, conv[:, c, :], ALU.mult, ALU.add)
                ins.then_inc(sem("ln.centered"), 1)
            dve.wait_ge(sem("ln.centered"), CONV_TILES)
            dve.sem_inc(emptied("ln.mean", 0), 1)
            wait_emptied(dve, "ln.var", 0)
            settle(nc.vector.reciprocal(tmp2[:, 0, 0:256], tmp[:, 0, 0:256]))
            for c in range(CONV_TILES):
                tt_(conv2[:, c, :], conv2[:, c, :], tmp2[:, 0, 0:256], ALU.mult).then_inc(sem("ln.scaled"), 1)
            residual("out0", [(xg, "g_mlp0", "mlp0.xg")])

            def mlp(l, inputs):
                invert(f"mlp{l}", 2)
                wait_emptied(dve, f"mlp{l}.bc", 0)
                for t in range(FF_TILES):
                    if t >= 4:
                        dve.wait_ge(sem(f"mlp{l}.hidden"), t - 3)
                    tile = (f"mlp_in{l}", t)
                    wait_tile(dve, *tile)
                    stt(slots[:, t % 4, :], bank(*tile)[:, 0:SEQ], 0.0, rb[:, :], ALU.max, ALU.mult)\
                        .then_inc(emptied(*tile), 1)
                residual(f"mlp_out{l}", inputs)

            mlp(0, [(xg, "g_mix1", "mix1.xg"), (xg2, "g_kv", "kv.xg")])
            invert("mix1", 2)
            wait_emptied(dve, "mix1.bc", 0)
            for a in range(2):
                scaled(("kv", a), tkv[:, a, 0:SEQ], bank("kv", a)[:, 0:SEQ], rb[:, :])
            for a in range(2):
                scaled(("kv", 2 + a), ksraw[:, a, :], bank("kv", 2 + a)[:, 0:SEQ], rb[:, :])
            dve.wait_ge(sem("tkv.padded"), 1)
            for a, n in enumerate("kv"):
                wait_emptied(dve, "kv", a)
                for g in range(2):
                    src = tkv[64 * g:64 * g + 64, a, :].rearrange("p (n s) -> p s n", s=16)
                    for par in range(2):
                        for half in range(2):
                            pe_ = const(f"pe_{n}", 16 * par + 8 * half, 8)[64 * g:64 * g + 64, :]
                            last = tt_(windows[64 * par:64 * par + 64, a, 8 * half:8 * half + 8, 16 * g:16 * g + 16],
                                       src[:, par:16:2, half:half + 16], bcast(pe_, 16), ALU.add)
                last.then_inc(sem(f"windows_{n}"), 1)
            invert("ks", 8)
            wait_tile(dve, "ks.bc", 0)
            for br in range(2):
                for g in range(2):
                    rows_ = slice(64 * g, 64 * g + 64)
                    for d in range(2):
                        last = stt(kd[64 * d:64 * d + 64, br, g, :], ksraw[rows_, br, :], const("g_k", 1 + br, 1)[rows_, :],
                                   bank("ks.bc", 0)[rows_, 256 * br:256 * br + 256], ALU.mult, ALU.mult)
            last.then_inc(emptied("ks.bc", 0), 1)
            for c in range(2):
                wait_emptied(dve, "cmp_v", c)
                for g in range(2):
                    last = nc.vector.tensor_copy(cmph6[:, c, g, :, :], rows(cmph[:, 1, c, 16 * g:16 * g + 16], 6))
            last.then_inc(sem("cmph6"), 1)
            for g in range(2):
                wait_tile(dve, "vc", g)
                tt_(vbd[0:96, g, :].rearrange("p (h d) -> p h d", h=6), rows(bank("vc", g)[0:96, 0:64], 6),
                    bcast(const("headblock")[0:96, :], 64), ALU.mult).then_inc(emptied("vc", g), 1)
            for t in range(KD):
                scaled(("b_in", t), y[:, t, :], bank("b_in", t)[:, 0:SEQ], rb[:, :])
            wait_emptied(dve, "kc.norm", 0)
            settle(nc.vector.reciprocal(krms[:, 64:96], krms[:, 32:64]))
            stt(kcmp, kraw, const("g_k", 0, 1), krms[:, 64:96], ALU.mult, ALU.mult).then_inc(sem("kcmp"), 1)
            invert("bq", 32)
            scaled(("gates", 0), gates[0:36, :], bank("gates", 0)[0:36, 0:SEQ], rb[0:36, :])
            normed_heads("bq", [y[:, t, :] for t in range(KD)], [q[:, t, :] for t in range(KD)],
                         [const("g_bq")] * 6 + [const("g_memq1")] * 2)
            wait_tile(dve, "gatesT", 0)
            settle(nc.vector.tensor_copy(flat(gate_tok[:, :, :]), bank("gatesT", 0)[:, 0:72]))
            dve.sem_inc(emptied("gatesT", 0), 1)
            attention("mem1", finish_plain)
            mem_out("mem1")
            for n in range(4):
                tt = n // 2
                for odd in range(2):
                    tile = ("cmp.S", 2 * n + odd)
                    wait_tile(dve, *tile)
                    dst = cmps[:, n, :].rearrange("p (h k) -> p h k", h=6)[:, odd:6:2, :]
                    stt(dst, bank(*tile)[:, 0:48].rearrange("p (h k) -> p h k", h=3), QK_SCALE,
                        rows(const("cmpbias", 16 * tt, 16), 3), ALU.mult, ALU.add).then_inc(emptied(*tile), 1)
            for odd in range(2):
                wait_emptied(dve, "cmp.S", 6 + odd)
            for n in range(4):
                for odd in range(2):
                    wait_emptied(dve, "cmp.S", 2 * n + odd)
            cs = flat(cmps).rearrange("p (h k) -> p h k", k=16)
            cp = flat(cmpp).rearrange("p (h k) -> p h k", k=16)
            cmax, csum = smalls[:, 0:24], smalls[:, 32:56]
            settle(nc.vector.reduce_max(cmax, cs, X_AXIS))
            settle(ts(cmax, cmax, -1e29, ALU.max))
            tt_(cp, cs, bcast(cmax, 16), ALU.subtract).then_inc(sem("cmp.centered"), 1)
            dve.wait_ge(sem("cmp.probs"), 1)
            settle(nc.vector.reduce_sum(csum, cp, X_AXIS))
            settle(ts(csum, csum, 1e-30, ALU.max))
            settle(nc.vector.reciprocal(csum, csum))
            gates_all = flat(gate_tok[:, :, :]).rearrange("p (h b) -> p h b", b=3)
            settle(tt_(csum, csum, gates_all[:, :, 0], ALU.mult))
            for n in range(4):
                wait_tile(dve, "cmp.T", n)
                nc.vector.tensor_copy(cmppT[0:96, n, :], bank("cmp.T", n)[0:96, 0:128]).then_inc(emptied("cmp.T", n), 1)
            for n in range(4):
                tt, g = n // 2, n % 2
                wait_out(dve, ("cmp", tt, g))
                tt_(otok[:, tt, 384 * g:384 * g + 384].rearrange("p (h d) -> p h d", h=6),
                    obank(("cmp", tt, g))[:, 0:384].rearrange("p (h d) -> p h d", h=6),
                    bcast(csum[:, 6 * n:6 * n + 6], 64), ALU.mult).then_inc(out_emptied(("cmp", tt, g)), 1)
            for n in range(4):
                wait_out_emptied(dve, ("cmp", n // 2, n % 2))
            attention("nsa", finish_gated)
            for n in range(4):
                tt, g = n // 2, n % 2
                wait_tile(dve, "nsa.oT", n)
                nc.vector.tensor_copy(mix[:, 3 * g:3 * g + 3, 128 * tt:128 * tt + 128],
                                      bank("nsa.oT", n)[:, 0:384].rearrange("p (a t) -> p a t", a=3))\
                    .then_inc(emptied("nsa.oT", n), 1)
            residual("out1", [(xg, "g_mlp1", "mlp1.xg")])
            mlp(1, [(xg, "g_smix", "smix.xg")])
            invert("smix", 2)
            dve.wait_ge(sem("positions_in"), 16)
            wait_tile(dve, "smix.stat", 0)
            f, ang, turns = tmp[:, 0, 0:256], tmp[:, 0, 256:512], tmp[:, 1, 0:256]
            sin_arg, cos_arg = tmp2[:, 0, 0:256], tmp2[:, 0, 256:512]
            two_pi = 2 * math.pi
            parts = pi_parts(two_pi)
            settle(nc.vector.tensor_copy(f, pos[:, :]))
            settle(ts(ang, f, const("invf"), ALU.mult))
            settle(ts(turns, ang, 1.0 / two_pi, ALU.mult, ROUNDER, ALU.add))
            settle(ts(turns, turns, -ROUNDER, ALU.add))
            for part in parts:
                settle(stt(ang, turns, -part, ang, ALU.mult, ALU.add))
            settle(ts(cos_arg, ang, math.pi / 2, ALU.add))
            settle(ts(f, cos_arg, math.pi, ALU.is_gt, -two_pi, ALU.mult))
            settle(tt_(cos_arg, cos_arg, f, ALU.add))
            step(ts(cos_arg, cos_arg, SIN_LIMIT, ALU.min, -SIN_LIMIT, ALU.max))
            settle()
            ts(sin_arg, ang, SIN_LIMIT, ALU.min, -SIN_LIMIT, ALU.max).then_inc(sem("angles"), 1)
            wait_emptied(dve, "smix.bc", 0)
            for t in range(4):
                wait_tile(dve, "s_in", t)
                stt(q[:, t, :], bank("s_in", t)[:, 0:SEQ], QK_SCALE, rb[:, :], ALU.mult, ALU.mult)\
                    .then_inc(emptied("s_in", t), 1)
            for t in range(4, 8):
                scaled(("s_in", t), q[:, t, :], bank("s_in", t)[:, 0:SEQ], rb[:, :])
            for t in range(2):
                scaled(("s_in", 12 + t), lat[:, t, :], bank("s_in", 12 + t)[:, 0:SEQ], rb[:, :])
            scaled(("s_lat", 0), lat[:, 2, :], bank("s_lat", 0)[:, 0:SEQ], rb[:, :])
            scaled(("s_lat", 1), krope[64:96, :], bank("s_lat", 1)[64:96, 0:SEQ], rb[64:96, :])
            invert("qlat", 2)
            invert("kvlat", 2)
            for t in range(2):
                wait_emptied(dve, "s_in", 12 + t)
            wait_tile(dve, "qlat.bc", 0)
            for t in range(2):
                last = stt(latn[:, t, :], lat[:, t, :], const("g_qlat", t, 1), bank("qlat.bc", 0)[:, 0:SEQ], ALU.mult, ALU.mult)
            last.then_inc(emptied("qlat.bc", 0), 1)
            wait_emptied(dve, "s_lat", 0)
            wait_tile(dve, "kvlat.bc", 0)
            stt(kvn, lat[:, 2, :], const("g_kvlat"), bank("kvlat.bc", 0)[:, 0:SEQ], ALU.mult, ALU.mult)\
                .then_inc(emptied("kvlat.bc", 0), 1)
            dve.wait_ge(sem("rope.tables"), 1)
            wait_emptied(dve, "s_lat", 1)
            wait_tile(dve, "krope.swap", 0)
            step(tt_(tmp[64:96, 0, 0:256], krope[64:96, :], cosT[64:96, :], ALU.mult))
            tt_(tmp[64:96, 0, 256:512], bank("krope.swap", 0)[64:96, 0:SEQ], sinT[64:96, :], ALU.mult)\
                .then_inc(emptied("krope.swap", 0), 1)
            settle()
            wait_emptied(dve, "krope.swap", 0)
            tt_(tmp[64:96, 1, 256:512], tmp[64:96, 0, 0:256], tmp[64:96, 0, 256:512], ALU.add).then_inc(sem("krope.rotated"), 1)
            for w in range(10):
                if w < 8:
                    zs = zt[:, w % 2, :]
                    dve.wait_ge(sem("sb.log"), w + 1)
                    stt(zs, bank("sb.Z", w)[:, 0:384], 0.0, zs, ALU.max, ALU.add).then_inc(emptied("sb.Z", w), 1)
                    wait_emptied(dve, "sb.Z", w)
                    tt_(sp[:, w % 2, :], zs, const("smask"), ALU.mult).then_inc(sem("sb.log_keep"), 1)
                if w >= 3 and w % 2:
                    pair = (w - 3) // 2
                    wait_out(dve, ("sb", pair))
                    nc.vector.tensor_copy(osb[:, pair, :], obank(("sb", pair))[:, 0:SEQ]).then_inc(out_emptied(("sb", pair)), 1)
            invert("sb", 2)
            for j in range(4):
                heads = slice(2 * j, 2 * j + 2)
                a, b = (tmp2[64:96, n, :].rearrange("p (h t) -> p h t", h=2) for n in range(2))
                for i in range(2):
                    wait_emptied(dve, "q_up", 2 * j + i)
                step(tt_(a, qcat[64:96, heads, :], rows(cosT[64:96, :], 2), ALU.mult))
                wait_tile(dve, "q.swap", j)
                tt_(b, bank("q.swap", j)[64:96, :].rearrange("p (h t) -> p h t", h=2), rows(sinT[64:96, :], 2), ALU.mult)\
                    .then_inc(emptied("q.swap", j), 1)
                settle()
                wait_emptied(dve, "q.swap", j)
                tt_(qcat[64:96, heads, :], a, b, ALU.add).then_inc(sem("qcat"), 1)
                dve.wait_ge(sem("qcat"), j + 1)
            for tt in range(TT):
                wait_tile(dve, "v_up", tt)
                nc.vector.tensor_copy(vmla[:, tt, :], bank("v_up", tt)[:, :]).then_inc(emptied("v_up", tt), 1)
            wait_tile(dve, "sb.bc", 0)
            for t in range(4):
                last = stt(mix[:, t, :], osb[:, t, :], const("g_sb", t, 1), bank("sb.bc", 0)[:, 0:SEQ], ALU.mult, ALU.mult)
            last.then_inc(emptied("sb.bc", 0), 1)
            attention("mla", finish_plain)
            for tt in range(TT):
                c = RC["mla"] + tt
                dve.wait_ge(sem("mla.root"), tt + 1)
                settle(nc.vector.reciprocal(rc[:, c:c + 1], smalls[:, c + 2:c + 3]))
                ts(otok[:, tt, 0:512], otok[:, tt, 0:512], rc[:, c:c + 1], ALU.mult).then_inc(sem("mla.o"), 1)
            for tt in range(TT):
                wait_tile(dve, "mla.oT", tt)
                tt_(mix[:, 4:8, 128 * tt:128 * tt + 128], bank("mla.oT", tt)[:, :].rearrange("p (a t) -> p a t", a=4),
                    bcast(const("g_mla"), 128), ALU.mult).then_inc(emptied("mla.oT", tt), 1)

            def post_norm(name, gname, stage, after=None):
                if stage:
                    for t in range(KD):
                        wait_emptied(dve, stage, t)
                wait_tile(dve, f"{name}.bc", 0)
                for t in range(KD):
                    ins = stt(y[:, t, :], y[:, t, :], const(gname, t, 1), bank(f"{name}.bc", 0)[:, 0:SEQ], ALU.mult, ALU.mult)
                    if t < KD - 1:
                        step(ins)
                    else:
                        ins.then_inc(emptied(f"{name}.bc", 0), 1)
                for t in range(KD):
                    if t == KD - 1:
                        wait_emptied(dve, f"{name}.bc", 0)
                    elif t == 0:
                        settle()
                    tt_(x[:, t, :], x[:, t, :], y[:, t, :], ALU.add)\
                        .then_inc(sem("result" if after is None else f"{name}.x"), 1)
                if after is not None:
                    for t in range(KD):
                        dve.wait_ge(sem(f"{name}.x"), t + 1)
                        ts(xg[:, t, :], x[:, t, :], const(f"g_{after}", t, 1), ALU.mult).then_inc(sem(f"{after}.xg"), 1)

            invert("postmix", 2)
            post_norm("postmix", "g_postmix", "o", "ffn")
            settle(nc.vector.memset(padded[:, :, 0:2], 0.0))
            invert("ffn", 2)
            wait_emptied(dve, "ffn.bc", 0)

            def gated(c):
                dve.wait_ge(sem("ffn.gelu"), c + 1)
                tt_(hidden[:, c, :], slots2[:, c % 4, :], slots[:, (2 * c + 1) % 4, :], ALU.mult).then_inc(sem("ffn.hidden"), 1)

            for c in range(UP_PAIRS):
                s = [(2 * c + i) % 4 for i in range(2)]
                col = [c, UP_PAIRS + c]
                for i in range(2):
                    scaled(("up", 2 * c + i), padded[:, s[i], 2:2 + SEQ], bank("up", 2 * c + i)[:, 0:SEQ], rb[:, :])
                for k in (2, 1, 0):
                    for i in range(2):
                        w = const("conv_w", 3 * col[i] + k, 1)
                        if k == 2:
                            wait_emptied(dve, "up", 2 * c + i)
                            step(ts(slots[:, s[i], :], padded[:, s[i], 2:2 + SEQ], w, ALU.mult, const("conv_b", col[i], 1), ALU.add))
                        else:
                            dve.wait_ge(sem("vector_step"), own[0] - 1)
                            ins = stt(slots[:, s[i], :], padded[:, s[i], k:k + SEQ], w, slots[:, s[i], :], ALU.mult, ALU.add)
                            if k == 0 and i == 0:
                                ins.then_inc(sem("ffn.gate"), 1)
                            else:
                                step(ins)
                    if k == 1:
                        settle()
                settle()
                if c >= 1:
                    gated(c - 1)
            gated(UP_PAIRS - 1)
            invert("postffn", 2)
            post_norm("postffn", "g_postffn", "down", "plegate")
            invert("plegate", 2)
            wait_emptied(dve, "plegate.bc", 0)
            for t in range(KD):
                wait_emptied(dve, "ple", t)
            for t in range(KD + 1):
                if t < KD:
                    scaled(("ple_gate", t), slots[:, t % 4, :], bank("ple_gate", t)[:, 0:SEQ], rb[:, :])
                if t >= 1:
                    dve.wait_ge(sem("ple.sigmoid"), t)
                    tt_(y[:, t - 1, :], slots2[:, (t - 1) % 4, :], xg2[:, t - 1, :], ALU.mult).then_inc(sem("ple.gated"), 1)
            invert("postple", 2)
            dve.wait_ge(sem("ple.gated"), KD)
            post_norm("postple", "g_postple", None)


def _rows(a, width):
    k = a.shape[0] // 128
    return a.reshape(k, 128, width).transpose(1, 0, 2).reshape(128, k * width)


def _pack_weights(i):
    import numpy as _np

    def cols(*parts):
        return _np.concatenate(parts, axis=1)

    u = i["a_w_in"][0]
    a_pairs = [cols(u[:, 128 * c:128 * c + 128], u[:, 768 + 128 * c:896 + 128 * c]) for c in range(6)]
    kv = i["w_kv"]
    part = [kv[:, 128 * n:128 * n + 128] for n in range(6)]
    b = i["b_w_in"][0]
    s = i["w_in_2"][0]
    up = i["w_up_2"][0]
    half = up.shape[1] // 2
    krope = cols(s[:, 1792:1920], _np.zeros((1024, 64), _np.float32), s[:, 1920:1952], _np.zeros((1024, 32), _np.float32))
    full = {
        "a_in": cols(*a_pairs, u[:, 1536:1792]),
        "mem_kv0": i["w_mem_kv"][0], "mem_kv1": i["w_mem_kv"][1],
        "out0": i["w_out"][0], "out1": i["w_out"][1],
        "mlp_in0": i["w_mlp_in"][0], "mlp_in1": i["w_mlp_in"][1],
        "mlp_out0": i["w_mlp_out"][0], "mlp_out1": i["w_mlp_out"][1],
        "kv": cols(part[0], part[1], part[2], part[4], part[3], part[5]),
        "cmp_k": i["cmp_w1_k"], "cmp_v": i["cmp_w1_v"],
        "b_in": b[:, 0:1024], "gates": b[:, 1024:1060],
        "s_in": s[:, 0:1792], "s_lat": krope,
        "q_up": i["w_q_up_2"][0], "kv_up": i["w_kv_up_2"][0],
        "o": i["w_o_2"][0],
        "up": cols(*[cols(up[:, 128 * c:128 * c + 128], up[:, half + 128 * c:half + 128 * c + 128])
                     for c in range(half // 128)]),
        "down": i["w_down_2"][0], "ple": i["w_ple_2"][0], "ple_gate": i["w_ple_gate_2"][0],
    }
    out = _np.zeros((NBLOCKS, 128, BLOCK_COLS), _np.float32)
    for n, (name, r0, kts, c0, width) in enumerate(WEIGHT_BLOCKS):
        block = full[name][128 * r0:128 * (r0 + kts), c0:c0 + width]
        out[n, :, :kts * width] = _rows(block, width)
    return out


def _pack_consts(i):
    import numpy as _np

    out = _np.zeros((128, NCONST), _np.float32)

    def put(name, a):
        a = _np.asarray(a)
        at, width = CONST_AT[name]
        out[:a.shape[0], at:at + width] = a.reshape(a.shape[0], width)

    def vec(name, a):
        put(name, a.reshape(-1, 128).T)

    def twice(a):
        return _np.concatenate([a, a], axis=0)

    for l in range(2):
        vec(f"g_mix{l}", i["norm_mix_g"][l])
        vec(f"g_mlp{l}", i["norm_mlp_g"][l])
        put(f"g_memq{l}", twice(i["mem_q_norm_g"][l])[:, None])
        put(f"g_memk{l}", twice(i["mem_k_norm_g"][l])[:, None])
    vec("g_mem", i["mem_norm_g"])
    vec("b_glu", i["a_b_glu"][0])
    put("dw", i["a_dw"][0].reshape(31, 6, 128).transpose(2, 1, 0).reshape(128, 186))
    vec("dw_b", i["a_dw_b"][0])
    vec("ln_g", i["a_ln_g"][0])
    vec("ln_b", i["a_ln_b"][0])
    vec("g_kv", i["kv_norm_g"])
    put("b_gate", i["b_gate_b"][0][:, None])
    put("g_bq", twice(i["b_q_norm_g"][0])[:, None])
    put("g_k", _np.concatenate([i["k_norm_g"].T, i["k_norm_g"].T], axis=0))
    for n in "kv":
        put(f"pe_{n}", twice(i[f"cmp_pe_{n}"].reshape(16, 2, 64).transpose(2, 1, 0).reshape(64, 32)))
        w2 = i[f"cmp_w2_{n}"].reshape(2, 128, 64).transpose(1, 0, 2)
        put(f"w2_{n}", _np.concatenate([w2, w2], axis=2) if n == "k" else w2)
    for name, key in (("g_smix", "g_pre_mix_2"), ("g_qlat", "g_q_lat_2"), ("g_kvlat", "g_kv_lat_2"),
                      ("g_sb", "g_grp_sb_2"), ("g_mla", "g_grp_mla_2"), ("g_postmix", "g_post_mix_2"),
                      ("g_ffn", "g_pre_ffn_2"), ("g_postffn", "g_post_ffn_2"), ("g_plegate", "g_ple_gate_2"),
                      ("b_plegate", "b_ple_gate_2"), ("g_postple", "g_post_ple_2"), ("conv_b", "conv_b_2")):
        vec(name, i[key][0])
    put("conv_w", i["conv_w_2"][0].reshape(3, 44, 128).transpose(2, 1, 0).reshape(128, 132))

    p = _np.arange(128)
    put("ident", (p[:, None] == p[None, :]).astype(_np.float32))
    put("ones", _np.ones((128, 128), _np.float32))
    put("headsel", (p[:, None] // 64 == _np.arange(2)[None, :]).astype(_np.float32))
    put("halfones", (p[:, None] // 64 == p[None, :] // 64).astype(_np.float32))
    swap = _np.zeros((128, 96), _np.float32)
    for m in range(32):
        swap[64 + (m + 16) % 32, 64 + m] = -1.0 if m < 16 else 1.0
    put("swap", swap)
    inv = (1.0 / (_np.float32(10000.0) ** (_np.arange(0, 32, 2, dtype=_np.float32) / _np.float32(32)))).astype(_np.float32)
    put("invf", _np.tile(inv, 8)[:, None])
    put("eps6", _np.full((128, 1), 1e-6, _np.float32))
    put("eps5", _np.full((128, 1), 1e-5, _np.float32))
    put("cbias", _np.where(p[None, :] <= p[:, None], 0.0, -1e30).astype(_np.float32))
    put("sbias", _np.where(p[:, None] < p[None, :], 0.0, -1e30).astype(_np.float32))
    strict = (p[:, None] < p[None, :]).astype(_np.float32)
    put("smask", _np.concatenate([strict, _np.ones((128, 128), _np.float32), strict], axis=1))
    put("negtri", -(p[:, None] >= p[None, :]).astype(_np.float32))
    put("negones", -_np.ones((128, 128), _np.float32))
    t = p[:, None, None] + 128 * _np.arange(2)[None, :, None]
    n = _np.arange(16)[None, None, :]
    put("cmpbias", _np.where((16 * n + 31 <= t) & (n < 15), 0.0, -1e30).astype(_np.float32))
    put("headblock", (p[:96, None] // 16 == _np.arange(6)[None, :]).astype(_np.float32))
    return out


def _transposed(a):
    n = a.shape[1] // 128
    return a.T.reshape(n, 128, a.shape[0]).transpose(1, 0, 2).reshape(128, n * a.shape[0]).copy()


def kernel(**inputs):
    import numpy as _np
    import concourse.bacc as _bacc
    from concourse import mybir as _mybir
    from concourse.bass_utils import run_bass_kernel_spmd as _run

    i = {k: _np.asarray(v) for k, v in inputs.items()}
    arrays = {
        "in_x": _transposed(i["x"][0]), "in_mem": _transposed(i["mem"][0]), "in_p": _transposed(i["p_2"][0, 0]),
        "in_positions": _np.ascontiguousarray(_np.broadcast_to(i["positions_2"], (128, SEQ))),
        "in_consts": _pack_consts(i), "in_weights": _pack_weights(i),
    }
    nc = _bacc.Bacc("TRN2", target_bir_lowering=False, num_devices=1)
    args = [nc.dram_tensor(n, a.shape, _mybir.dt.from_np(a.dtype), kind="ExternalInput").ap() for n, a in arrays.items()]
    args.append(nc.dram_tensor("out_0", [128, KD * SEQ], _mybir.dt.float32, kind="ExternalOutput").ap())
    build(nc, *args)
    r = _run(nc, [arrays], core_ids=[0])
    y = r.results[0]["out_0"].reshape(128, KD, SEQ).transpose(2, 1, 0).reshape(1, SEQ, KD * 128)
    return _np.ascontiguousarray(y)
```

```python
import math
from contextlib import ExitStack

import numpy as np

import concourse.bass as bass
from concourse import mybir

F32 = mybir.dt.float32
F32R = mybir.dt.float32r
BF16 = mybir.dt.bfloat16
I32 = mybir.dt.int32
ALU = mybir.AluOpType
ACT = mybir.ActivationFunctionType
X_AXIS = mybir.AxisListType.X

SEQ = 256
KD = 8
TT = SEQ // 128
BLOCK_COLS = 2048
RING = 4
NPS = 6
FF_TILES = 32
UP_PAIRS = 22
MLP_CHUNKS = (8, 8, 8, 8)
UP_CHUNKS = (8, 8, 6)
SPLIT = 4
CONV_TILES = 6
TAPS = 31
PAD = TAPS - 1
QK_SCALE = 64 ** -0.5
MLA_SCALE = 96 ** -0.5
ROUNDER = 1.5 * 2.0 ** 23
SIN_LIMIT = 3.1415925


def pi_parts(value):
    parts = []
    for bits in (8, 8):
        scale = 2.0 ** (bits - math.floor(math.log2(value)))
        parts.append(math.floor(value * scale) / scale)
        value -= parts[-1]
    return parts + [float(np.float32(value))]


def weight_blocks():
    out = []

    def add(name, rows, columns, width=256, first=0, column=0):
        for c in range(column, column + columns, width):
            for r in range(first, first + rows, KD):
                out.append((name, r, min(KD, first + rows - r), c, min(width, column + columns - c)))

    def mlp(into, back, sizes, per_hidden_tile):
        for n in range(len(sizes) + 1):
            if n < len(sizes):
                width = 128 * per_hidden_tile
                add(into, KD, sizes[n] * width, column=n * KD * width)
            if n >= 1:
                add(back, sizes[n - 1], 1024, first=KD * (n - 1))

    add("a_in", KD, 1792)
    add("mem_kv0", KD, 512)
    add("mem_kv1", KD, 512)
    add("out0", KD, 1024)
    mlp("mlp_in0", "mlp_out0", MLP_CHUNKS, 1)
    add("kv", KD, 768)
    add("b_in", KD, 512)
    add("cmp_k", 16, 256)
    add("cmp_v", 16, 256)
    add("b_in", KD, 512, column=512)
    add("gates", KD, 36)
    add("out1", KD, 1024)
    mlp("mlp_in1", "mlp_out1", MLP_CHUNKS, 1)
    add("s_in", KD, 1792)
    add("s_lat", KD, 256)
    add("q_up", 2, 768, 768)
    add("kv_up", 1, 1024, 1024)
    add("o", KD, 1024)
    add("ple", 2, 1024, 1024)
    mlp("up", "down", UP_CHUNKS, 2)
    add("ple_gate", KD, 1024)
    return out


WEIGHT_BLOCKS = weight_blocks()
NBLOCKS = len(WEIGHT_BLOCKS)
DIRECT = ("cmp_k", "cmp_v", "gates", "q_up", "kv_up", "ple")
BLOCK_AT = {(name, r, c): n for n, (name, r, _, c, _) in enumerate(WEIGHT_BLOCKS)}

CONSTS = [
    ("g_mix0", 8), ("g_mix1", 8), ("g_mlp0", 8), ("g_mlp1", 8), ("g_memq0", 1), ("g_memq1", 1), ("g_memk0", 1),
    ("g_memk1", 1), ("g_mem", 8), ("b_glu", 12), ("dw", 186), ("dw_b", 6), ("ln_g", 6), ("ln_b", 6), ("g_kv", 8),
    ("b_gate", 1), ("g_bq", 1), ("g_k", 3), ("pe_k", 32), ("pe_v", 32), ("w2_k", 256), ("w2_v", 128),
    ("g_smix", 8), ("g_qlat", 2), ("g_kvlat", 1), ("g_sb", 4), ("g_mla", 4), ("g_postmix", 8), ("g_ffn", 8),
    ("g_postffn", 8), ("g_plegate", 8), ("b_plegate", 8), ("g_postple", 8), ("conv_b", 44), ("conv_w", 132),
    ("ident", 128), ("ones", 128), ("headsel", 2), ("halfones", 128), ("swap", 96), ("invf", 1), ("eps6", 1),
    ("eps5", 1), ("cbias", 128), ("sbias", 128), ("smask", 384), ("negtri", 128), ("negones", 128),
    ("cmpbias", 32), ("headblock", 6),
]
CONST_AT = {}
NCONST = 0
for _name, _width in CONSTS:
    CONST_AT[_name] = (NCONST, _width)
    NCONST += _width


class Unit:

    def __init__(self, branch, tt, heads, outs, group, first, last):
        self.branch, self.tt, self.heads, self.outs = branch, tt, heads, outs
        self.group, self.first, self.last = group, first, last
        self.keys = SEQ if branch == "mem" else 128 * (tt + 1)


def attention_units(kind):
    units = []

    def group(branch, tt, runs, base):
        for n, heads in enumerate(runs):
            units.append(Unit(branch, tt, heads, [h - base for h in heads], (kind, branch, tt, base),
                              n == 0, n == len(runs) - 1))

    if kind in ("mem0", "mem1"):
        for tt in range(TT):
            group("mem", tt, [(0, 2), (1, 3)], 0)
    elif kind == "nsa":
        for tt in range(TT):
            for base in (0, 6):
                even, odd = tuple(range(base, base + 6, 2)), tuple(range(base + 1, base + 6, 2))
                runs = [even, odd] if tt == 0 else [even[:2], odd[:2], even[2:], odd[2:]]
                for branch in ("slc", "win"):
                    group(branch, tt, runs, base)
    else:
        for tt in range(TT):
            step = 4 if tt == 0 else 2
            group("mla", tt, [tuple(range(h, h + step)) for h in range(0, 8, step)], 0)
    return units


ATTENTIONS = ("mem0", "mem1", "nsa", "mla")
UNITS = {kind: attention_units(kind) for kind in ATTENTIONS}
FIRST_UNIT = {}
_n = 0
for _kind in ATTENTIONS:
    FIRST_UNIT[_kind] = _n
    _n += len(UNITS[_kind])
STAT_COL = {}
_n = 0
for _kind in ATTENTIONS:
    for _u, _unit in enumerate(UNITS[_kind]):
        STAT_COL[_kind, _u] = _n
        _n += len(_unit.heads)
NSTAT = _n


def psum_tiles():
    out = []

    def linear(stage, n, first=0):
        out.extend((stage, t) for t in range(first, first + n))

    def attention(kind):
        n = len(UNITS[kind])
        for w in range(n + 2):
            if w < n:
                out.append((kind, "S", w))
            if 1 <= w <= n:
                out.append((kind, "T", w - 1))

    def mlp(into, back, sizes, per):
        for n in range(len(sizes) + 1):
            if n < len(sizes):
                linear(into, sizes[n] * per, KD * n * per)
            if n >= 1:
                linear(back, KD, KD * (n - 1))

    linear("mem.stat", 1)
    linear("mix0.stat", 1)
    linear("mix0.bc", 1)
    linear("a_in", 4)
    linear("mem.bc", 1)
    linear("a_in", 10, 4)
    linear("qm0.stat", 1)
    linear("mem_kv0", 4)
    linear("qm0.bc", 1)
    linear("mk0.stat", 1)
    linear("mem_kv1", 4)
    linear("mk0.bc", 1)
    linear("mk1.stat", 1)
    linear("mk1.bc", 1)
    attention("mem0")
    linear("mem0.oT", 2)
    linear("ln.mean", 1)
    linear("ln.var", 1)
    linear("out0", 8)
    linear("mlp0.stat", 1)
    linear("mlp0.bc", 1)
    mlp("mlp_in0", "mlp_out0", MLP_CHUNKS, 1)
    linear("mix1.stat", 1)
    linear("mix1.bc", 1)
    linear("kv", 6)
    linear("ks.stat", 1)
    linear("cmp_k", 2)
    linear("ks.bc", 1)
    linear("cmp_v", 2)
    linear("kc", 1)
    linear("vc", 2)
    linear("b_in", 8)
    linear("kc.norm", 1)
    linear("bq.stat", 1)
    linear("gates", 1)
    linear("bq.bc", 4)
    linear("gatesT", 1)
    attention("mem1")
    linear("mem1.oT", 2)
    for tt in range(TT):
        for g in range(2):
            out += [("cmp.S", 2 * (2 * tt + g) + odd) for odd in range(2)]
    for tt in range(TT):
        for g in range(2):
            out.append(("cmp.T", 2 * tt + g))
    attention("nsa")
    linear("nsa.oT", 4)
    linear("out1", 8)
    linear("mlp1.stat", 1)
    linear("mlp1.bc", 1)
    mlp("mlp_in1", "mlp_out1", MLP_CHUNKS, 1)
    linear("smix.stat", 1)
    linear("smix.bc", 1)
    linear("s_in", 14)
    linear("s_lat", 2)
    linear("qlat.stat", 1)
    linear("kvlat.stat", 1)
    linear("qlat.bc", 1)
    linear("kvlat.bc", 1)
    linear("krope.swap", 1)
    for w in range(8 + 1):
        if w < 8:
            out.append(("sb.Z", w))
        if w >= 1:
            out.append(("sb.W", w - 1))
    linear("sb.stat", 1)
    linear("q_up", 8)
    linear("q.swap", 4)
    linear("k_up", 8)
    linear("v_up", 2)
    linear("sb.bc", 1)
    attention("mla")
    linear("mla.oT", 2)
    linear("o", 8)
    linear("postmix.stat", 1)
    linear("postmix.bc", 1)
    linear("ple", 8)
    linear("ffn.stat", 1)
    linear("ffn.bc", 1)
    mlp("up", "down", UP_CHUNKS, 2)
    linear("postffn.stat", 1)
    linear("postffn.bc", 1)
    linear("plegate.stat", 1)
    linear("plegate.bc", 1)
    linear("ple_gate", 8)
    linear("postple.stat", 1)
    linear("postple.bc", 1)
    return out


TILE = {name: n for n, name in enumerate(psum_tiles())}


def output_groups():
    out = []
    for kind in ("mem0", "mem1"):
        out += [u.group for u in UNITS[kind] if u.last]
    out += [("cmp", tt, g) for tt in range(TT) for g in range(2)]
    out += [u.group for u in UNITS["nsa"] if u.last]
    out += [("sb", pair) for pair in range(4)]
    out += [u.group for u in UNITS["mla"] if u.last]
    return out


def tile_of(name, r, c):
    back = name.startswith("mlp_out") or name == "down"
    return (name, 2 * (c // 256) + (KD * (r // KD) if back else 0))


WEIGHT_TILES = []
for _n, (_name, _r, _, _c, _) in enumerate(WEIGHT_BLOCKS):
    if _name not in DIRECT:
        _stage, _t = tile_of(_name, _r, _c)
        WEIGHT_TILES += [(_n, _half, (_stage, _t + _half)) for _half in range(2)]
NTILES = len(WEIGHT_TILES)
WEIGHTS_OF = {tile: w for w, (_, _, tile) in enumerate(WEIGHT_TILES)}
DIRECT_LAST = {"gates": ("gates", 0), "q_up": ("q_up", 7), "kv_up": ("v_up", 1), "ple": ("ple", 7)}


def low_part_engines():
    return ["gpsimd" if tile[0] in ("a_in", "mem_kv0", "mem_kv1") or w % 4 == 3 else "vector"
            for w, (_, _, tile) in enumerate(WEIGHT_TILES)]


LOW_ENGINE = low_part_engines()
LOW_COUNT = [LOW_ENGINE[:w + 1].count(LOW_ENGINE[w]) for w in range(NTILES)]
OUT = {name: n for n, name in enumerate(output_groups())}


def build(nc, x_in, mem_in, p_in, pos_in, consts_in, weights_in, out):
    ctx = ExitStack()
    with ctx:
        def sb(name, shape, dt=F32):
            return ctx.enter_context(nc.sbuf_tensor(name, shape, dt))

        semaphores = {}

        def sem(name):
            if name not in semaphores:
                semaphores[name] = ctx.enter_context(nc.semaphore(name.replace(".", "_")))
            return semaphores[name]

        def flatten(t):
            return t[:, :, :].rearrange("p a b -> p (a b)")

        C = sb("consts", [128, NCONST])
        ring = sb("ring", [128, RING, BLOCK_COLS])
        x = sb("x", [128, KD, SEQ])
        act32 = sb("act32", [128, KD, SEQ])
        act_hi = sb("act_hi", [128, KD, SEQ], F32R)
        act_lo = sb("act_lo", [128, KD, SEQ], F32R)
        split_hi = sb("split_hi", [128, SPLIT, 1024], F32R)
        split_lo = sb("split_lo", [128, SPLIT, 1024], F32R)
        y = sb("y", [128, KD, SEQ])
        sq = sb("sq", [128, KD, SEQ])
        mix = act32
        q = sb("q", [128, KD, SEQ])
        probs = sb("probs", [128, 2, 512])
        probsT = sb("probsT", [128, 2, 512])
        otok = sb("otok", [128, TT, 768])
        memk = sb("memk", [128, 2, 2, SEQ])
        memv = sb("memv", [128, 2, TT, 256])
        kd = sb("kd", [128, 2, 2, SEQ])
        vsw = sb("vsw", [128, TT, 256])
        smalls = sb("smalls", [128, 64])
        rc = sb("rc", [128, 64])
        rb = sb("rb", [128, SEQ])
        negmax = sb("negmax", [128, NSTAT])
        rowmax = sb("rowmax", [128, NSTAT])
        rowsum = sb("rowsum", [128, NSTAT])
        rowinv = sb("rowinv", [128, 16])
        tmp = sb("tmp", [128, 2, 512])
        tmp2 = sb("tmp2", [128, 2, 512])
        ident_b = sb("ident_b", [128, 128], BF16)
        cbias_b = sb("cbias_b", [128, 128], BF16)
        sbias_b = sb("sbias_b", [128, 128], BF16)
        gate_tok = sb("gate_tok", [128, TT, 36])

        with nc.sbuf_tensor("hidden_hi", [128, 2, KD, SEQ], F32R) as hidden_hi, \
                nc.sbuf_tensor("hidden_lo", [128, 2, KD, SEQ], F32R) as hidden_lo:
            pass
        temps = sb("temps", [128, 4 * KD * SEQ])
        hid = temps[:, :]
        glu = hid[:, 0:CONV_TILES * (SEQ + PAD)].rearrange("p (c t) -> p c t", c=CONV_TILES)
        conv = hid[:, 4096:4096 + 1536].rearrange("p (c t) -> p c t", c=CONV_TILES)
        conv2 = q[:, 2:8, :]
        tkv = hid[:, 0:544].rearrange("p (a t) -> p a t", a=2)
        windows = hid[:, 1024:2048].rearrange("p (a l n) -> p a l n", a=2, l=16)
        cmph = hid[:, 2048:2176].rearrange("p (a c n) -> p a c n", a=2, c=2)
        cmph6 = hid[:, 2304:2304 + 384].rearrange("p (c g j n) -> p c g j n", c=2, g=2, j=6)
        vbd = hid[:, 3072:3840].rearrange("p (g d) -> p g d", g=2)
        kcmp = hid[:, 3840:3872]
        kraw = hid[:, 3872:3904]
        krms = hid[:, 3904:4000]
        cmps = hid[:, 4096:4096 + 4 * 96].rearrange("p (u n) -> p u n", u=4)
        cmpp = hid[:, 4608:4608 + 4 * 96].rearrange("p (u n) -> p u n", u=4)
        cmppT = hid[:, 5120:5120 + 4 * 128].rearrange("p (u n) -> p u n", u=4)
        gates = hid[:, 5632:5888]
        ksraw = hid[:, 6144:6656].rearrange("p (a t) -> p a t", a=2)
        sbv = hid[:, 0:1024].rearrange("p (a n) -> p a n", a=2)
        qcat = hid[:, 1024:3072].rearrange("p (h t) -> p h t", h=8)
        kcat = hid[:, 3072:5120].rearrange("p (h t) -> p h t", h=8)
        vmla = hid[:, 5120:6144].rearrange("p (a n) -> p a n", a=2)
        lat = hid[:, 6144:6144 + 768].rearrange("p (a t) -> p a t", a=3)
        cosT = hid[:, 6912:7168]
        sinT = hid[:, 7168:7424]
        krope = hid[:, 7424:7680]
        latn = hid[:, 7680:7680 + 512].rearrange("p (a t) -> p a t", a=2)
        kvn = mix[:, 7, :]
        sp = memk[:, :, :, :].rearrange("p a b c -> p (a b c)")[:, 0:768].rearrange("p (s n) -> p s n", s=2)
        wt = memv[:, :, :, :].rearrange("p a b c -> p (a b c)")[:, 0:768].rearrange("p (s n) -> p s n", s=2)
        osb = y[:, 0:4, :]
        zt = y[:, 4:7, :].rearrange("p a b -> p (a b)").rearrange("p (s n) -> p s n", s=2)
        padded = flatten(sq)[:, 0:4 * (SEQ + 2)].rearrange("p (s t) -> p s t", s=4)
        slots = flatten(tmp).rearrange("p (s t) -> p s t", s=4)
        slots2 = flatten(tmp2).rearrange("p (s t) -> p s t", s=4)
        pT = sb("pT", [128, 2, SEQ])
        pos = sb("pos", [128, SEQ], I32)

        banks = [ctx.enter_context(nc.psum_tensor(f"bank{n}", [128, 512], F32)) for n in range(NPS)]
        obanks = [ctx.enter_context(nc.psum_tensor(f"obank{n}", [128, 512], F32)) for n in range(2)]

        def const(name, a=0, n=None):
            at, width = CONST_AT[name]
            return C[:, at + a:at + (width if n is None else a + n)]

        def block_done(eng, b):
            name, r, _, c, _ = WEIGHT_BLOCKS[b]
            if name in DIRECT_LAST:
                wait_tile(eng, *DIRECT_LAST[name])
            elif name in DIRECT:
                if r:
                    wait_tile(eng, name, 1)
                else:
                    eng.wait_ge(sem("compress_used"), 1 if name == "cmp_k" else 2)
            else:
                for half in range(2):
                    low_ready(eng, WEIGHTS_OF[tile_of(name, r, c)[0], tile_of(name, r, c)[1] + half])

        def low_ready(eng, w):
            eng.wait_ge(sem(f"low_{LOW_ENGINE[w]}"), LOW_COUNT[w])

        def raw_weights(w):
            b, half, _ = WEIGHT_TILES[w]
            n = 128 * WEIGHT_BLOCKS[b][2]
            return ring[:, b % RING, n * half:n * half + n], n

        def split_high(act, w):
            if w >= NTILES:
                return
            b = WEIGHT_TILES[w][0]
            act.wait_ge(sem(f"weights_in{b % RING}"), 16 * (b // RING + 1))
            if w >= SPLIT:
                wait_tile(act, *WEIGHT_TILES[w - SPLIT][2])
            src, n = raw_weights(w)
            nc.scalar.activation(split_hi[:, w % SPLIT, 0:n], src, ACT.Copy).then_inc(sem("high_parts"), 1)

        def split_low(eng, engine, w):
            if w >= NTILES or LOW_ENGINE[w] != engine:
                return
            eng.wait_ge(sem("high_parts"), w + 1)
            src, n = raw_weights(w)
            (nc.vector if engine == "vector" else nc.gpsimd).tensor_tensor(
                split_lo[:, w % SPLIT, 0:n], src, split_hi[:, w % SPLIT, 0:n].bitcast(F32), ALU.subtract)\
                .then_inc(sem(f"low_{engine}"), 1)

        def bank(*tile):
            return banks[TILE[tile] % NPS]

        def wait_tile(eng, *tile):
            eng.wait_ge(sem("psum_ready"), TILE[tile] + 1)

        def emptied(*tile):
            return sem(f"bank_emptied{TILE[tile] % NPS}")

        def wait_emptied(eng, *tile):
            eng.wait_ge(emptied(*tile), TILE[tile] // NPS + 1)

        def obank(name):
            return obanks[OUT[name] % 2]

        def wait_out(eng, name):
            eng.wait_ge(sem("out_ready"), OUT[name] + 1)

        def out_emptied(name):
            return sem(f"obank_emptied{OUT[name] % 2}")

        def wait_out_emptied(eng, name):
            eng.wait_ge(out_emptied(name), OUT[name] // 2 + 1)

        def flat(ap):
            return ap.rearrange("p a b -> p (a b)")

        def bcast(ap, n):
            return ap.unsqueeze(2).to_broadcast([ap.shape[0], ap.shape[1], n])

        def rows(ap, n):
            return ap.unsqueeze(1).to_broadcast([ap.shape[0], n, ap.shape[1]])

        RC = {"mem": 0, "mix0": 2, "mlp0": 4, "mix1": 6, "mlp1": 8, "smix": 10, "postmix": 12, "ffn": 14,
              "postffn": 16, "plegate": 18, "postple": 20, "qlat": 22, "kvlat": 24, "sb": 26, "mla": 28,
              "qm0": 32, "mk0": 32, "mk1": 32, "ks": 32, "bq": 32}
        HEAD_NORMS = {"qm0": 2, "mk0": 2, "mk1": 2, "ks": 2, "bq": 8}

        block = ctx.enter_context(nc.Block())

        @block.sync
        def _(sp_):
            def load(b):
                _, _, kts, _, width = WEIGHT_BLOCKS[b]
                sp_.dma_start(ring[:, b % RING, 0:kts * width], weights_in[b, :, 0:kts * width])\
                   .then_inc(sem(f"weights_in{b % RING}"), 16)

            for b in range(NBLOCKS):
                if b >= RING:
                    block_done(sp_, b - RING)
                load(b)
            sp_.wait_ge(sem("result"), KD)
            sp_.dma_start(out, flat(x[:, :, :])).then_inc(sem("stored"), 16)
            sp_.wait_ge(sem("stored"), 16)

        @block.tensor
        def _(pe):
            def take(*tile):
                n = TILE[tile]
                if n >= NPS:
                    pe.wait_ge(sem(f"bank_emptied{n % NPS}"), n // NPS)
                return banks[n % NPS]

            def mm(dst, lhsT, rhs, start=True, stop=True):
                return nc.tensor.matmul(dst, lhsT, rhs, start=start, stop=stop)

            def ready(last):
                last.then_inc(sem("psum_ready"), 1)

            def product(dst, stationary, moving, start, stop):
                for n, (i, j) in enumerate(((0, 0), (0, 1), (1, 0))):
                    last = mm(dst, stationary[i], moving[j], start and n == 0, stop and n == 2)
                return last

            def split_tile(stage, t):
                w = WEIGHTS_OF[stage, t]
                low_ready(pe, w)
                kts = WEIGHT_BLOCKS[WEIGHT_TILES[w][0]][2]
                return [part[:, w % SPLIT, 0:128 * kts].rearrange("p (k c) -> p k c", k=kts)
                        for part in (split_hi, split_lo)], kts

            def linear(stage, first, count, act):
                for t in range(first, first + count):
                    w, kts = split_tile(stage, t)
                    dst = take(stage, t)
                    for k in range(kts):
                        last = product(dst[:, 0:SEQ], [part[:, k, :] for part in w], [part[:, k, :] for part in act],
                                       k == 0, k == kts - 1)
                    ready(last)

            def linear_tokens(stage, first, count, act):
                for t in range(first, first + count):
                    w, kts = split_tile(stage, t)
                    dst = take(stage, t)
                    for tt in range(TT):
                        tok = slice(128 * tt, 128 * tt + 128)
                        for k in range(kts):
                            last = product(dst[:, tok], [part[:, k, tok] for part in act], [part[:, k, :] for part in w],
                                           k == 0, k == kts - 1)
                    ready(last)

            def full_stat(name, nt, src=None, signal=None):
                src = sq if src is None else src
                pe.wait_ge(sem(f"{name}.squares"), nt if signal is None else signal)
                dst = take(f"{name}.stat", 0)
                for tt in range(TT):
                    for k in range(nt):
                        last = mm(dst[:, tt:tt + 1], src[:, k, 128 * tt:128 * tt + 128], const("ones", 0, 1),
                                  k == 0, k == nt - 1)
                ready(last)

            def full_bcast(name):
                pe.wait_ge(sem(f"{name}.rc"), 1)
                dst = take(f"{name}.bc", 0)
                for tt in range(TT):
                    c = RC[name] + tt
                    last = mm(dst[:, 128 * tt:128 * tt + 128], rc[:, c:c + 1].to_broadcast([128, 128]), const("ident"))
                ready(last)

            def head_stat(name):
                nt = HEAD_NORMS[name]
                pe.wait_ge(sem(f"{name}.squares"), 1)
                dst = take(f"{name}.stat", 0)
                for tt in range(TT):
                    for k in range(nt):
                        c = tt * 2 * nt + 2 * k
                        last = mm(dst[:, c:c + 2], sq[:, k, 128 * tt:128 * tt + 128], const("headsel"))
                ready(last)

            def head_bcast(name):
                nt = HEAD_NORMS[name]
                pe.wait_ge(sem(f"{name}.rc"), 1)
                for pair in range(nt // 2):
                    dst = take(f"{name}.bc", pair)
                    for k in (2 * pair, 2 * pair + 1):
                        for tt in range(TT):
                            c = RC[name] + tt * 2 * nt + 2 * k
                            at = (k % 2) * SEQ + 128 * tt
                            for i in range(2):
                                last = mm(dst[64 * i:64 * i + 64, at:at + 128],
                                          rc[:, c + i:c + i + 1].to_broadcast([128, 64]), const("ident"))
                    ready(last)

            def transpose(dst, src):
                k = src.shape[0]
                return nc.tensor.transpose(dst, src, const("ident")[0:k, 0:k])

            def operands(u, h):
                tok = slice(128 * u.tt, 128 * u.tt + 128)
                half = slice(64 * (h % 2), 64 * (h % 2) + 64)
                return tok, half

            def scores(kind, u, n):
                if n == 0 and kind == "nsa":
                    wait_emptied(pe, "kv", 4)
                    wait_emptied(pe, "kv", 5)
                dst = take(kind, "S", n)
                for i, h in enumerate(u.heads):
                    tok, half = operands(u, h)
                    if kind in ("mem0", "mem1"):
                        a = q[half, (6 if kind == "mem1" else 0) + h // 2, tok]
                        b = memk[half, int(kind[3]), h // 2, 0:u.keys]
                    elif kind == "nsa":
                        a = q[half, h // 2, tok]
                        b = kd[half, 0 if u.branch == "slc" else 1, h // 6, 0:u.keys]
                    else:
                        a = qcat[0:96, h, tok]
                        b = kcat[0:96, h, 0:u.keys]
                    masked = u.branch != "mem"
                    last = mm(dst[:, i * u.keys:(i + 1) * u.keys], a, b, True, not masked)
                    if masked:
                        at = i * u.keys + 128 * u.tt
                        last = mm(dst[:, at:at + 128], ident_b[:, :], cbias_b[:, :], False, True)
                ready(last)

            def probs_transposed(kind, u, n):
                slot = (FIRST_UNIT[kind] + n) % 2
                wait_emptied(pe, kind, "S", n)
                dst = take(kind, "T", n)
                for i in range(len(u.heads) * u.keys // 128):
                    last = transpose(dst[:, 128 * i:128 * i + 128], probs[:, slot, 128 * i:128 * i + 128])
                ready(last)

            def outputs(kind, u, n):
                slot = (FIRST_UNIT[kind] + n) % 2
                wait_emptied(pe, kind, "T", n)
                o = OUT[u.group]
                if u.first and o >= 2:
                    pe.wait_ge(out_emptied(u.group), o // 2)
                dst = obank(u.group)
                nk = u.keys // 128
                for i, h in enumerate(u.heads):
                    for k in range(nk):
                        if u.branch == "mem":
                            v = memv[:, int(kind[3]), k, 64 * h:64 * h + 64]
                        elif kind == "nsa":
                            c = (0 if u.branch == "slc" else 128) + 64 * (h // 6)
                            v = vsw[:, k, c:c + 64]
                        else:
                            v = vmla[:, k, 64 * h:64 * h + 64]
                        at = 64 * u.outs[i]
                        c = 128 * (i * nk + k)
                        last = mm(dst[:, at:at + 64], probsT[:, slot, c:c + 128], v, k == 0, k == nk - 1)
                if u.last:
                    last.then_inc(sem("out_ready"), 1)

            def attention(kind):
                units = UNITS[kind]
                for w in range(len(units) + 2):
                    if w < len(units):
                        scores(kind, units[w], w)
                    if 1 <= w <= len(units):
                        probs_transposed(kind, units[w - 1], w - 1)
                    if w >= 2:
                        outputs(kind, units[w - 2], w - 2)

            projected = (act_hi, act_lo)

            def chunk_of(n):
                return [part[:, n % 2, :, :] for part in (hidden_hi, hidden_lo)]

            def mlp(into, back, signal, sizes, per, act):
                for n in range(len(sizes) + 1):
                    if n < len(sizes):
                        linear(into, KD * n * per, sizes[n] * per, act)
                    if n >= 1:
                        pe.wait_ge(sem(signal), KD * (n - 1) + sizes[n - 1])
                        linear(back, KD * (n - 1), KD, chunk_of(n - 1))

            def block_ready(name, r=0):
                b = BLOCK_AT[name, r, 0]
                pe.wait_ge(sem(f"weights_in{b % RING}"), 16 * (b // RING + 1))
                _, _, kts, _, width = WEIGHT_BLOCKS[b]
                return ring[:, b % RING, 0:kts * width].rearrange("p (k c) -> p k c", k=kts)

            pe.wait_ge(sem("consts_in"), 16)
            full_stat("mem", KD, src=q, signal=1)
            full_stat("mix0", KD, signal=1)
            full_bcast("mix0")
            pe.wait_ge(sem("mix0.act"), 1)
            linear("a_in", 0, 4, projected)
            full_bcast("mem")
            linear("a_in", 4, 10, projected)
            head_stat("qm0")
            for l in range(2):
                if l == 0:
                    pe.wait_ge(sem("mem.act"), 1)
                linear(f"mem_kv{l}", 0, 2, chunk_of(1))
                linear_tokens(f"mem_kv{l}", 2, 2, chunk_of(1))
                if l == 0:
                    head_bcast("qm0")
                    head_stat("mk0")
                else:
                    head_bcast("mk0")
                    head_stat("mk1")
            head_bcast("mk1")
            for stage in ("qm0.bc", "mk0.bc", "mk1.bc"):
                wait_emptied(pe, stage, 0)
            for l in range(2):
                for t in (2, 3):
                    wait_emptied(pe, f"mem_kv{l}", t)
            attention("mem0")

            def mem_out_transposed(kind):
                for tt in range(TT):
                    pe.wait_ge(sem(f"{kind}.o"), tt + 1)
                    dst = take(f"{kind}.oT", tt)
                    for i in range(2):
                        last = transpose(dst[:, 128 * i:128 * i + 128], otok[:, tt, 128 * i:128 * i + 128])
                    ready(last)

            mem_out_transposed("mem0")
            pe.wait_ge(sem("conv.done"), CONV_TILES)
            dst = take("ln.mean", 0)
            for c in range(CONV_TILES):
                last = mm(dst[:, 0:SEQ], const("ones"), conv[:, c, :], c == 0, c == CONV_TILES - 1)
            ready(last)
            pe.wait_ge(sem("ln.squares"), 1)
            dst = take("ln.var", 0)
            for c in range(CONV_TILES):
                last = mm(dst[:, 0:SEQ], const("ones"), sq[:, c, :], c == 0, c == CONV_TILES - 1)
            ready(last)
            pe.wait_ge(sem("mixed0.act"), CONV_TILES)
            for tt in range(TT):
                wait_emptied(pe, "mem0.oT", tt)
            linear("out0", 0, KD, projected)

            def mlp_block(l):
                full_stat(f"mlp{l}", KD)
                full_bcast(f"mlp{l}")
                pe.wait_ge(sem(f"mlp{l}.act"), KD // 2)
                mlp(f"mlp_in{l}", f"mlp_out{l}", f"mlp{l}.hidden", MLP_CHUNKS, 1, projected)

            mlp_block(0)
            full_stat("mix1", KD)
            full_bcast("mix1")
            pe.wait_ge(sem("kv.act"), KD)
            linear("kv", 0, 4, chunk_of(0))
            linear_tokens("kv", 4, 2, chunk_of(0))
            head_stat("ks")

            def compress(n, a):
                pe.wait_ge(sem(f"windows_{n}"), 1)
                dst = [take(f"cmp_{n}", c) for c in range(2)]
                for half in range(2):
                    w = block_ready(f"cmp_{n}", KD * half)
                    for c in range(2):
                        for k in range(KD):
                            last = mm(dst[c][:, 0:32], w[:, k, 128 * c:128 * c + 128], windows[:, a, 8 * half + k, :],
                                      half + k == 0, half == 1 and k == KD - 1)
                        if half == 1 and c == 0:
                            ready(last)
                    if half == 0:
                        last.then_inc(sem("compress_used"), 1)
                    else:
                        ready(last)

            compress("k", 0)
            head_bcast("ks")
            compress("v", 1)
            wait_emptied(pe, "cmp_k", 1)
            dst = take("kc", 0)
            w2k = const("w2_k").rearrange("p (k c) -> p k c", k=2)
            for k in range(2):
                last = mm(dst[:, 0:32], w2k[:, k, :], cmph[:, 0, k, :], k == 0, k == 1)
            ready(last)
            pe.wait_ge(sem("cmph6"), 1)
            w2v = const("w2_v").rearrange("p (k c) -> p k c", k=2)
            for g in range(2):
                dst = take("vc", g)
                for k in range(2):
                    last = mm(dst[0:96, 0:64], cmph6[:, k, g, :, :].rearrange("p j n -> p (j n)"), w2v[:, k, :], k == 0, k == 1)
                ready(last)
            pe.wait_ge(sem("mix1.act"), KD)
            linear("b_in", 0, KD, projected)
            pe.wait_ge(sem("kc.squares"), 1)
            dst = take("kc.norm", 0)
            ready(mm(dst[:, 0:32], const("halfones"), krms[:, 0:32]))
            head_stat("bq")
            w = block_ready("gates")
            dst = take("gates", 0)
            for k in range(KD):
                last = mm(dst[0:36, 0:SEQ], w[:, k, 0:36], act32[:, k, :], k == 0, k == KD - 1)
            ready(last)
            head_bcast("bq")
            pe.wait_ge(sem("gates.sigmoid"), 1)
            dst = take("gatesT", 0)
            for tt in range(TT):
                last = transpose(dst[:, 36 * tt:36 * tt + 36], gates[0:36, 128 * tt:128 * tt + 128])
            ready(last)
            for pair in range(4):
                wait_emptied(pe, "bq.bc", pair)
            attention("mem1")
            mem_out_transposed("mem1")
            pe.wait_ge(sem("kcmp"), 1)
            for n in range(4):
                tt, g = n // 2, n % 2
                for odd in range(2):
                    dst = take("cmp.S", 2 * n + odd)
                    half = slice(64 * odd, 64 * odd + 64)
                    for i in range(3):
                        last = mm(dst[:, 16 * i:16 * i + 16], q[half, 3 * g + i, 128 * tt:128 * tt + 128],
                                  kcmp[half, 16 * g:16 * g + 16])
                    ready(last)
            for n in range(4):
                pe.wait_ge(sem("cmp.probs"), 1)
                ready(transpose(take("cmp.T", n)[0:96, 0:128], cmpp[:, n, :]))
            for g in range(2):
                wait_emptied(pe, "vc", g)
            for n in range(4):
                tt, g = n // 2, n % 2
                wait_emptied(pe, "cmp.T", n)
                o = OUT["cmp", tt, g]
                if o >= 2:
                    pe.wait_ge(out_emptied(("cmp", tt, g)), o // 2)
                mm(obank(("cmp", tt, g))[:, 0:384], cmppT[0:96, n, :], vbd[0:96, g, :]).then_inc(sem("out_ready"), 1)
            wait_emptied(pe, "ks.bc", 0)
            attention("nsa")
            for n in range(4):
                tt, g = n // 2, n % 2
                pe.wait_ge(sem("nsa.o"), n + 1)
                dst = take("nsa.oT", n)
                for i in range(3):
                    c = 384 * g + 128 * i
                    last = transpose(dst[:, 128 * i:128 * i + 128], otok[:, tt, c:c + 128])
                ready(last)
            for n in range(4):
                wait_emptied(pe, "nsa.oT", n)
            for tt in range(TT):
                wait_emptied(pe, "mem1.oT", tt)
            linear("out1", 0, KD, projected)
            mlp_block(1)
            full_stat("smix", KD)
            full_bcast("smix")
            pe.wait_ge(sem("smix.act"), KD)
            linear("s_in", 0, 8, projected)
            linear_tokens("s_in", 8, 4, projected)
            linear("s_in", 12, 2, projected)
            linear("s_lat", 0, 2, projected)
            full_stat("qlat", 2, signal=1)
            full_stat("kvlat", 1, src=sq[:, 2:3, :], signal=1)
            full_bcast("qlat")
            full_bcast("kvlat")
            wait_emptied(pe, "s_lat", 1)
            dst = take("krope.swap", 0)
            ready(mm(dst[0:96, 0:SEQ], const("swap")[64:96, :], krope[64:96, :]))

            def z_products(dst, h, stop):
                half = slice(64 * (h % 2), 64 * (h % 2) + 64)
                kk, qq = q[half, 4 + h // 2, :], q[half, h // 2, :]
                mm(dst[:, 0:256], kk[:, 0:128], qq[:, 0:256], True, stop)
                return kk, qq

            def sb_scores(h):
                dst = take("sb.Z", h)
                kk, qq = z_products(dst, h, True)
                ready(mm(dst[:, 256:384], kk[:, 128:256], qq[:, 128:256]))

            def sb_weights(h):
                pe.wait_ge(sem("sb.log_keep"), h + 1)
                dst = take("sb.W", h)
                L = sp[:, h % 2, :]
                kk, qq = z_products(dst, h, False)
                mm(dst[:, 0:256], const("negtri"), L[:, 0:256], False, False)
                mm(dst[:, 128:256], const("negones"), L[:, 256:384], False, False)
                mm(dst[:, 0:128], ident_b[:, :], sbias_b[:, :], False, True)
                mm(dst[:, 256:384], kk[:, 128:256], qq[:, 128:256], True, False)
                mm(dst[:, 256:384], const("negtri"), L[:, 256:384], False, False)
                ready(mm(dst[:, 256:384], ident_b[:, :], sbias_b[:, :], False, True))

            def sb_outputs(h):
                wait_emptied(pe, "sb.W", h)
                o = OUT["sb", h // 2]
                if h % 2 == 0 and o >= 2:
                    pe.wait_ge(out_emptied(("sb", h // 2)), o // 2)
                dst = obank(("sb", h // 2))[64 * (h % 2):64 * (h % 2) + 64, :]
                W = wt[:, h % 2, :]
                mm(dst[:, 0:256], sbv[:, 0, 64 * h:64 * h + 64], W[:, 0:256], True, False)
                last = mm(dst[:, 128:256], sbv[:, 1, 64 * h:64 * h + 64], W[:, 256:384], False, True)
                if h % 2:
                    last.then_inc(sem("out_ready"), 1)

            for t in range(8, 12):
                wait_emptied(pe, "s_in", t)
            for w_ in range(10):
                if w_ < 8:
                    sb_scores(w_)
                if 1 <= w_ <= 8:
                    sb_weights(w_ - 1)
                if w_ >= 2:
                    sb_outputs(w_ - 2)
            full_stat("sb", 4)
            wait_emptied(pe, "qlat.bc", 0)
            w = block_ready("q_up")
            for h in range(8):
                dst = take("q_up", h)
                for k in range(2):
                    last = mm(dst[0:96, 0:SEQ], w[:, k, 96 * h:96 * h + 96], latn[:, k, :], k == 0, k == 1)
                ready(last)
            for j in range(4):
                wait_emptied(pe, "q_up", 2 * j)
                wait_emptied(pe, "q_up", 2 * j + 1)
                dst = take("q.swap", j)
                for i in range(2):
                    last = mm(dst[0:96, SEQ * i:SEQ * i + SEQ], const("swap")[64:96, :], qcat[64:96, 2 * j + i, :])
                ready(last)
            wait_emptied(pe, "kvlat.bc", 0)
            w = block_ready("kv_up")
            for h in range(8):
                ready(mm(take("k_up", h)[0:64, 0:SEQ], w[:, 0, 128 * h:128 * h + 64], kvn))
            wv = w[:, 0, :].rearrange("p (h c) -> p h c", h=8)[:, :, 64:128]
            for tt in range(TT):
                ready(mm(take("v_up", tt)[:, :].rearrange("p (h c) -> p h c", h=8), kvn[:, 128 * tt:128 * tt + 128], wv))
            full_bcast("sb")
            pe.wait_ge(sem("qcat"), 4)
            pe.wait_ge(sem("kcat"), 1)
            wait_emptied(pe, "k_up", 7)
            wait_emptied(pe, "v_up", 0)
            wait_emptied(pe, "v_up", 1)
            attention("mla")
            for tt in range(TT):
                pe.wait_ge(sem("mla.o"), tt + 1)
                dst = take("mla.oT", tt)
                for i in range(4):
                    last = transpose(dst[:, 128 * i:128 * i + 128], otok[:, tt, 128 * i:128 * i + 128])
                ready(last)
            pe.wait_ge(sem("o.act"), 2)
            linear("o", 0, KD, projected)
            full_stat("postmix", KD)
            full_bcast("postmix")
            w = block_ready("ple")
            for t in range(KD):
                dst = take("ple", t)
                for k in range(2):
                    last = mm(dst[:, 0:SEQ], w[:, k, 128 * t:128 * t + 128], pT[:, k, :], k == 0, k == 1)
                ready(last)
            full_stat("ffn", KD)
            full_bcast("ffn")
            pe.wait_ge(sem("ffn.act"), KD)
            mlp("up", "down", "ffn.hidden", UP_CHUNKS, 2, projected)
            full_stat("postffn", KD)
            full_bcast("postffn")
            full_stat("plegate", KD)
            full_bcast("plegate")
            pe.wait_ge(sem("plegate.act"), KD)
            linear("ple_gate", 0, KD, projected)
            full_stat("postple", KD)
            full_bcast("postple")

        @block.scalar
        def _(act):
            own = [0]

            def settle(ins):
                own[0] += 1
                ins.then_inc(sem("scalar_step"), 1)
                act.wait_ge(sem("scalar_step"), own[0])

            def do(dst, src, func, bias=0.0, scale=1.0, **more):
                return nc.scalar.activation(dst, src, func, bias=bias, scale=scale, **more)

            def copy(dst, src, scale=1.0):
                return nc.scalar.activation(dst, src, ACT.Copy, scale=scale)

            def root(name, n, dim):
                wait_tile(act, f"{name}.stat", 0)
                c = RC[name]
                do(smalls[:, c:c + n], bank(f"{name}.stat", 0)[:, 0:n], ACT.Sqrt, const("eps6"), 1.0 / dim)\
                    .then_inc(emptied(f"{name}.stat", 0), 1)

            def keep_bcast(name):
                wait_tile(act, f"{name}.bc", 0)
                copy(rb[:, :], bank(f"{name}.bc", 0)[:, 0:SEQ]).then_inc(emptied(f"{name}.bc", 0), 1)

            def empty(tile, dst, src, func=ACT.Copy):
                wait_tile(act, *tile)
                return copy(dst, src).then_inc(emptied(*tile), 1)

            def pump(stage, t):
                split_high(act, WEIGHTS_OF[stage, t] + SPLIT)

            def high(dst, src, signal):
                copy(dst, src).then_inc(sem(signal), 1)

            def squares_of_x(stage, first, norm, inputs, late):
                for t in range(KD):
                    wait_emptied(act, stage, first + t)
                    do(sq[:, t, :], x[:, t, :], ACT.Square).then_inc(sem(f"{norm}.squares"), 1)
                    pump(stage, first + t)
                    if not late:
                        for src, dst, name in inputs:
                            act.wait_ge(sem(f"{name}.gain"), t + 1)
                            high(dst[:, t, :], src[:, t, :], f"{name}.high")
                if late:
                    for src, dst, name in inputs:
                        act.wait_ge(sem(f"{name}.gain"), KD)
                        for t in range(0, KD, 2):
                            high(flat(dst[:, t:t + 2, :]), flat(src[:, t:t + 2, :]), f"{name}.high")

            def exponentials(kind):
                for n, u in enumerate(UNITS[kind]):
                    slot = (FIRST_UNIT[kind] + n) % 2
                    act.wait_ge(sem("negmax"), FIRST_UNIT[kind] + n + 1)
                    ps = bank(kind, "S", n)
                    for i in range(len(u.heads)):
                        c = STAT_COL[kind, n] + i
                        last = do(probs[:, slot, u.keys * i:u.keys * (i + 1)], ps[:, u.keys * i:u.keys * (i + 1)],
                                  ACT.Exp, negmax[:, c:c + 1], MLA_SCALE if kind == "mla" else QK_SCALE,
                                  accum_out=rowsum[:, c:c + 1])
                    last.then_inc(emptied(kind, "S", n), 1)

            act.dma_start(flat(y[:, :, :]), mem_in).then_inc(sem("mem_in"), 16)
            act.dma_start(flat(x[:, :, :]), x_in).then_inc(sem("x_in"), 16)
            act.dma_start(C[:, :], consts_in).then_inc(sem("consts_in"), 16)
            act.dma_start(flat(pT[:, :, :]), p_in).then_inc(sem("p_in"), 16)
            act.dma_start(pos[:, :], pos_in).then_inc(sem("positions_in"), 16)
            act.wait_ge(sem("mem_in"), 16)
            do(flat(q[:, :, :]), flat(y[:, :, :]), ACT.Square).then_inc(sem("mem.squares"), 1)
            act.wait_ge(sem("x_in"), 16)
            do(flat(sq[:, :, :]), flat(x[:, :, :]), ACT.Square).then_inc(sem("mix0.squares"), 1)
            act.wait_ge(sem("consts_in"), 16)
            for w in range(SPLIT):
                split_high(act, w)
            act.wait_ge(sem("mix0.gain"), 1)
            high(flat(act_hi[:, :, :]), flat(act32[:, :, :]), "mix0.high")
            root("mem", 2, 1024)
            root("mix0", 2, 1024)
            keep_bcast("mix0")

            def gate(c):
                act.wait_ge(sem("glu.gate"), c + 1)
                do(tmp[:, c % 2, 256:512], tmp2[:, c % 2, 256:512], ACT.Sigmoid, const("b_glu", 6 + c, 1))\
                    .then_inc(sem("glu.sigmoid"), 1)

            for c in range(CONV_TILES):
                if c >= 2:
                    act.wait_ge(sem("glu.ready"), c - 1)
                for i in range(2):
                    empty(("a_in", 2 * c + i), tmp[:, c % 2, 256 * i:256 * i + 256], bank("a_in", 2 * c + i)[:, 0:SEQ])
                    pump("a_in", 2 * c + i)
                if c >= 1:
                    gate(c - 1)
                if c == 1:
                    wait_emptied(act, "mem.bc", 0)
                    high(flat(hidden_hi[:, 1, :, :]), flat(y[:, :, :]), "mem.high")
            gate(CONV_TILES - 1)
            for i in range(2):
                pump("a_in", 12 + i)
            wait_emptied(act, "a_in", 12)
            wait_emptied(act, "a_in", 13)
            do(flat(sq[:, 0:2, :]), flat(y[:, 0:2, :]), ACT.Square).then_inc(sem("qm0.squares"), 1)
            root("qm0", 8, 64)
            for l in range(2):
                for t in range(2):
                    empty((f"mem_kv{l}", t), y[:, 2 + 2 * l + t, :], bank(f"mem_kv{l}", t)[:, 0:SEQ])
                    pump(f"mem_kv{l}", t)
                for t in range(2):
                    wait_emptied(act, f"mem_kv{l}", t)
                do(flat(sq[:, 0:2, :]), flat(y[:, 2 + 2 * l:4 + 2 * l, :]), ACT.Square).then_inc(sem(f"mk{l}.squares"), 1)
                for t in range(2):
                    empty((f"mem_kv{l}", 2 + t), memv[:, l, :, 128 * t:128 * t + 128],
                          bank(f"mem_kv{l}", 2 + t)[:, 0:256].rearrange("p (a c) -> p a c", a=2))
                    pump(f"mem_kv{l}", 2 + t)
                root(f"mk{l}", 8, 64)
            exponentials("mem0")

            def mem_out(kind):
                for tt in range(TT):
                    wait_tile(act, f"{kind}.oT", tt)
                    copy(act_hi[:, 6:8, 128 * tt:128 * tt + 128],
                         bank(f"{kind}.oT", tt)[:, 0:256].rearrange("p (a t) -> p a t", a=2)).then_inc(sem(f"{kind}.high"), 1)

            mem_out("mem0")
            act.wait_ge(sem("ln.centered"), CONV_TILES)
            do(flat(sq[:, 0:6, :]), flat(conv2), ACT.Square).then_inc(sem("ln.squares"), 1)
            wait_tile(act, "ln.var", 0)
            do(tmp[:, 0, 0:256], bank("ln.var", 0)[:, 0:SEQ], ACT.Sqrt, const("eps5"), 1.0 / 768)\
                .then_inc(emptied("ln.var", 0), 1)
            for c in range(CONV_TILES):
                act.wait_ge(sem("ln.scaled"), c + 1)
                for dst in (mix, act_hi):
                    last = do(dst[:, c, :], conv2[:, c, :], ACT.Silu, const("ln_b", c, 1), const("ln_g", c, 1))
                last.then_inc(sem("mixed0.high"), 1)

            def mlp(l, norm, inputs):
                squares_of_x(f"out{l}", 0, f"mlp{l}", [(act32, act_hi, f"mlp{l}")], True)
                root(f"mlp{l}", 2, 1024)
                keep_bcast(f"mlp{l}")
                into, back = f"mlp_in{l}", f"mlp_out{l}"
                for n in range(len(MLP_CHUNKS) + 1):
                    if n < len(MLP_CHUNKS):
                        for t in range(KD * n, KD * n + KD):
                            wait_emptied(act, into, t)
                            do(slots2[:, t % 4, :], slots[:, t % 4, :], ACT.Square)
                            do(hidden_hi[:, n % 2, t % KD, :], slots[:, t % 4, :], ACT.Square).then_inc(sem(f"mlp{l}.high_hidden"), 1)
                            pump(into, t)
                    if 1 <= n < len(MLP_CHUNKS):
                        for t in range(KD * (n - 1), KD * n):
                            pump(back, t)
                squares_of_x(back, KD * (len(MLP_CHUNKS) - 1), norm, inputs, False)
                root(norm, 2, 1024)
                keep_bcast(norm)

            mlp(0, "mix1", [(y, hidden_hi[:, 0, :, :], "kv"), (act32, act_hi, "mix1")])
            for t in range(4):
                pump("kv", t)
            for t in range(2):
                wait_emptied(act, "kv", 2 + t)
            do(flat(sq[:, 0:2, :]), flat(ksraw), ACT.Square).then_inc(sem("ks.squares"), 1)

            def token_tile(tile, dst, norm):
                wait_tile(act, *tile)
                for tt in range(TT):
                    c = RC[norm] + tt
                    last = copy(dst[:, tt, :], bank(*tile)[:, 128 * tt:128 * tt + 128], rc[:, c:c + 1])
                last.then_inc(emptied(*tile), 1)
                pump(*tile)

            for t in range(2):
                token_tile(("kv", 4 + t), vsw[:, :, 128 * t:128 * t + 128], "mix1")
            root("ks", 8, 64)
            for a, n in enumerate("kv"):
                for c in range(2):
                    wait_tile(act, f"cmp_{n}", c)
                    do(cmph[:, a, c, :], bank(f"cmp_{n}", c)[:, 0:32], ACT.Gelu_apprx_tanh)\
                        .then_inc(emptied(f"cmp_{n}", c), 1)
            empty(("kc", 0), kraw, bank("kc", 0)[:, 0:32])
            wait_emptied(act, "kc", 0)
            do(krms[:, 0:32], kraw, ACT.Square).then_inc(sem("kc.squares"), 1)
            for t in range(KD):
                wait_emptied(act, "b_in", t)
                last = do(sq[:, t, :], y[:, t, :], ACT.Square)
                if t == KD - 1:
                    last.then_inc(sem("bq.squares"), 1)
                pump("b_in", t)
            wait_tile(act, "kc.norm", 0)
            do(krms[:, 32:64], bank("kc.norm", 0)[:, 0:32], ACT.Sqrt, const("eps6"), 1.0 / 64)\
                .then_inc(emptied("kc.norm", 0), 1)
            root("bq", 32, 64)
            wait_emptied(act, "gates", 0)
            do(gates[0:36, :], gates[0:36, :], ACT.Sigmoid, const("b_gate")[0:36, :]).then_inc(sem("gates.sigmoid"), 1)
            exponentials("mem1")
            mem_out("mem1")
            act.wait_ge(sem("cmp.centered"), 1)
            do(flat(cmpp), flat(cmpp), ACT.Exp).then_inc(sem("cmp.probs"), 1)
            exponentials("nsa")
            for n in range(4):
                tt, g = n // 2, n % 2
                wait_tile(act, "nsa.oT", n)
                copy(act_hi[:, 3 * g:3 * g + 3, 128 * tt:128 * tt + 128],
                     bank("nsa.oT", n)[:, 0:384].rearrange("p (a t) -> p a t", a=3)).then_inc(sem("nsa.high"), 1)
            mlp(1, "smix", [(act32, act_hi, "smix")])
            act.wait_ge(sem("angles"), 1)
            do(sinT, tmp2[:, 0, 0:256], ACT.Sin)
            do(cosT, tmp2[:, 0, 256:512], ACT.Sin).then_inc(sem("rope.tables"), 1)
            for t in range(8):
                pump("s_in", t)
            for t in range(4):
                token_tile(("s_in", 8 + t), sbv[:, :, 128 * t:128 * t + 128], "smix")
            for t in range(2):
                pump("s_in", 12 + t)
                wait_emptied(act, "s_in", 12 + t)
            do(flat(sq[:, 0:2, :]), flat(lat[:, 0:2, :]), ACT.Square).then_inc(sem("qlat.squares"), 1)
            for t in range(2):
                pump("s_lat", t)
            wait_emptied(act, "s_lat", 0)
            do(sq[:, 2, :], lat[:, 2, :], ACT.Square).then_inc(sem("kvlat.squares"), 1)
            root("qlat", 2, 256)
            root("kvlat", 2, 128)
            for w in range(9):
                if w < 8:
                    wait_tile(act, "sb.Z", w)
                    if w >= 2:
                        act.wait_ge(sem("sb.log_keep"), w - 1)
                    zs = zt[:, w % 2, :]
                    settle(do(zs, bank("sb.Z", w)[:, 0:384], ACT.Abs))
                    settle(do(zs, zs, ACT.Exp, scale=-1.0))
                    do(zs, zs, ACT.Ln, 1.0).then_inc(sem("sb.log"), 1)
                if w >= 1:
                    wait_tile(act, "sb.W", w - 1)
                    do(wt[:, (w - 1) % 2, :], bank("sb.W", w - 1)[:, 0:384], ACT.Exp).then_inc(emptied("sb.W", w - 1), 1)
                if w >= 3 and w % 2:
                    pair = (w - 3) // 2
                    wait_out_emptied(act, ("sb", pair))
                    do(sq[:, pair, :], osb[:, pair, :], ACT.Square).then_inc(sem("sb.squares"), 1)
            wait_out_emptied(act, ("sb", 3))
            do(sq[:, 3, :], osb[:, 3, :], ACT.Square).then_inc(sem("sb.squares"), 1)
            root("sb", 2, 512)
            for h in range(8):
                empty(("q_up", h), qcat[0:96, h, :], bank("q_up", h)[0:96, 0:SEQ])
            for h in range(8):
                empty(("k_up", h), kcat[0:64, h, :], bank("k_up", h)[0:64, 0:SEQ])
            wait_emptied(act, "sb.bc", 0)
            high(flat(act_hi[:, 0:4, :]), flat(mix[:, 0:4, :]), "sb.high")
            exponentials("mla")
            for tt in range(TT):
                c = RC["mla"] + tt
                wait_out_emptied(act, ("mla", "mla", tt, 0))
                settle(do(flat(sq[:, 0:2, :]), otok[:, tt, 0:512], ACT.Square, accum_out=smalls[:, c:c + 1]))
                do(smalls[:, c + 2:c + 3], smalls[:, c:c + 1], ACT.Sqrt, const("eps6"), 1.0 / 512)\
                    .then_inc(sem("mla.root"), 1)
            for tt in range(TT):
                wait_emptied(act, "mla.oT", tt)
            high(flat(act_hi[:, 4:8, :]), flat(mix[:, 4:8, :]), "mla.high")

            def raw_outputs(stage, norm):
                for t in range(KD):
                    wait_tile(act, stage, t)
                    ps = bank(stage, t)[:, 0:SEQ]
                    do(sq[:, t, :], ps, ACT.Square).then_inc(sem(f"{norm}.squares"), 1)
                    copy(y[:, t, :], ps).then_inc(emptied(stage, t), 1)
                    pump(stage, t)
                root(norm, 2, 1024)

            def squares_after(norm, after):
                for t in range(KD):
                    act.wait_ge(sem(f"{after}.x"), t + 1)
                    do(sq[:, t, :], x[:, t, :], ACT.Square).then_inc(sem(f"{norm}.squares"), 1)
                    act.wait_ge(sem(f"{norm}.gain"), t + 1)
                    high(act_hi[:, t, :], act32[:, t, :], f"{norm}.high")

            raw_outputs("o", "postmix")
            for t in range(KD):
                empty(("ple", t), q[:, t, :], bank("ple", t)[:, 0:SEQ])
            squares_after("ffn", "postmix")
            root("ffn", 2, 1024)
            keep_bcast("ffn")

            def first_taps(c):
                for i, col in enumerate((c, UP_PAIRS + c)):
                    wait_emptied(act, "up", 2 * c + i)
                    sl = (2 * c + i) % 4
                    do(slots[:, sl, :], padded[:, sl, 2:2 + SEQ], ACT.Identity, const("conv_b", col, 1), const("conv_w", 3 * col + 2, 1))\
                        .then_inc(sem("ffn.first_taps"), 1)

            def gelu(c):
                act.wait_ge(sem("ffn.gate"), c + 1)
                do(slots2[:, c % 4, :], slots[:, (2 * c) % 4, :], ACT.Gelu_apprx_tanh).then_inc(sem("ffn.gelu"), 1)

            def high_hidden(c):
                act.wait_ge(sem("ffn.product"), c + 1)
                high(hidden_hi[:, (c // KD) % 2, c % KD, :], slots2[:, c % 4, :], "ffn.high_hidden")

            for n in range(len(UP_CHUNKS) + 1):
                if n < len(UP_CHUNKS):
                    for c in range(KD * n, KD * n + UP_CHUNKS[n]):
                        first_taps(c)
                        for i in range(2):
                            pump("up", 2 * c + i)
                        if c > KD * n:
                            high_hidden(c - 1)
                        gelu(c)
                    high_hidden(c)
                if n >= 1:
                    for t in range(KD * (n - 1), KD * n):
                        if n == len(UP_CHUNKS):
                            wait_emptied(act, "down", t)
                            do(sq[:, t % KD, :], y[:, t % KD, :], ACT.Square).then_inc(sem("postffn.squares"), 1)
                        pump("down", t)
            root("postffn", 2, 1024)
            squares_after("plegate", "postffn")
            root("plegate", 2, 1024)
            keep_bcast("plegate")
            for t in range(KD + 1):
                if t < KD:
                    wait_emptied(act, "ple_gate", t)
                    do(slots2[:, t % 4, :], slots[:, t % 4, :], ACT.Sigmoid, const("b_plegate", t, 1))\
                        .then_inc(sem("ple.sigmoid"), 1)
                    pump("ple_gate", t)
                if t >= 1:
                    act.wait_ge(sem("ple.gated"), t)
                    do(sq[:, t - 1, :], y[:, t - 1, :], ACT.Square).then_inc(sem("postple.squares"), 1)
            root("postple", 2, 1024)

        @block.gpsimd
        def _(pool):
            def tt_(dst, a, b, op):
                return nc.gpsimd.tensor_tensor(dst, a, b, op)

            nc.gpsimd.memset(glu[:, :, 0:PAD], 0.0).then_inc(sem("glu.padded"), 1)
            pool.wait_ge(sem("consts_in"), 16)
            nc.gpsimd.tensor_copy(ident_b[:, :], const("ident"))
            nc.gpsimd.tensor_copy(cbias_b[:, :], const("cbias"))
            nc.gpsimd.tensor_copy(sbias_b[:, :], const("sbias")).then_inc(sem("bf16_consts"), 1)
            done = [0]

            def low_parts(upto):
                while done[0] < min(upto, NTILES):
                    split_low(pool, "gpsimd", done[0])
                    done[0] += 1

            low_parts(SPLIT)
            wait_emptied(pool, "mix0.bc", 0)
            for c in range(CONV_TILES):
                s = c % 2
                wait_emptied(pool, "a_in", 2 * c + 1)
                wait_emptied(pool, "a_in", 2 * c)
                tt_(tmp2[:, s, 256:512], tmp[:, s, 256:512], rb[:, :], ALU.mult).then_inc(sem("glu.gate"), 1)
                tt_(tmp2[:, s, 0:256], tmp[:, s, 0:256], rb[:, :], ALU.mult).then_inc(sem("glu.scaled"), 1)
                pool.wait_ge(sem("glu.scaled"), 2 * c + 1)
                nc.gpsimd.tensor_scalar(tmp2[:, s, 0:256], tmp2[:, s, 0:256], const("b_glu", c, 1), None, ALU.add)\
                    .then_inc(sem("glu.scaled"), 1)
                pool.wait_ge(sem("glu.scaled"), 2 * c + 2)
                pool.wait_ge(sem("glu.sigmoid"), c + 1)
                tt_(glu[:, c, PAD:PAD + SEQ], tmp2[:, s, 0:256], tmp[:, s, 256:512], ALU.mult).then_inc(sem("glu.ready"), 1)
                low_parts(SPLIT + 2 * c + 2)
            low_parts(WEIGHTS_OF["kv", 5] + 1)
            wait_tile(pool, "kv", 5)
            nc.gpsimd.memset(tkv[:, :, 256:272], 0.0).then_inc(sem("tkv.padded"), 1)
            low_parts(WEIGHTS_OF["s_lat", 1] + SPLIT)
            pool.wait_ge(sem("krope.rotated"), 1)
            nc.gpsimd.tensor_copy(kcat[64:96, :, :], rows(tmp[64:96, 1, 256:512], 8)).then_inc(sem("kcat"), 1)
            pool.wait_ge(sem("kcat"), 1)
            low_parts(NTILES)

        @block.vector
        def _(dve):
            own = [0]

            def step(ins):
                own[0] += 1
                ins.then_inc(sem("vector_step"), 1)

            def settle(ins=None):
                if ins is not None:
                    step(ins)
                dve.wait_ge(sem("vector_step"), own[0])

            def tt_(dst, a, b, op):
                return nc.vector.tensor_tensor(dst, a, b, op)

            def ts(dst, a, s, op, s2=None, op2=None):
                if op2 is None:
                    return nc.vector.tensor_scalar(dst, a, s, None, op)
                return nc.vector.tensor_scalar(dst, a, s, s2, op, op2)

            def stt(dst, a, s, b, op0, op1):
                return nc.vector.scalar_tensor_tensor(out=dst, in0=a, scalar=s, in1=b, op0=op0, op1=op1)

            def invert(name, n):
                wait_emptied(dve, f"{name}.stat", 0)
                c = RC[name]
                nc.vector.reciprocal(rc[:, c:c + n], smalls[:, c:c + n]).then_inc(sem(f"{name}.rc"), 1)

            def scaled(tile, dst, src, factor):
                wait_tile(dve, *tile)
                tt_(dst, src, factor, ALU.mult).then_inc(emptied(*tile), 1)

            def pump(stage, t):
                split_low(dve, "vector", WEIGHTS_OF[stage, t] + SPLIT)

            def low(dst_, src, high_, signal):
                tt_(dst_, src, high_.bitcast(F32), ALU.subtract).then_inc(sem(signal), 1)

            def low_input(buffers, name, t, n=1):
                src, high_, low_ = buffers
                dve.wait_ge(sem(f"{name}.high"), t // n + 1)
                low(flat(low_[:, t:t + n, :]), flat(src[:, t:t + n, :]), flat(high_[:, t:t + n, :]), f"{name}.act")

            def add_output(stage, t):
                wait_tile(dve, stage, t)
                tt_(x[:, t % KD, :], x[:, t % KD, :], bank(stage, t)[:, 0:SEQ], ALU.add).then_inc(emptied(stage, t), 1)

            def residual(stage, first, inputs, late):
                for t in range(KD):
                    add_output(stage, first + t)
                    wait_emptied(dve, stage, first + t)
                    for buffers, gname, name in inputs:
                        ts(buffers[0][:, t, :], x[:, t, :], const(gname, t, 1), ALU.mult).then_inc(sem(f"{name}.gain"), 1)
                    pump(stage, first + t)
                    if t >= 1 and not late:
                        for buffers, _, name in inputs:
                            low_input(buffers, name, t - 1)
                for buffers, _, name in inputs:
                    if late:
                        for t in range(0, KD, 2):
                            low_input(buffers, name, t, 2)
                    else:
                        low_input(buffers, name, KD - 1)

            def normed_heads(name, srcs, dsts, gs):
                for pair in range(len(srcs) // 2):
                    wait_tile(dve, f"{name}.bc", pair)
                    for k in (2 * pair, 2 * pair + 1):
                        last = stt(dsts[k], srcs[k], gs[k], bank(f"{name}.bc", pair)[:, 256 * (k % 2):256 * (k % 2) + 256],
                                   ALU.mult, ALU.mult)
                    last.then_inc(emptied(f"{name}.bc", pair), 1)

            def heads_of(ap, outs):
                v = ap.rearrange("p (h d) -> p h d", d=64)
                s = outs[1] - outs[0] if len(outs) > 1 else 1
                return v[:, outs[0]:outs[-1] + 1:s, :]

            def attention(kind, finish):
                units = UNITS[kind]
                scale = MLA_SCALE if kind == "mla" else QK_SCALE
                for w in range(len(units) + 2):
                    if w < len(units):
                        u = units[w]
                        nh, c = len(u.heads), STAT_COL[kind, w]
                        wait_tile(dve, kind, "S", w)
                        s = bank(kind, "S", w)[:, 0:nh * u.keys].rearrange("p (h k) -> p h k", h=nh)
                        settle(nc.vector.reduce_max(rowmax[:, c:c + nh], s, X_AXIS))
                        ts(negmax[:, c:c + nh], rowmax[:, c:c + nh], -scale, ALU.mult).then_inc(sem("negmax"), 1)
                    if 1 <= w <= len(units):
                        slot = (FIRST_UNIT[kind] + w - 1) % 2
                        n = len(units[w - 1].heads) * units[w - 1].keys
                        wait_tile(dve, kind, "T", w - 1)
                        nc.vector.tensor_copy(probsT[:, slot, 0:n], bank(kind, "T", w - 1)[:, 0:n])\
                            .then_inc(emptied(kind, "T", w - 1), 1)
                    if w >= 2 and units[w - 2].last:
                        finish(kind, units[w - 2].group)

            def group_units(kind, group):
                return [(n, u) for n, u in enumerate(UNITS[kind]) if u.group == group]

            def inverse_sums(kind, group):
                us = group_units(kind, group)
                c0 = STAT_COL[kind, us[0][0]]
                total = sum(len(u.heads) for _, u in us)
                wait_emptied(dve, kind, "S", us[-1][0])
                settle(nc.vector.reciprocal(rowinv[:, 0:total], rowsum[:, c0:c0 + total]))
                return us

            def finish_plain(kind, group):
                us = inverse_sums(kind, group)
                wait_out(dve, group)
                _, _, tt, _ = group
                ps = obank(group)
                width = 512 if kind == "mla" else 256
                c = 0
                for _, u in us:
                    nh = len(u.heads)
                    last = tt_(heads_of(otok[:, tt, 0:width], u.outs), heads_of(ps[:, 0:width], u.outs),
                               bcast(rowinv[:, c:c + nh], 64), ALU.mult)
                    c += nh
                last.then_inc(out_emptied(group), 1)
                if kind != "mla":
                    own_ready(group, kind)

            def own_ready(group, kind):
                wait_out_emptied(dve, group)
                dve.sem_inc(sem(f"{kind}.o"), 1)

            def finish_gated(kind, group):
                us = inverse_sums(kind, group)
                _, branch, tt, base = group
                b = 1 if branch == "slc" else 2
                gview = gate_tok[:, tt, :].rearrange("p (h b) -> p h b", b=3)
                c = 0
                for _, u in us:
                    nh = len(u.heads)
                    s = u.heads[1] - u.heads[0] if nh > 1 else 1
                    step(tt_(rowinv[:, c:c + nh], rowinv[:, c:c + nh], gview[:, u.heads[0]:u.heads[-1] + 1:s, b], ALU.mult))
                    c += nh
                settle()
                wait_out(dve, group)
                ps = obank(group)
                c = 0
                part = tmp[:, 0, 0:384]
                for _, u in us:
                    nh = len(u.heads)
                    last = tt_(heads_of(part, u.outs), heads_of(ps[:, 0:384], u.outs), bcast(rowinv[:, c:c + nh], 64), ALU.mult)
                    c += nh
                last.then_inc(out_emptied(group), 1)
                wait_out_emptied(dve, group)
                o = otok[:, tt, 64 * base:64 * base + 384]
                ins = tt_(o, o, part, ALU.add)
                if branch == "win":
                    ins.then_inc(sem("nsa.o"), 1)
                else:
                    settle(ins)

            for w in range(SPLIT):
                split_low(dve, "vector", w)
            dve.wait_ge(sem("consts_in"), 16)
            dve.wait_ge(sem("x_in"), 16)
            for t in range(KD):
                last = ts(act32[:, t, :], x[:, t, :], const("g_mix0", t, 1), ALU.mult)
            last.then_inc(sem("mix0.gain"), 1)
            inputs = (act32, act_hi, act_lo)
            low_input(inputs, "mix0", 0, KD)
            invert("mem", 2)
            invert("mix0", 2)
            dve.wait_ge(sem("mem_in"), 16)
            wait_tile(dve, "mem.bc", 0)
            for t in range(KD):
                last = stt(y[:, t, :], y[:, t, :], const("g_mem", t, 1), bank("mem.bc", 0)[:, 0:SEQ], ALU.mult, ALU.mult)
            last.then_inc(emptied("mem.bc", 0), 1)

            def convolve(c):
                dve.wait_ge(sem("glu.ready"), c + 1)
                if c == 0:
                    dve.wait_ge(sem("glu.padded"), 1)
                sums = (conv[:, c, :], conv2[:, c, :])

                def tap(j):
                    return const("dw", TAPS * c + j, 1)

                step(ts(sums[0], glu[:, c, 0:SEQ], tap(0), ALU.mult, const("dw_b", c, 1), ALU.add))
                step(ts(sums[1], glu[:, c, 1:1 + SEQ], tap(1), ALU.mult))
                for j in range(2, TAPS):
                    dve.wait_ge(sem("vector_step"), own[0] - 1)
                    step(stt(sums[j % 2], glu[:, c, j:j + SEQ], tap(j), sums[j % 2], ALU.mult, ALU.add))
                settle()
                tt_(sums[0], sums[0], sums[1], ALU.add).then_inc(sem("conv.done"), 1)

            for c in range(4):
                convolve(c)
                if c == 0:
                    low_input((y, hidden_hi[:, 1, :, :], hidden_lo[:, 1, :, :]), "mem", 0, KD)
            wait_emptied(dve, "mix0.bc", 0)
            for t in range(2):
                scaled(("a_in", 12 + t), y[:, t, :], bank("a_in", 12 + t)[:, 0:SEQ], rb[:, :])
            convolve(4)
            invert("qm0", 8)
            normed_heads("qm0", [y[:, t, :] for t in range(2)], [q[:, t, :] for t in range(2)], [const("g_memq0")] * 2)
            for l in range(2):
                invert(f"mk{l}", 8)
                normed_heads(f"mk{l}", [y[:, 2 + 2 * l + t, :] for t in range(2)], [memk[:, l, t, :] for t in range(2)],
                             [const(f"g_memk{l}")] * 2)
                if l == 0:
                    convolve(5)
            for stage in ("a_in", "mem_kv0", "mem_kv1"):
                for t in range(14 if stage == "a_in" else 4):
                    pump(stage, t)
            attention("mem0", finish_plain)

            def mem_out(kind):
                for tt in range(TT):
                    dve.wait_ge(sem(f"{kind}.high"), tt + 1)
                    part = slice(128 * tt, 128 * tt + 128)
                    tt_(act_lo[:, 6:8, part], bank(f"{kind}.oT", tt)[:, 0:256].rearrange("p (a t) -> p a t", a=2),
                        act_hi[:, 6:8, part].bitcast(F32), ALU.subtract).then_inc(emptied(f"{kind}.oT", tt), 1)

            mem_out("mem0")
            dve.wait_ge(sem("conv.done"), CONV_TILES)
            wait_tile(dve, "ln.mean", 0)
            for c in range(CONV_TILES):
                ins = stt(conv2[:, c, :], bank("ln.mean", 0)[:, 0:SEQ], -1.0 / 768, conv[:, c, :], ALU.mult, ALU.add)
                ins.then_inc(sem("ln.centered"), 1)
            dve.wait_ge(sem("ln.centered"), CONV_TILES)
            dve.sem_inc(emptied("ln.mean", 0), 1)
            wait_emptied(dve, "ln.var", 0)
            settle(nc.vector.reciprocal(tmp2[:, 0, 0:256], tmp[:, 0, 0:256]))
            for c in range(CONV_TILES):
                tt_(conv2[:, c, :], conv2[:, c, :], tmp2[:, 0, 0:256], ALU.mult).then_inc(sem("ln.scaled"), 1)
            for c in range(CONV_TILES):
                dve.wait_ge(sem("mixed0.high"), c + 1)
                low(act_lo[:, c, :], mix[:, c, :], act_hi[:, c, :], "mixed0.act")

            def mlp(l, inputs_):
                residual(f"out{l}", 0, [(inputs, f"g_mlp{l}", f"mlp{l}")], True)
                invert(f"mlp{l}", 2)
                wait_emptied(dve, f"mlp{l}.bc", 0)
                into, back = f"mlp_in{l}", f"mlp_out{l}"

                def low_hidden(t):
                    n = t // KD
                    dve.wait_ge(sem(f"mlp{l}.high_hidden"), t + 1)
                    low(hidden_lo[:, n % 2, t % KD, :], slots2[:, t % 4, :], hidden_hi[:, n % 2, t % KD, :], f"mlp{l}.hidden")

                for n in range(len(MLP_CHUNKS) + 1):
                    if n < len(MLP_CHUNKS):
                        for t in range(KD * n, KD * n + KD):
                            wait_tile(dve, into, t)
                            stt(slots[:, t % 4, :], bank(into, t)[:, 0:SEQ], 0.0, rb[:, :], ALU.max, ALU.mult)\
                                .then_inc(emptied(into, t), 1)
                            pump(into, t)
                            if t >= KD * n + 2:
                                low_hidden(t - 2)
                        low_hidden(t - 1)
                        low_hidden(t)
                    if 1 <= n < len(MLP_CHUNKS):
                        for t in range(KD * (n - 1), KD * n):
                            add_output(back, t)
                            pump(back, t)
                residual(back, KD * (len(MLP_CHUNKS) - 1), inputs_, False)

            mlp(0, [((y, hidden_hi[:, 0, :, :], hidden_lo[:, 0, :, :]), "g_kv", "kv"), (inputs, "g_mix1", "mix1")])
            invert("mix1", 2)
            wait_emptied(dve, "mix1.bc", 0)
            for t in range(4):
                pump("kv", t)
            wait_tile(dve, "kv", 5)
            for a in range(2):
                scaled(("kv", a), tkv[:, a, 0:SEQ], bank("kv", a)[:, 0:SEQ], rb[:, :])
            for a in range(2):
                scaled(("kv", 2 + a), ksraw[:, a, :], bank("kv", 2 + a)[:, 0:SEQ], rb[:, :])
            for t in (4, 5):
                pump("kv", t)
            dve.wait_ge(sem("tkv.padded"), 1)
            for a, n in enumerate("kv"):
                wait_emptied(dve, "kv", a)
                for g in range(2):
                    src = tkv[64 * g:64 * g + 64, a, :].rearrange("p (n s) -> p s n", s=16)
                    for par in range(2):
                        for half in range(2):
                            pe_ = const(f"pe_{n}", 16 * par + 8 * half, 8)[64 * g:64 * g + 64, :]
                            last = tt_(windows[64 * par:64 * par + 64, a, 8 * half:8 * half + 8, 16 * g:16 * g + 16],
                                       src[:, par:16:2, half:half + 16], bcast(pe_, 16), ALU.add)
                last.then_inc(sem(f"windows_{n}"), 1)
            invert("ks", 8)
            wait_tile(dve, "ks.bc", 0)
            for br in range(2):
                for g in range(2):
                    rows_ = slice(64 * g, 64 * g + 64)
                    for d in range(2):
                        last = stt(kd[64 * d:64 * d + 64, br, g, :], ksraw[rows_, br, :], const("g_k", 1 + br, 1)[rows_, :],
                                   bank("ks.bc", 0)[rows_, 256 * br:256 * br + 256], ALU.mult, ALU.mult)
            last.then_inc(emptied("ks.bc", 0), 1)
            for c in range(2):
                wait_emptied(dve, "cmp_v", c)
                for g in range(2):
                    last = nc.vector.tensor_copy(cmph6[:, c, g, :, :], rows(cmph[:, 1, c, 16 * g:16 * g + 16], 6))
            last.then_inc(sem("cmph6"), 1)
            for g in range(2):
                wait_tile(dve, "vc", g)
                tt_(vbd[0:96, g, :].rearrange("p (h d) -> p h d", h=6), rows(bank("vc", g)[0:96, 0:64], 6),
                    bcast(const("headblock")[0:96, :], 64), ALU.mult).then_inc(emptied("vc", g), 1)
            for t in range(KD):
                scaled(("b_in", t), y[:, t, :], bank("b_in", t)[:, 0:SEQ], rb[:, :])
                pump("b_in", t)
            wait_emptied(dve, "kc.norm", 0)
            settle(nc.vector.reciprocal(krms[:, 64:96], krms[:, 32:64]))
            stt(kcmp, kraw, const("g_k", 0, 1), krms[:, 64:96], ALU.mult, ALU.mult).then_inc(sem("kcmp"), 1)
            invert("bq", 32)
            scaled(("gates", 0), gates[0:36, :], bank("gates", 0)[0:36, 0:SEQ], rb[0:36, :])
            normed_heads("bq", [y[:, t, :] for t in range(KD)], [q[:, t, :] for t in range(KD)],
                         [const("g_bq")] * 6 + [const("g_memq1")] * 2)
            wait_tile(dve, "gatesT", 0)
            settle(nc.vector.tensor_copy(flat(gate_tok[:, :, :]), bank("gatesT", 0)[:, 0:72]))
            dve.sem_inc(emptied("gatesT", 0), 1)
            attention("mem1", finish_plain)
            mem_out("mem1")
            for n in range(4):
                tt = n // 2
                for odd in range(2):
                    tile = ("cmp.S", 2 * n + odd)
                    wait_tile(dve, *tile)
                    dst = cmps[:, n, :].rearrange("p (h k) -> p h k", h=6)[:, odd:6:2, :]
                    stt(dst, bank(*tile)[:, 0:48].rearrange("p (h k) -> p h k", h=3), QK_SCALE,
                        rows(const("cmpbias", 16 * tt, 16), 3), ALU.mult, ALU.add).then_inc(emptied(*tile), 1)
            for odd in range(2):
                wait_emptied(dve, "cmp.S", 6 + odd)
            for n in range(4):
                for odd in range(2):
                    wait_emptied(dve, "cmp.S", 2 * n + odd)
            cs = flat(cmps).rearrange("p (h k) -> p h k", k=16)
            cp = flat(cmpp).rearrange("p (h k) -> p h k", k=16)
            cmax, csum = smalls[:, 0:24], smalls[:, 32:56]
            settle(nc.vector.reduce_max(cmax, cs, X_AXIS))
            settle(ts(cmax, cmax, -1e29, ALU.max))
            tt_(cp, cs, bcast(cmax, 16), ALU.subtract).then_inc(sem("cmp.centered"), 1)
            dve.wait_ge(sem("cmp.probs"), 1)
            settle(nc.vector.reduce_sum(csum, cp, X_AXIS))
            settle(ts(csum, csum, 1e-30, ALU.max))
            settle(nc.vector.reciprocal(csum, csum))
            gates_all = flat(gate_tok[:, :, :]).rearrange("p (h b) -> p h b", b=3)
            settle(tt_(csum, csum, gates_all[:, :, 0], ALU.mult))
            for n in range(4):
                wait_tile(dve, "cmp.T", n)
                nc.vector.tensor_copy(cmppT[0:96, n, :], bank("cmp.T", n)[0:96, 0:128]).then_inc(emptied("cmp.T", n), 1)
            for n in range(4):
                tt, g = n // 2, n % 2
                wait_out(dve, ("cmp", tt, g))
                tt_(otok[:, tt, 384 * g:384 * g + 384].rearrange("p (h d) -> p h d", h=6),
                    obank(("cmp", tt, g))[:, 0:384].rearrange("p (h d) -> p h d", h=6),
                    bcast(csum[:, 6 * n:6 * n + 6], 64), ALU.mult).then_inc(out_emptied(("cmp", tt, g)), 1)
            for n in range(4):
                wait_out_emptied(dve, ("cmp", n // 2, n % 2))
            attention("nsa", finish_gated)
            for n in range(4):
                tt, g = n // 2, n % 2
                dve.wait_ge(sem("nsa.high"), n + 1)
                part = slice(128 * tt, 128 * tt + 128)
                tt_(act_lo[:, 3 * g:3 * g + 3, part], bank("nsa.oT", n)[:, 0:384].rearrange("p (a t) -> p a t", a=3),
                    act_hi[:, 3 * g:3 * g + 3, part].bitcast(F32), ALU.subtract).then_inc(emptied("nsa.oT", n), 1)
            mlp(1, [(inputs, "g_smix", "smix")])
            invert("smix", 2)
            dve.wait_ge(sem("positions_in"), 16)
            wait_tile(dve, "smix.stat", 0)
            f, ang, turns = tmp[:, 0, 0:256], tmp[:, 0, 256:512], tmp[:, 1, 0:256]
            sin_arg, cos_arg = tmp2[:, 0, 0:256], tmp2[:, 0, 256:512]
            two_pi = 2 * math.pi
            parts = pi_parts(two_pi)
            settle(nc.vector.tensor_copy(f, pos[:, :]))
            settle(ts(ang, f, const("invf"), ALU.mult))
            settle(ts(turns, ang, 1.0 / two_pi, ALU.mult, ROUNDER, ALU.add))
            settle(ts(turns, turns, -ROUNDER, ALU.add))
            for part in parts:
                settle(stt(ang, turns, -part, ang, ALU.mult, ALU.add))
            settle(ts(cos_arg, ang, math.pi / 2, ALU.add))
            settle(ts(f, cos_arg, math.pi, ALU.is_gt, -two_pi, ALU.mult))
            settle(tt_(cos_arg, cos_arg, f, ALU.add))
            step(ts(cos_arg, cos_arg, SIN_LIMIT, ALU.min, -SIN_LIMIT, ALU.max))
            settle()
            ts(sin_arg, ang, SIN_LIMIT, ALU.min, -SIN_LIMIT, ALU.max).then_inc(sem("angles"), 1)
            wait_emptied(dve, "smix.bc", 0)
            for t in range(4):
                wait_tile(dve, "s_in", t)
                stt(q[:, t, :], bank("s_in", t)[:, 0:SEQ], QK_SCALE, rb[:, :], ALU.mult, ALU.mult)\
                    .then_inc(emptied("s_in", t), 1)
                pump("s_in", t)
            for t in range(4, 8):
                scaled(("s_in", t), q[:, t, :], bank("s_in", t)[:, 0:SEQ], rb[:, :])
                pump("s_in", t)
            for t in range(8, 12):
                pump("s_in", t)
            for t in range(2):
                scaled(("s_in", 12 + t), lat[:, t, :], bank("s_in", 12 + t)[:, 0:SEQ], rb[:, :])
                pump("s_in", 12 + t)
            scaled(("s_lat", 0), lat[:, 2, :], bank("s_lat", 0)[:, 0:SEQ], rb[:, :])
            scaled(("s_lat", 1), krope[64:96, :], bank("s_lat", 1)[64:96, 0:SEQ], rb[64:96, :])
            for t in range(2):
                pump("s_lat", t)
            invert("qlat", 2)
            invert("kvlat", 2)
            for t in range(2):
                wait_emptied(dve, "s_in", 12 + t)
            wait_tile(dve, "qlat.bc", 0)
            for t in range(2):
                last = stt(latn[:, t, :], lat[:, t, :], const("g_qlat", t, 1), bank("qlat.bc", 0)[:, 0:SEQ], ALU.mult, ALU.mult)
            last.then_inc(emptied("qlat.bc", 0), 1)
            wait_emptied(dve, "s_lat", 0)
            wait_tile(dve, "kvlat.bc", 0)
            stt(kvn, lat[:, 2, :], const("g_kvlat"), bank("kvlat.bc", 0)[:, 0:SEQ], ALU.mult, ALU.mult)\
                .then_inc(emptied("kvlat.bc", 0), 1)
            dve.wait_ge(sem("rope.tables"), 1)
            wait_emptied(dve, "s_lat", 1)
            wait_tile(dve, "krope.swap", 0)
            step(tt_(tmp[64:96, 0, 0:256], krope[64:96, :], cosT[64:96, :], ALU.mult))
            tt_(tmp[64:96, 0, 256:512], bank("krope.swap", 0)[64:96, 0:SEQ], sinT[64:96, :], ALU.mult)\
                .then_inc(emptied("krope.swap", 0), 1)
            settle()
            wait_emptied(dve, "krope.swap", 0)
            tt_(tmp[64:96, 1, 256:512], tmp[64:96, 0, 0:256], tmp[64:96, 0, 256:512], ALU.add).then_inc(sem("krope.rotated"), 1)
            for w in range(10):
                if w < 8:
                    zs = zt[:, w % 2, :]
                    dve.wait_ge(sem("sb.log"), w + 1)
                    stt(zs, bank("sb.Z", w)[:, 0:384], 0.0, zs, ALU.max, ALU.add).then_inc(emptied("sb.Z", w), 1)
                    wait_emptied(dve, "sb.Z", w)
                    tt_(sp[:, w % 2, :], zs, const("smask"), ALU.mult).then_inc(sem("sb.log_keep"), 1)
                if w >= 3 and w % 2:
                    pair = (w - 3) // 2
                    wait_out(dve, ("sb", pair))
                    nc.vector.tensor_copy(osb[:, pair, :], obank(("sb", pair))[:, 0:SEQ]).then_inc(out_emptied(("sb", pair)), 1)
            invert("sb", 2)
            for j in range(4):
                heads = slice(2 * j, 2 * j + 2)
                a, b = (tmp2[64:96, n, :].rearrange("p (h t) -> p h t", h=2) for n in range(2))
                for i in range(2):
                    wait_emptied(dve, "q_up", 2 * j + i)
                step(tt_(a, qcat[64:96, heads, :], rows(cosT[64:96, :], 2), ALU.mult))
                wait_tile(dve, "q.swap", j)
                tt_(b, bank("q.swap", j)[64:96, :].rearrange("p (h t) -> p h t", h=2), rows(sinT[64:96, :], 2), ALU.mult)\
                    .then_inc(emptied("q.swap", j), 1)
                settle()
                wait_emptied(dve, "q.swap", j)
                tt_(qcat[64:96, heads, :], a, b, ALU.add).then_inc(sem("qcat"), 1)
                dve.wait_ge(sem("qcat"), j + 1)
            for tt in range(TT):
                wait_tile(dve, "v_up", tt)
                nc.vector.tensor_copy(vmla[:, tt, :], bank("v_up", tt)[:, :]).then_inc(emptied("v_up", tt), 1)
            wait_tile(dve, "sb.bc", 0)
            for t in range(4):
                last = stt(mix[:, t, :], osb[:, t, :], const("g_sb", t, 1), bank("sb.bc", 0)[:, 0:SEQ], ALU.mult, ALU.mult)
            last.then_inc(emptied("sb.bc", 0), 1)
            dve.wait_ge(sem("sb.high"), 1)
            low(flat(act_lo[:, 0:4, :]), flat(mix[:, 0:4, :]), flat(act_hi[:, 0:4, :]), "o.act")
            attention("mla", finish_plain)
            for tt in range(TT):
                c = RC["mla"] + tt
                dve.wait_ge(sem("mla.root"), tt + 1)
                settle(nc.vector.reciprocal(rc[:, c:c + 1], smalls[:, c + 2:c + 3]))
                ts(otok[:, tt, 0:512], otok[:, tt, 0:512], rc[:, c:c + 1], ALU.mult).then_inc(sem("mla.o"), 1)
            for tt in range(TT):
                wait_tile(dve, "mla.oT", tt)
                tt_(mix[:, 4:8, 128 * tt:128 * tt + 128], bank("mla.oT", tt)[:, :].rearrange("p (a t) -> p a t", a=4),
                    bcast(const("g_mla"), 128), ALU.mult).then_inc(emptied("mla.oT", tt), 1)
            dve.wait_ge(sem("mla.high"), 1)
            low(flat(act_lo[:, 4:8, :]), flat(mix[:, 4:8, :]), flat(act_hi[:, 4:8, :]), "o.act")

            def post_norm(name, gname, stage, after=None):
                if stage:
                    for t in range(KD):
                        wait_emptied(dve, stage, t)
                        pump(stage, t)
                wait_tile(dve, f"{name}.bc", 0)
                for t in range(KD):
                    ins = stt(y[:, t, :], y[:, t, :], const(gname, t, 1), bank(f"{name}.bc", 0)[:, 0:SEQ], ALU.mult, ALU.mult)
                    if t < KD - 1:
                        step(ins)
                    else:
                        ins.then_inc(emptied(f"{name}.bc", 0), 1)
                for t in range(KD):
                    if t == KD - 1:
                        wait_emptied(dve, f"{name}.bc", 0)
                    elif t == 0:
                        settle()
                    tt_(x[:, t, :], x[:, t, :], y[:, t, :], ALU.add)\
                        .then_inc(sem("result" if after is None else f"{name}.x"), 1)
                if after is not None:
                    for t in range(KD):
                        dve.wait_ge(sem(f"{name}.x"), t + 1)
                        ts(act32[:, t, :], x[:, t, :], const(f"g_{after}", t, 1), ALU.mult).then_inc(sem(f"{after}.gain"), 1)
                        if t >= 1:
                            low_input(inputs, after, t - 1)
                    low_input(inputs, after, KD - 1)

            for t in range(KD):
                pump("o", t)
            invert("postmix", 2)
            post_norm("postmix", "g_postmix", None, "ffn")
            invert("ffn", 2)
            wait_emptied(dve, "ffn.bc", 0)
            settle(nc.vector.memset(padded[:, :, 0:2], 0.0))

            def hidden_product(c):
                dve.wait_ge(sem("ffn.gelu"), c + 1)
                tt_(slots2[:, c % 4, :], slots2[:, c % 4, :], slots[:, (2 * c + 1) % 4, :], ALU.mult)\
                    .then_inc(sem("ffn.product"), 1)

            def low_hidden(c):
                n = (c // KD) % 2
                dve.wait_ge(sem("ffn.high_hidden"), c + 1)
                low(hidden_lo[:, n, c % KD, :], slots2[:, c % 4, :], hidden_hi[:, n, c % KD, :], "ffn.hidden")

            def taps(c):
                for k in (1, 0):
                    for i, col in enumerate((c, UP_PAIRS + c)):
                        sl = (2 * c + i) % 4
                        if k == 1:
                            dve.wait_ge(sem("ffn.first_taps"), 2 * c + i + 1)
                        else:
                            dve.wait_ge(sem("vector_step"), own[0] - (1 - i))
                        ins = stt(slots[:, sl, :], padded[:, sl, k:k + SEQ], const("conv_w", 3 * col + k, 1), slots[:, sl, :],
                                  ALU.mult, ALU.add)
                        if k == 0 and i == 0:
                            ins.then_inc(sem("ffn.gate"), 1)
                        else:
                            step(ins)

            for n in range(len(UP_CHUNKS) + 1):
                if n < len(UP_CHUNKS):
                    first = KD * n
                    for c in range(first, first + UP_CHUNKS[n]):
                        for i in range(2):
                            sl = (2 * c + i) % 4
                            scaled(("up", 2 * c + i), padded[:, sl, 2:2 + SEQ], bank("up", 2 * c + i)[:, 0:SEQ], rb[:, :])
                        for i in range(2):
                            pump("up", 2 * c + i)
                        if c > first:
                            settle()
                            hidden_product(c - 1)
                        taps(c)
                        if c > first:
                            low_hidden(c - 1)
                    settle()
                    hidden_product(c)
                    low_hidden(c)
                if n >= 1:
                    for t in range(KD * (n - 1), KD * n):
                        wait_tile(dve, "down", t)
                        ps = bank("down", t)[:, 0:SEQ]
                        dst = y[:, t % KD, :]
                        if n == 1:
                            ins = nc.vector.tensor_copy(dst, ps)
                        else:
                            ins = tt_(dst, dst, ps, ALU.add)
                        ins.then_inc(emptied("down", t), 1)
                        pump("down", t)
            invert("postffn", 2)
            post_norm("postffn", "g_postffn", None, "plegate")
            invert("plegate", 2)
            wait_emptied(dve, "plegate.bc", 0)
            for t in range(KD):
                wait_emptied(dve, "ple", t)
            for t in range(KD + 1):
                if t < KD:
                    scaled(("ple_gate", t), slots[:, t % 4, :], bank("ple_gate", t)[:, 0:SEQ], rb[:, :])
                    pump("ple_gate", t)
                if t >= 1:
                    dve.wait_ge(sem("ple.sigmoid"), t)
                    tt_(y[:, t - 1, :], slots2[:, (t - 1) % 4, :], q[:, t - 1, :], ALU.mult).then_inc(sem("ple.gated"), 1)
            invert("postple", 2)
            dve.wait_ge(sem("ple.gated"), KD)
            post_norm("postple", "g_postple", None)


def _rows(a, width):
    k = a.shape[0] // 128
    return a.reshape(k, 128, width).transpose(1, 0, 2).reshape(128, k * width)


def _pack_weights(i):
    import numpy as _np

    def cols(*parts):
        return _np.concatenate(parts, axis=1)

    u = i["a_w_in"][0]
    a_pairs = [cols(u[:, 128 * c:128 * c + 128], u[:, 768 + 128 * c:896 + 128 * c]) for c in range(6)]
    kv = i["w_kv"]
    part = [kv[:, 128 * n:128 * n + 128] for n in range(6)]
    b = i["b_w_in"][0]
    s = i["w_in_2"][0]
    up = i["w_up_2"][0]
    half = up.shape[1] // 2
    krope = cols(s[:, 1792:1920], _np.zeros((1024, 64), _np.float32), s[:, 1920:1952], _np.zeros((1024, 32), _np.float32))
    full = {
        "a_in": cols(*a_pairs, u[:, 1536:1792]),
        "mem_kv0": i["w_mem_kv"][0], "mem_kv1": i["w_mem_kv"][1],
        "out0": i["w_out"][0], "out1": i["w_out"][1],
        "mlp_in0": i["w_mlp_in"][0], "mlp_in1": i["w_mlp_in"][1],
        "mlp_out0": i["w_mlp_out"][0], "mlp_out1": i["w_mlp_out"][1],
        "kv": cols(part[0], part[1], part[2], part[4], part[3], part[5]),
        "cmp_k": i["cmp_w1_k"], "cmp_v": i["cmp_w1_v"],
        "b_in": b[:, 0:1024], "gates": b[:, 1024:1060],
        "s_in": s[:, 0:1792], "s_lat": krope,
        "q_up": i["w_q_up_2"][0], "kv_up": i["w_kv_up_2"][0],
        "o": i["w_o_2"][0],
        "up": cols(*[cols(up[:, 128 * c:128 * c + 128], up[:, half + 128 * c:half + 128 * c + 128])
                     for c in range(half // 128)]),
        "down": i["w_down_2"][0], "ple": i["w_ple_2"][0], "ple_gate": i["w_ple_gate_2"][0],
    }
    out = _np.zeros((NBLOCKS, 128, BLOCK_COLS), _np.float32)
    for n, (name, r0, kts, c0, width) in enumerate(WEIGHT_BLOCKS):
        block = full[name][128 * r0:128 * (r0 + kts), c0:c0 + width]
        step = width if name in DIRECT else 128
        for c in range(0, width, step):
            out[n, :, kts * c:kts * (c + step)] = _rows(block[:, c:c + step], step)
    return out


def _pack_consts(i):
    import numpy as _np

    out = _np.zeros((128, NCONST), _np.float32)

    def put(name, a):
        a = _np.asarray(a)
        at, width = CONST_AT[name]
        out[:a.shape[0], at:at + width] = a.reshape(a.shape[0], width)

    def vec(name, a):
        put(name, a.reshape(-1, 128).T)

    def twice(a):
        return _np.concatenate([a, a], axis=0)

    for l in range(2):
        vec(f"g_mix{l}", i["norm_mix_g"][l])
        vec(f"g_mlp{l}", i["norm_mlp_g"][l])
        put(f"g_memq{l}", twice(i["mem_q_norm_g"][l])[:, None])
        put(f"g_memk{l}", twice(i["mem_k_norm_g"][l])[:, None])
    vec("g_mem", i["mem_norm_g"])
    vec("b_glu", i["a_b_glu"][0])
    put("dw", i["a_dw"][0].reshape(31, 6, 128).transpose(2, 1, 0).reshape(128, 186))
    vec("dw_b", i["a_dw_b"][0])
    vec("ln_g", i["a_ln_g"][0])
    vec("ln_b", i["a_ln_b"][0])
    vec("g_kv", i["kv_norm_g"])
    put("b_gate", i["b_gate_b"][0][:, None])
    put("g_bq", twice(i["b_q_norm_g"][0])[:, None])
    put("g_k", _np.concatenate([i["k_norm_g"].T, i["k_norm_g"].T], axis=0))
    for n in "kv":
        put(f"pe_{n}", twice(i[f"cmp_pe_{n}"].reshape(16, 2, 64).transpose(2, 1, 0).reshape(64, 32)))
        w2 = i[f"cmp_w2_{n}"].reshape(2, 128, 64).transpose(1, 0, 2)
        put(f"w2_{n}", _np.concatenate([w2, w2], axis=2) if n == "k" else w2)
    for name, key in (("g_smix", "g_pre_mix_2"), ("g_qlat", "g_q_lat_2"), ("g_kvlat", "g_kv_lat_2"),
                      ("g_sb", "g_grp_sb_2"), ("g_mla", "g_grp_mla_2"), ("g_postmix", "g_post_mix_2"),
                      ("g_ffn", "g_pre_ffn_2"), ("g_postffn", "g_post_ffn_2"), ("g_plegate", "g_ple_gate_2"),
                      ("b_plegate", "b_ple_gate_2"), ("g_postple", "g_post_ple_2"), ("conv_b", "conv_b_2")):
        vec(name, i[key][0])
    put("conv_w", i["conv_w_2"][0].reshape(3, 44, 128).transpose(2, 1, 0).reshape(128, 132))

    p = _np.arange(128)
    put("ident", (p[:, None] == p[None, :]).astype(_np.float32))
    put("ones", _np.ones((128, 128), _np.float32))
    put("headsel", (p[:, None] // 64 == _np.arange(2)[None, :]).astype(_np.float32))
    put("halfones", (p[:, None] // 64 == p[None, :] // 64).astype(_np.float32))
    swap = _np.zeros((128, 96), _np.float32)
    for m in range(32):
        swap[64 + (m + 16) % 32, 64 + m] = -1.0 if m < 16 else 1.0
    put("swap", swap)
    inv = (1.0 / (_np.float32(10000.0) ** (_np.arange(0, 32, 2, dtype=_np.float32) / _np.float32(32)))).astype(_np.float32)
    put("invf", _np.tile(inv, 8)[:, None])
    put("eps6", _np.full((128, 1), 1e-6, _np.float32))
    put("eps5", _np.full((128, 1), 1e-5, _np.float32))
    put("cbias", _np.where(p[None, :] <= p[:, None], 0.0, -1e30).astype(_np.float32))
    put("sbias", _np.where(p[:, None] < p[None, :], 0.0, -1e30).astype(_np.float32))
    strict = (p[:, None] < p[None, :]).astype(_np.float32)
    put("smask", _np.concatenate([strict, _np.ones((128, 128), _np.float32), strict], axis=1))
    put("negtri", -(p[:, None] >= p[None, :]).astype(_np.float32))
    put("negones", -_np.ones((128, 128), _np.float32))
    t = p[:, None, None] + 128 * _np.arange(2)[None, :, None]
    n = _np.arange(16)[None, None, :]
    put("cmpbias", _np.where((16 * n + 31 <= t) & (n < 15), 0.0, -1e30).astype(_np.float32))
    put("headblock", (p[:96, None] // 16 == _np.arange(6)[None, :]).astype(_np.float32))
    return out


def _transposed(a):
    n = a.shape[1] // 128
    return a.T.reshape(n, 128, a.shape[0]).transpose(1, 0, 2).reshape(128, n * a.shape[0]).copy()


def kernel(**inputs):
    import numpy as _np
    import concourse.bacc as _bacc
    from concourse import mybir as _mybir
    from concourse.bass_utils import run_bass_kernel_spmd as _run

    i = {k: _np.asarray(v) for k, v in inputs.items()}
    arrays = {
        "in_x": _transposed(i["x"][0]), "in_mem": _transposed(i["mem"][0]), "in_p": _transposed(i["p_2"][0, 0]),
        "in_positions": _np.ascontiguousarray(_np.broadcast_to(i["positions_2"], (128, SEQ))),
        "in_consts": _pack_consts(i), "in_weights": _pack_weights(i),
    }
    nc = _bacc.Bacc("TRN2", target_bir_lowering=False, num_devices=1)
    args = [nc.dram_tensor(n, a.shape, _mybir.dt.from_np(a.dtype), kind="ExternalInput").ap() for n, a in arrays.items()]
    args.append(nc.dram_tensor("out_0", [128, KD * SEQ], _mybir.dt.float32, kind="ExternalOutput").ap())
    build(nc, *args)
    r = _run(nc, [arrays], core_ids=[0])
    y = r.results[0]["out_0"].reshape(128, KD, SEQ).transpose(2, 1, 0).reshape(1, SEQ, KD * 128)
    return _np.ascontiguousarray(y)
```

```python
import math
from contextlib import ExitStack

import numpy as np

import concourse.bass as bass
from concourse import mybir

F32 = mybir.dt.float32
F32R = mybir.dt.float32r
BF16 = mybir.dt.bfloat16
I32 = mybir.dt.int32
ALU = mybir.AluOpType
ACT = mybir.ActivationFunctionType
X_AXIS = mybir.AxisListType.X

SEQ = 256
KD = 8
TT = SEQ // 128
BLOCK_COLS = 2048
RING = 4
NPS = 6
FF_TILES = 32
UP_PAIRS = 22
MLP_CHUNKS = (8, 8, 8, 8)
UP_CHUNKS = (8, 8, 6)
SPLIT = 4
CONV_TILES = 6
TAPS = 31
PAD = TAPS - 1
QK_SCALE = 64 ** -0.5
MLA_SCALE = 96 ** -0.5
ROUNDER = 1.5 * 2.0 ** 23
SIN_LIMIT = 3.1415925


def pi_parts(value):
    parts = []
    for bits in (8, 8):
        scale = 2.0 ** (bits - math.floor(math.log2(value)))
        parts.append(math.floor(value * scale) / scale)
        value -= parts[-1]
    return parts + [float(np.float32(value))]


def weight_blocks():
    out = []

    def add(name, rows, columns, width=256, first=0, column=0):
        for c in range(column, column + columns, width):
            for r in range(first, first + rows, KD):
                out.append((name, r, min(KD, first + rows - r), c, min(width, column + columns - c)))

    def mlp(into, back, sizes, per_hidden_tile):
        for n in range(len(sizes) + 1):
            if n < len(sizes):
                width = 128 * per_hidden_tile
                add(into, KD, sizes[n] * width, column=n * KD * width)
            if n >= 1:
                add(back, sizes[n - 1], 1024, first=KD * (n - 1))

    add("a_in", KD, 1792)
    add("mem_kv0", KD, 512)
    add("mem_kv1", KD, 512)
    add("out0", KD, 1024)
    mlp("mlp_in0", "mlp_out0", MLP_CHUNKS, 1)
    add("kv", KD, 768)
    add("b_in", KD, 512)
    add("cmp_k", 16, 256)
    add("b_in", KD, 512, column=512)
    add("cmp_v", 16, 256)
    add("gates", KD, 36)
    add("out1", KD, 1024)
    mlp("mlp_in1", "mlp_out1", MLP_CHUNKS, 1)
    add("s_in", KD, 1792)
    add("s_lat", KD, 256)
    add("q_up", 2, 768, 768)
    add("kv_up", 1, 1024, 1024)
    add("o", KD, 1024)
    add("ple", 2, 1024, 1024)
    mlp("up", "down", UP_CHUNKS, 2)
    add("ple_gate", KD, 1024)
    return out


WEIGHT_BLOCKS = weight_blocks()
NBLOCKS = len(WEIGHT_BLOCKS)
DIRECT = ("cmp_k", "cmp_v", "gates", "q_up", "kv_up", "ple")
BLOCK_AT = {(name, r, c): n for n, (name, r, _, c, _) in enumerate(WEIGHT_BLOCKS)}

CONSTS = [
    ("g_mix0", 8), ("g_mix1", 8), ("g_mlp0", 8), ("g_mlp1", 8), ("g_memq0", 1), ("g_memq1", 1), ("g_memk0", 1),
    ("g_memk1", 1), ("g_mem", 8), ("b_glu", 12), ("dw", 186), ("dw_b", 6), ("ln_g", 6), ("ln_b", 6), ("ident", 128),
    ("ones", 128), ("headsel", 2), ("eps6", 1), ("eps5", 1), ("g_kv", 8),
    ("b_gate", 1), ("g_bq", 1), ("g_k", 3), ("pe_k", 32), ("pe_v", 32), ("w2_k", 256), ("w2_v", 128),
    ("g_smix", 8), ("g_qlat", 2), ("g_kvlat", 1), ("g_sb", 4), ("g_mla", 4), ("g_postmix", 8), ("g_ffn", 8),
    ("g_postffn", 8), ("g_plegate", 8), ("b_plegate", 8), ("g_postple", 8), ("conv_b", 44), ("conv_w", 132),
    ("halfones", 128), ("swap", 96), ("invf", 1), ("cbias", 128), ("sbias", 128), ("smask", 384), ("negtri", 128), ("negones", 128),
    ("cmpbias", 32), ("headblock", 6),
]
CONST_AT = {}
NCONST = 0
for _name, _width in CONSTS:
    CONST_AT[_name] = (NCONST, _width)
    NCONST += _width
FIRST_CONSTS = CONST_AT["g_kv"][0]


class Unit:

    def __init__(self, branch, tt, heads, outs, group, first, last):
        self.branch, self.tt, self.heads, self.outs = branch, tt, heads, outs
        self.group, self.first, self.last = group, first, last
        self.keys = SEQ if branch == "mem" else 128 * (tt + 1)


def attention_units(kind):
    units = []

    def group(branch, tt, runs, base):
        for n, heads in enumerate(runs):
            units.append(Unit(branch, tt, heads, [h - base for h in heads], (kind, branch, tt, base),
                              n == 0, n == len(runs) - 1))

    if kind in ("mem0", "mem1"):
        for tt in range(TT):
            group("mem", tt, [(0, 2), (1, 3)], 0)
    elif kind == "nsa":
        for tt in range(TT):
            for base in (0, 6):
                even, odd = tuple(range(base, base + 6, 2)), tuple(range(base + 1, base + 6, 2))
                runs = [even, odd] if tt == 0 else [even[:2], odd[:2], even[2:], odd[2:]]
                for branch in ("slc", "win"):
                    group(branch, tt, runs, base)
    else:
        for tt in range(TT):
            step = 4 if tt == 0 else 2
            group("mla", tt, [tuple(range(h, h + step)) for h in range(0, 8, step)], 0)
    return units


ATTENTIONS = ("mem0", "mem1", "nsa", "mla")
UNITS = {kind: attention_units(kind) for kind in ATTENTIONS}
FIRST_UNIT = {}
_n = 0
for _kind in ATTENTIONS:
    FIRST_UNIT[_kind] = _n
    _n += len(UNITS[_kind])
STAT_COL = {}
_n = 0
for _kind in ATTENTIONS:
    for _u, _unit in enumerate(UNITS[_kind]):
        STAT_COL[_kind, _u] = _n
        _n += len(_unit.heads)
NSTAT = _n


def psum_tiles():
    out = []

    def linear(stage, n, first=0):
        out.extend((stage, t) for t in range(first, first + n))

    def normed(name, stage, n):
        linear(stage, 2)
        linear(f"{name}.stat", 1)
        linear(stage, 1, 2)
        linear(f"{name}.bc", 1)
        linear(stage, n - 3, 3)

    def attention(kind):
        n = len(UNITS[kind])
        out.append((kind, "S", 0))
        for w in range(n + 2):
            if w + 1 < n:
                out.append((kind, "S", w + 1))
            if 1 <= w <= n:
                out.append((kind, "T", w - 1))

    def mlp(name, into, back, sizes, per):
        for n in range(len(sizes) + 1):
            if n == 0:
                normed(name, into, sizes[0] * per)
            elif n < len(sizes):
                linear(into, sizes[n] * per, KD * n * per)
            if n >= 1:
                linear(back, KD, KD * (n - 1))

    normed("mix0", "a_in", 6)
    linear("mem.stat", 1)
    linear("a_in", 2, 6)
    linear("mem.bc", 1)
    linear("a_in", 6, 8)
    linear("qm0.stat", 1)
    linear("mem_kv0", 4)
    linear("qm0.bc", 1)
    linear("mk0.stat", 1)
    linear("mem_kv1", 4)
    linear("mk0.bc", 1)
    linear("mk1.stat", 1)
    linear("mk1.bc", 1)
    attention("mem0")
    linear("mem0.oT", 2)
    linear("ln.mean", 1)
    linear("ln.var", 1)
    linear("out0", 8)
    mlp("mlp0", "mlp_in0", "mlp_out0", MLP_CHUNKS, 1)
    normed("mix1", "kv", 6)
    linear("ks.stat", 1)
    linear("b_in", 4)
    linear("cmp_k", 2)
    linear("ks.bc", 1)
    linear("b_in", 4, 4)
    linear("cmp_v", 2)
    linear("kc", 1)
    linear("vc", 2)
    linear("kc.norm", 1)
    linear("bq.stat", 1)
    linear("bq.bc", 4)
    for tt in range(TT):
        for g in range(2):
            out += [("cmp.S", 2 * (2 * tt + g) + odd) for odd in range(2)]
    linear("gates", 1)
    linear("gatesT", 1)
    attention("mem1")
    linear("mem1.oT", 2)
    for tt in range(TT):
        for g in range(2):
            out.append(("cmp.T", 2 * tt + g))
    attention("nsa")
    linear("nsa.oT", 4)
    linear("out1", 8)
    mlp("mlp1", "mlp_in1", "mlp_out1", MLP_CHUNKS, 1)
    normed("smix", "s_in", 14)
    linear("s_lat", 2)
    linear("qlat.stat", 1)
    linear("kvlat.stat", 1)
    linear("qlat.bc", 1)
    linear("kvlat.bc", 1)
    linear("krope.swap", 1)
    for w in range(8 + 1):
        if w < 8:
            out.append(("sb.Z", w))
        if w >= 1:
            out.append(("sb.W", w - 1))
    linear("sb.stat", 1)
    linear("q_up", 8)
    linear("q.swap", 4)
    linear("k_up", 8)
    linear("v_up", 2)
    linear("sb.bc", 1)
    attention("mla")
    linear("mla.oT", 2)
    linear("o", 8)
    linear("postmix.stat", 1)
    linear("postmix.bc", 1)
    linear("ple", 8)
    mlp("ffn", "up", "down", UP_CHUNKS, 2)
    linear("postffn.stat", 1)
    linear("postffn.bc", 1)
    normed("plegate", "ple_gate", 8)
    linear("postple.stat", 1)
    linear("postple.bc", 1)
    return out


TILE = {name: n for n, name in enumerate(psum_tiles())}


def output_groups():
    out = []
    for kind in ("mem0", "mem1"):
        out += [u.group for u in UNITS[kind] if u.last]
    out += [("cmp", tt, g) for tt in range(TT) for g in range(2)]
    out += [u.group for u in UNITS["nsa"] if u.last]
    out += [("sb", pair) for pair in range(4)]
    out += [u.group for u in UNITS["mla"] if u.last]
    return out


def tile_of(name, r, c):
    back = name.startswith("mlp_out") or name == "down"
    return (name, 2 * (c // 256) + (KD * (r // KD) if back else 0))


WEIGHT_TILES = []
for _n, (_name, _r, _, _c, _) in enumerate(WEIGHT_BLOCKS):
    if _name not in DIRECT:
        _stage, _t = tile_of(_name, _r, _c)
        WEIGHT_TILES += [(_n, _half, (_stage, _t + _half)) for _half in range(2)]
NTILES = len(WEIGHT_TILES)
WEIGHTS_OF = {tile: w for w, (_, _, tile) in enumerate(WEIGHT_TILES)}
DIRECT_LAST = {"gates": ("gates", 0), "q_up": ("q_up", 7), "kv_up": ("v_up", 1), "ple": ("ple", 7)}


def low_part_engines():
    return ["gpsimd" if tile[0] in ("a_in", "mem_kv0", "mem_kv1") or w % (2 if tile[0] == "up" else 4) == 1 else "vector"
            for w, (_, _, tile) in enumerate(WEIGHT_TILES)]


LOW_ENGINE = low_part_engines()
LOW_COUNT = [LOW_ENGINE[:w + 1].count(LOW_ENGINE[w]) for w in range(NTILES)]
OUT = {name: n for n, name in enumerate(output_groups())}


def build(nc, x_in, mem_in, p_in, pos_in, consts_in, weights_in, out):
    ctx = ExitStack()
    with ctx:
        def sb(name, shape, dt=F32):
            return ctx.enter_context(nc.sbuf_tensor(name, shape, dt))

        semaphores = {}

        def sem(name):
            if name not in semaphores:
                semaphores[name] = ctx.enter_context(nc.semaphore(name.replace(".", "_")))
            return semaphores[name]

        def flatten(t):
            return t[:, :, :].rearrange("p a b -> p (a b)")

        C = sb("consts", [128, NCONST])
        ring = sb("ring", [128, RING, BLOCK_COLS])
        x = sb("x", [128, KD, SEQ])
        act32 = sb("act32", [128, KD, SEQ])
        act_hi = sb("act_hi", [128, KD, SEQ], F32R)
        act_lo = sb("act_lo", [128, KD, SEQ], F32R)
        split_hi = sb("split_hi", [128, SPLIT, 1024], F32R)
        split_lo = sb("split_lo", [128, SPLIT, 1024], F32R)
        with nc.sbuf_tensor("mlp_hi", [128, KD, SEQ], F32R) as mlp_hi, nc.sbuf_tensor("mlp_lo", [128, KD, SEQ], F32R) as mlp_lo:
            pass
        y = sb("y", [128, KD, SEQ])
        q = sb("q", [128, KD, SEQ])
        sq = sb("sq", [128, KD, SEQ])
        mix = act32
        probs = sb("probs", [128, 2, 512])
        probsT = sb("probsT", [128, 2, 512])
        otok = sb("otok", [128, TT, 768])
        memk = sb("memk", [128, 2, 2, SEQ])
        memv = sb("memv", [128, 2, TT, 256])
        kd = sb("kd", [128, 2, 2, SEQ])
        vsw = sb("vsw", [128, TT, 256])
        smalls = sb("smalls", [128, 64])
        rc = sb("rc", [128, 64])
        rb = sb("rb", [128, SEQ])
        square_sum = sb("square_sum", [128, SEQ])
        unused_roots = sb("unused_roots", [128, 16])
        negmax = sb("negmax", [128, NSTAT])
        rowmax = sb("rowmax", [128, NSTAT])
        rowsum = sb("rowsum", [128, NSTAT])
        rowinv = sb("rowinv", [128, 16])
        tmp = sb("tmp", [128, 2, 512])
        tmp2 = sb("tmp2", [128, 2, 512])
        ident_b = sb("ident_b", [128, 128], BF16)
        cbias_b = sb("cbias_b", [128, 128], BF16)
        sbias_b = sb("sbias_b", [128, 128], BF16)
        gate_tok = sb("gate_tok", [128, TT, 36])

        with nc.sbuf_tensor("hidden_hi", [128, 2, KD, SEQ], F32R) as hidden_hi, \
                nc.sbuf_tensor("hidden_lo", [128, 2, KD, SEQ], F32R) as hidden_lo:
            pass
        temps = sb("temps", [128, 4 * KD * SEQ])
        hid = temps[:, :]
        glu = hid[:, 0:CONV_TILES * (SEQ + PAD)].rearrange("p (c t) -> p c t", c=CONV_TILES)
        conv = hid[:, 4096:4096 + 1536].rearrange("p (c t) -> p c t", c=CONV_TILES)
        conv2 = q[:, 2:8, :]
        tkv = hid[:, 6656:6656 + 544].rearrange("p (a t) -> p a t", a=2)
        windows = hid[:, 1024:2048].rearrange("p (a l n) -> p a l n", a=2, l=16)
        cmph = hid[:, 2048:2176].rearrange("p (a c n) -> p a c n", a=2, c=2)
        cmph6 = hid[:, 2304:2304 + 384].rearrange("p (c g j n) -> p c g j n", c=2, g=2, j=6)
        vbd = hid[:, 3072:3840].rearrange("p (g d) -> p g d", g=2)
        kcmp = hid[:, 3840:3872]
        kraw = hid[:, 3872:3904]
        krms = hid[:, 3904:4000]
        cmps = hid[:, 4096:4096 + 4 * 96].rearrange("p (u n) -> p u n", u=4)
        cmpp = hid[:, 4608:4608 + 4 * 96].rearrange("p (u n) -> p u n", u=4)
        cmppT = hid[:, 5120:5120 + 4 * 128].rearrange("p (u n) -> p u n", u=4)
        gates = hid[:, 5632:5888]
        ksraw = hid[:, 6144:6656].rearrange("p (a t) -> p a t", a=2)
        sbv = hid[:, 0:1024].rearrange("p (a n) -> p a n", a=2)
        qcat = hid[:, 1024:3072].rearrange("p (h t) -> p h t", h=8)
        kcat = hid[:, 3072:5120].rearrange("p (h t) -> p h t", h=8)
        vmla = hid[:, 5120:6144].rearrange("p (a n) -> p a n", a=2)
        lat = hid[:, 6144:6144 + 768].rearrange("p (a t) -> p a t", a=3)
        cosT = hid[:, 6912:7168]
        sinT = hid[:, 7168:7424]
        krope = hid[:, 7424:7680]
        latn = hid[:, 7680:7680 + 512].rearrange("p (a t) -> p a t", a=2)
        kvn = mix[:, 7, :]
        sp = memk[:, :, :, :].rearrange("p a b c -> p (a b c)")[:, 0:768].rearrange("p (s n) -> p s n", s=2)
        wt = memv[:, :, :, :].rearrange("p a b c -> p (a b c)")[:, 0:768].rearrange("p (s n) -> p s n", s=2)
        osb = y[:, 0:4, :]
        zt = y[:, 4:7, :].rearrange("p a b -> p (a b)").rearrange("p (s n) -> p s n", s=2)
        padded = flatten(sq)[:, 0:4 * (SEQ + 2)].rearrange("p (s t) -> p s t", s=4)
        slots = flatten(tmp).rearrange("p (s t) -> p s t", s=4)
        slots2 = flatten(tmp2).rearrange("p (s t) -> p s t", s=4)
        pT = sb("pT", [128, 2, SEQ])
        pos = sb("pos", [128, SEQ], I32)

        banks = [ctx.enter_context(nc.psum_tensor(f"bank{n}", [128, 512], F32)) for n in range(NPS)]
        obanks = [ctx.enter_context(nc.psum_tensor(f"obank{n}", [128, 512], F32)) for n in range(2)]

        def const(name, a=0, n=None):
            at, width = CONST_AT[name]
            return C[:, at + a:at + (width if n is None else a + n)]

        def block_done(eng, b):
            name, r, _, c, _ = WEIGHT_BLOCKS[b]
            if name in DIRECT_LAST:
                wait_tile(eng, *DIRECT_LAST[name])
            elif name in DIRECT:
                if r:
                    wait_tile(eng, name, 1)
                else:
                    eng.wait_ge(sem("compress_used"), 1 if name == "cmp_k" else 2)
            else:
                for half in range(2):
                    low_ready(eng, WEIGHTS_OF[tile_of(name, r, c)[0], tile_of(name, r, c)[1] + half])

        def low_ready(eng, w):
            eng.wait_ge(sem(f"low_{LOW_ENGINE[w]}"), LOW_COUNT[w])

        def raw_weights(w):
            b, half, _ = WEIGHT_TILES[w]
            n = 128 * WEIGHT_BLOCKS[b][2]
            return ring[:, b % RING, n * half:n * half + n], n

        def split_high(act, w):
            if w >= NTILES:
                return
            b = WEIGHT_TILES[w][0]
            act.wait_ge(sem(f"weights_in{b % RING}"), 16 * (b // RING + 1))
            if w >= SPLIT:
                wait_tile(act, *WEIGHT_TILES[w - SPLIT][2])
            src, n = raw_weights(w)
            nc.scalar.activation(split_hi[:, w % SPLIT, 0:n], src, ACT.Copy).then_inc(sem("high_parts"), 1)

        def split_low(eng, engine, w):
            if w >= NTILES or LOW_ENGINE[w] != engine:
                return
            eng.wait_ge(sem("high_parts"), w + 1)
            src, n = raw_weights(w)
            (nc.vector if engine == "vector" else nc.gpsimd).tensor_tensor(
                split_lo[:, w % SPLIT, 0:n], src, split_hi[:, w % SPLIT, 0:n].bitcast(F32), ALU.subtract)\
                .then_inc(sem(f"low_{engine}"), 1)

        def bank(*tile):
            return banks[TILE[tile] % NPS]

        def wait_tile(eng, *tile):
            eng.wait_ge(sem("psum_ready"), TILE[tile] + 1)

        def emptied(*tile):
            return sem(f"bank_emptied{TILE[tile] % NPS}")

        def wait_emptied(eng, *tile):
            eng.wait_ge(emptied(*tile), TILE[tile] // NPS + 1)

        def obank(name):
            return obanks[OUT[name] % 2]

        def wait_out(eng, name):
            eng.wait_ge(sem("out_ready"), OUT[name] + 1)

        def out_emptied(name):
            return sem(f"obank_emptied{OUT[name] % 2}")

        def wait_out_emptied(eng, name):
            eng.wait_ge(out_emptied(name), OUT[name] // 2 + 1)

        def flat(ap):
            return ap.rearrange("p a b -> p (a b)")

        def bcast(ap, n):
            return ap.unsqueeze(2).to_broadcast([ap.shape[0], ap.shape[1], n])

        def rows(ap, n):
            return ap.unsqueeze(1).to_broadcast([ap.shape[0], n, ap.shape[1]])

        RC = {"mem": 0, "mix0": 2, "mlp0": 4, "mix1": 6, "mlp1": 8, "smix": 10, "postmix": 12, "ffn": 14,
              "postffn": 16, "plegate": 18, "postple": 20, "qlat": 22, "kvlat": 24, "sb": 26, "mla": 28,
              "qm0": 32, "mk0": 32, "mk1": 32, "ks": 32, "bq": 32}
        HEAD_NORMS = {"qm0": 2, "mk0": 2, "mk1": 2, "ks": 2, "bq": 8}

        block = ctx.enter_context(nc.Block())

        @block.sync
        def _(sp_):
            def load(b):
                _, _, kts, _, width = WEIGHT_BLOCKS[b]
                sp_.dma_start(ring[:, b % RING, 0:kts * width], weights_in[b, :, 0:kts * width])\
                   .then_inc(sem(f"weights_in{b % RING}"), 16)

            for b in range(NBLOCKS):
                if b >= RING:
                    block_done(sp_, b - RING)
                load(b)
            sp_.wait_ge(sem("result"), KD)
            sp_.dma_start(out, flat(x[:, :, :])).then_inc(sem("stored"), 16)
            sp_.wait_ge(sem("stored"), 16)

        @block.tensor
        def _(pe):
            def take(*tile):
                n = TILE[tile]
                if n >= NPS:
                    pe.wait_ge(sem(f"bank_emptied{n % NPS}"), n // NPS)
                return banks[n % NPS]

            def mm(dst, lhsT, rhs, start=True, stop=True):
                return nc.tensor.matmul(dst, lhsT, rhs, start=start, stop=stop)

            def ready(last):
                last.then_inc(sem("psum_ready"), 1)

            def product(dst, stationary, moving, start, stop):
                for n, (i, j) in enumerate(((0, 0), (0, 1), (1, 0))):
                    last = mm(dst, stationary[i], moving[j], start and n == 0, stop and n == 2)
                return last

            def split_tile(stage, t):
                w = WEIGHTS_OF[stage, t]
                low_ready(pe, w)
                kts = WEIGHT_BLOCKS[WEIGHT_TILES[w][0]][2]
                return [part[:, w % SPLIT, 0:128 * kts].rearrange("p (k c) -> p k c", k=kts)
                        for part in (split_hi, split_lo)], kts

            def linear(stage, first, count, act, arriving=None, arrivals=KD):
                for t in range(first, first + count):
                    w, kts = split_tile(stage, t)
                    dst = take(stage, t)
                    for k in range(kts):
                        if arriving is not None and t == first and k < arrivals:
                            pe.wait_ge(sem(arriving), k + 1)
                        last = product(dst[:, 0:SEQ], [part[:, k, :] for part in w], [part[:, k, :] for part in act],
                                       k == 0, k == kts - 1)
                    ready(last)

            def linear_tokens(stage, first, count, act):
                for t in range(first, first + count):
                    w, kts = split_tile(stage, t)
                    dst = take(stage, t)
                    for tt in range(TT):
                        tok = slice(128 * tt, 128 * tt + 128)
                        for k in range(kts):
                            last = product(dst[:, tok], [part[:, k, tok] for part in act], [part[:, k, :] for part in w],
                                           k == 0, k == kts - 1)
                    ready(last)

            def full_stat(name, nt, src=None, signal=None):
                src = sq if src is None else src
                pe.wait_ge(sem(f"{name}.squares"), nt if signal is None else signal)
                dst = take(f"{name}.stat", 0)
                for tt in range(TT):
                    for k in range(nt):
                        last = mm(dst[:, tt:tt + 1], src[:, k, 128 * tt:128 * tt + 128], const("ones", 0, 1),
                                  k == 0, k == nt - 1)
                ready(last)

            def folded_stat(name):
                pe.wait_ge(sem(f"{name}.folded"), 1)
                dst = take(f"{name}.stat", 0)
                for tt in range(TT):
                    last = mm(dst[:, tt:tt + 1], square_sum[:, 128 * tt:128 * tt + 128], const("ones", 0, 1))
                ready(last)

            def full_bcast(name):
                pe.wait_ge(sem(f"{name}.rc"), 1)
                dst = take(f"{name}.bc", 0)
                for tt in range(TT):
                    c = RC[name] + tt
                    last = mm(dst[:, 128 * tt:128 * tt + 128], rc[:, c:c + 1].to_broadcast([128, 128]), const("ident"))
                ready(last)

            def normed(name, stage, act):
                linear(stage, 0, 2, act, f"{name}.act")
                folded_stat(name)
                linear(stage, 2, 1, act)
                full_bcast(name)

            def head_stat(name):
                nt = HEAD_NORMS[name]
                pe.wait_ge(sem(f"{name}.squares"), 1)
                dst = take(f"{name}.stat", 0)
                for tt in range(TT):
                    for k in range(nt):
                        c = tt * 2 * nt + 2 * k
                        last = mm(dst[:, c:c + 2], sq[:, k, 128 * tt:128 * tt + 128], const("headsel"))
                ready(last)

            def head_bcast(name):
                nt = HEAD_NORMS[name]
                pe.wait_ge(sem(f"{name}.rc"), 1)
                for pair in range(nt // 2):
                    dst = take(f"{name}.bc", pair)
                    for k in (2 * pair, 2 * pair + 1):
                        for tt in range(TT):
                            c = RC[name] + tt * 2 * nt + 2 * k
                            at = (k % 2) * SEQ + 128 * tt
                            for i in range(2):
                                last = mm(dst[64 * i:64 * i + 64, at:at + 128],
                                          rc[:, c + i:c + i + 1].to_broadcast([128, 64]), const("ident"))
                    ready(last)

            def transpose(dst, src):
                k = src.shape[0]
                return nc.tensor.transpose(dst, src, const("ident")[0:k, 0:k])

            def operands(u, h):
                tok = slice(128 * u.tt, 128 * u.tt + 128)
                half = slice(64 * (h % 2), 64 * (h % 2) + 64)
                return tok, half

            def scores(kind, u, n):
                if n == 0 and kind == "nsa":
                    wait_emptied(pe, "kv", 4)
                    wait_emptied(pe, "kv", 5)
                dst = take(kind, "S", n)
                for i, h in enumerate(u.heads):
                    tok, half = operands(u, h)
                    if kind in ("mem0", "mem1"):
                        a = q[half, (6 if kind == "mem1" else 0) + h // 2, tok]
                        b = memk[half, int(kind[3]), h // 2, 0:u.keys]
                    elif kind == "nsa":
                        a = q[half, h // 2, tok]
                        b = kd[half, 0 if u.branch == "slc" else 1, h // 6, 0:u.keys]
                    else:
                        a = qcat[0:96, h, tok]
                        b = kcat[0:96, h, 0:u.keys]
                    masked = u.branch != "mem"
                    last = mm(dst[:, i * u.keys:(i + 1) * u.keys], a, b, True, not masked)
                    if masked:
                        at = i * u.keys + 128 * u.tt
                        last = mm(dst[:, at:at + 128], ident_b[:, :], cbias_b[:, :], False, True)
                ready(last)

            def probs_transposed(kind, u, n):
                slot = (FIRST_UNIT[kind] + n) % 2
                wait_emptied(pe, kind, "S", n)
                dst = take(kind, "T", n)
                for i in range(len(u.heads) * u.keys // 128):
                    last = transpose(dst[:, 128 * i:128 * i + 128], probs[:, slot, 128 * i:128 * i + 128])
                ready(last)

            def outputs(kind, u, n):
                slot = (FIRST_UNIT[kind] + n) % 2
                wait_emptied(pe, kind, "T", n)
                o = OUT[u.group]
                if u.first and o >= 2:
                    pe.wait_ge(out_emptied(u.group), o // 2)
                dst = obank(u.group)
                nk = u.keys // 128
                for i, h in enumerate(u.heads):
                    for k in range(nk):
                        if u.branch == "mem":
                            v = memv[:, int(kind[3]), k, 64 * h:64 * h + 64]
                        elif kind == "nsa":
                            c = (0 if u.branch == "slc" else 128) + 64 * (h // 6)
                            v = vsw[:, k, c:c + 64]
                        else:
                            v = vmla[:, k, 64 * h:64 * h + 64]
                        at = 64 * u.outs[i]
                        c = 128 * (i * nk + k)
                        last = mm(dst[:, at:at + 64], probsT[:, slot, c:c + 128], v, k == 0, k == nk - 1)
                if u.last:
                    last.then_inc(sem("out_ready"), 1)

            def attention(kind):
                units = UNITS[kind]
                scores(kind, units[0], 0)
                for w in range(len(units) + 2):
                    if w + 1 < len(units):
                        scores(kind, units[w + 1], w + 1)
                    if 1 <= w <= len(units):
                        probs_transposed(kind, units[w - 1], w - 1)
                    if w >= 2:
                        outputs(kind, units[w - 2], w - 2)

            projected = (act_hi, act_lo)
            into_mlp = (mlp_hi, mlp_lo)

            def chunk_of(n):
                return [part[:, n % 2, :, :] for part in (hidden_hi, hidden_lo)]

            def mlp(name, into, back, signal, sizes, per, act):
                for n in range(len(sizes) + 1):
                    if n == 0:
                        normed(name, into, act)
                        linear(into, 3, sizes[0] * per - 3, act)
                    elif n < len(sizes):
                        linear(into, KD * n * per, sizes[n] * per, act)
                    if n >= 1:
                        pe.wait_ge(sem(signal), KD * (n - 1) + sizes[n - 1])
                        linear(back, KD * (n - 1), KD, chunk_of(n - 1))

            def block_ready(name, r=0):
                b = BLOCK_AT[name, r, 0]
                pe.wait_ge(sem(f"weights_in{b % RING}"), 16 * (b // RING + 1))
                _, _, kts, _, width = WEIGHT_BLOCKS[b]
                return ring[:, b % RING, 0:kts * width].rearrange("p (k c) -> p k c", k=kts)

            pe.wait_ge(sem("consts_in"), 16)
            normed("mix0", "a_in", projected)
            linear("a_in", 3, 3, projected)
            full_stat("mem", KD, signal=1)
            linear("a_in", 6, 2, projected)
            full_bcast("mem")
            linear("a_in", 8, 6, projected)
            head_stat("qm0")
            for l in range(2):
                if l == 0:
                    pe.wait_ge(sem("mem.act"), 2)
                linear(f"mem_kv{l}", 0, 2, chunk_of(1))
                linear_tokens(f"mem_kv{l}", 2, 2, chunk_of(1))
                if l == 0:
                    head_bcast("qm0")
                    head_stat("mk0")
                else:
                    head_bcast("mk0")
                    head_stat("mk1")
            head_bcast("mk1")
            for stage in ("qm0.bc", "mk0.bc", "mk1.bc"):
                wait_emptied(pe, stage, 0)
            for l in range(2):
                for t in (2, 3):
                    wait_emptied(pe, f"mem_kv{l}", t)
            attention("mem0")

            def mem_out_transposed(kind):
                for tt in range(TT):
                    pe.wait_ge(sem(f"{kind}.o"), tt + 1)
                    dst = take(f"{kind}.oT", tt)
                    for i in range(2):
                        last = transpose(dst[:, 128 * i:128 * i + 128], otok[:, tt, 128 * i:128 * i + 128])
                    ready(last)

            mem_out_transposed("mem0")
            pe.wait_ge(sem("conv.done"), CONV_TILES)
            dst = take("ln.mean", 0)
            for c in range(CONV_TILES):
                last = mm(dst[:, 0:SEQ], const("ones"), conv[:, c, :], c == 0, c == CONV_TILES - 1)
            ready(last)
            pe.wait_ge(sem("ln.squares"), 1)
            dst = take("ln.var", 0)
            for c in range(CONV_TILES):
                last = mm(dst[:, 0:SEQ], const("ones"), sq[:, c, :], c == 0, c == CONV_TILES - 1)
            ready(last)
            for tt in range(TT):
                wait_emptied(pe, "mem0.oT", tt)
            linear("out0", 0, KD, projected, "mixed0.act", CONV_TILES)

            def mlp_block(l):
                mlp(f"mlp{l}", f"mlp_in{l}", f"mlp_out{l}", f"mlp{l}.hidden", MLP_CHUNKS, 1, into_mlp)

            mlp_block(0)
            pe.wait_ge(sem("more_consts_in"), 16)
            normed("mix1", "kv", chunk_of(0))
            linear("kv", 3, 1, chunk_of(0))
            linear_tokens("kv", 4, 2, chunk_of(0))
            head_stat("ks")

            def compress(n, a):
                pe.wait_ge(sem(f"windows_{n}"), 1)
                dst = [take(f"cmp_{n}", c) for c in range(2)]
                for half in range(2):
                    w = block_ready(f"cmp_{n}", KD * half)
                    for c in range(2):
                        for k in range(KD):
                            last = mm(dst[c][:, 0:32], w[:, k, 128 * c:128 * c + 128], windows[:, a, 8 * half + k, :],
                                      half + k == 0, half == 1 and k == KD - 1)
                        if half == 1 and c == 0:
                            ready(last)
                    if half == 0:
                        last.then_inc(sem("compress_used"), 1)
                    else:
                        ready(last)

            pe.wait_ge(sem("queries.act"), KD)
            linear("b_in", 0, 4, projected)
            compress("k", 0)
            head_bcast("ks")
            linear("b_in", 4, 4, projected)
            compress("v", 1)
            wait_emptied(pe, "cmp_k", 1)
            dst = take("kc", 0)
            w2k = const("w2_k").rearrange("p (k c) -> p k c", k=2)
            for k in range(2):
                last = mm(dst[:, 0:32], w2k[:, k, :], cmph[:, 0, k, :], k == 0, k == 1)
            ready(last)
            pe.wait_ge(sem("cmph6"), 1)
            w2v = const("w2_v").rearrange("p (k c) -> p k c", k=2)
            for g in range(2):
                dst = take("vc", g)
                for k in range(2):
                    last = mm(dst[0:96, 0:64], cmph6[:, k, g, :, :].rearrange("p j n -> p (j n)"), w2v[:, k, :], k == 0, k == 1)
                ready(last)
            pe.wait_ge(sem("kc.squares"), 1)
            dst = take("kc.norm", 0)
            ready(mm(dst[:, 0:32], const("halfones"), krms[:, 0:32]))
            head_stat("bq")
            head_bcast("bq")
            for pair in range(4):
                wait_emptied(pe, "bq.bc", pair)
            pe.wait_ge(sem("kcmp"), 1)
            for n in range(4):
                tt, g = n // 2, n % 2
                for odd in range(2):
                    dst = take("cmp.S", 2 * n + odd)
                    half = slice(64 * odd, 64 * odd + 64)
                    for i in range(3):
                        last = mm(dst[:, 16 * i:16 * i + 16], q[half, 3 * g + i, 128 * tt:128 * tt + 128],
                                  kcmp[half, 16 * g:16 * g + 16])
                    ready(last)
            w = block_ready("gates")
            dst = take("gates", 0)
            for k in range(KD):
                last = mm(dst[0:36, 0:SEQ], w[:, k, 0:36], act32[:, k, :], k == 0, k == KD - 1)
            ready(last)
            pe.wait_ge(sem("gates.sigmoid"), 1)
            dst = take("gatesT", 0)
            for tt in range(TT):
                last = transpose(dst[:, 36 * tt:36 * tt + 36], gates[0:36, 128 * tt:128 * tt + 128])
            ready(last)
            attention("mem1")
            mem_out_transposed("mem1")
            for n in range(4):
                pe.wait_ge(sem("cmp.probs"), 1)
                ready(transpose(take("cmp.T", n)[0:96, 0:128], cmpp[:, n, :]))
            for g in range(2):
                wait_emptied(pe, "vc", g)
            for n in range(4):
                tt, g = n // 2, n % 2
                wait_emptied(pe, "cmp.T", n)
                o = OUT["cmp", tt, g]
                if o >= 2:
                    pe.wait_ge(out_emptied(("cmp", tt, g)), o // 2)
                mm(obank(("cmp", tt, g))[:, 0:384], cmppT[0:96, n, :], vbd[0:96, g, :]).then_inc(sem("out_ready"), 1)
            wait_emptied(pe, "ks.bc", 0)
            pe.wait_ge(sem("bf16_consts"), 1)
            attention("nsa")
            for n in range(4):
                tt, g = n // 2, n % 2
                pe.wait_ge(sem("nsa.o"), n + 1)
                dst = take("nsa.oT", n)
                for i in range(3):
                    c = 384 * g + 128 * i
                    last = transpose(dst[:, 128 * i:128 * i + 128], otok[:, tt, c:c + 128])
                ready(last)
            for n in range(4):
                wait_emptied(pe, "nsa.oT", n)
            for tt in range(TT):
                wait_emptied(pe, "mem1.oT", tt)
            linear("out1", 0, KD, projected)
            mlp_block(1)
            normed("smix", "s_in", projected)
            linear("s_in", 3, 5, projected)
            linear_tokens("s_in", 8, 4, projected)
            linear("s_in", 12, 2, projected)
            linear("s_lat", 0, 2, projected)
            full_stat("qlat", 2, signal=1)
            full_stat("kvlat", 1, src=sq[:, 2:3, :], signal=1)
            full_bcast("qlat")
            full_bcast("kvlat")
            wait_emptied(pe, "s_lat", 1)
            dst = take("krope.swap", 0)
            ready(mm(dst[0:96, 0:SEQ], const("swap")[64:96, :], krope[64:96, :]))

            def z_products(dst, h, stop):
                half = slice(64 * (h % 2), 64 * (h % 2) + 64)
                kk, qq = q[half, 4 + h // 2, :], q[half, h // 2, :]
                mm(dst[:, 0:256], kk[:, 0:128], qq[:, 0:256], True, stop)
                return kk, qq

            def sb_scores(h):
                dst = take("sb.Z", h)
                kk, qq = z_products(dst, h, True)
                ready(mm(dst[:, 256:384], kk[:, 128:256], qq[:, 128:256]))

            def sb_weights(h):
                pe.wait_ge(sem("sb.log_keep"), h + 1)
                dst = take("sb.W", h)
                L = sp[:, h % 2, :]
                kk, qq = z_products(dst, h, False)
                mm(dst[:, 0:256], const("negtri"), L[:, 0:256], False, False)
                mm(dst[:, 128:256], const("negones"), L[:, 256:384], False, False)
                mm(dst[:, 0:128], ident_b[:, :], sbias_b[:, :], False, True)
                mm(dst[:, 256:384], kk[:, 128:256], qq[:, 128:256], True, False)
                mm(dst[:, 256:384], const("negtri"), L[:, 256:384], False, False)
                ready(mm(dst[:, 256:384], ident_b[:, :], sbias_b[:, :], False, True))

            def sb_outputs(h):
                wait_emptied(pe, "sb.W", h)
                o = OUT["sb", h // 2]
                if h % 2 == 0 and o >= 2:
                    pe.wait_ge(out_emptied(("sb", h // 2)), o // 2)
                dst = obank(("sb", h // 2))[64 * (h % 2):64 * (h % 2) + 64, :]
                W = wt[:, h % 2, :]
                mm(dst[:, 0:256], sbv[:, 0, 64 * h:64 * h + 64], W[:, 0:256], True, False)
                last = mm(dst[:, 128:256], sbv[:, 1, 64 * h:64 * h + 64], W[:, 256:384], False, True)
                if h % 2:
                    last.then_inc(sem("out_ready"), 1)

            for t in range(8, 12):
                wait_emptied(pe, "s_in", t)
            for w_ in range(10):
                if w_ < 8:
                    sb_scores(w_)
                if 1 <= w_ <= 8:
                    sb_weights(w_ - 1)
                if w_ >= 2:
                    sb_outputs(w_ - 2)
            full_stat("sb", 4)
            wait_emptied(pe, "qlat.bc", 0)
            w = block_ready("q_up")
            for h in range(8):
                dst = take("q_up", h)
                for k in range(2):
                    last = mm(dst[0:96, 0:SEQ], w[:, k, 96 * h:96 * h + 96], latn[:, k, :], k == 0, k == 1)
                ready(last)
            for j in range(4):
                wait_emptied(pe, "q_up", 2 * j)
                wait_emptied(pe, "q_up", 2 * j + 1)
                dst = take("q.swap", j)
                for i in range(2):
                    last = mm(dst[0:96, SEQ * i:SEQ * i + SEQ], const("swap")[64:96, :], qcat[64:96, 2 * j + i, :])
                ready(last)
            wait_emptied(pe, "kvlat.bc", 0)
            w = block_ready("kv_up")
            for h in range(8):
                ready(mm(take("k_up", h)[0:64, 0:SEQ], w[:, 0, 128 * h:128 * h + 64], kvn))
            wv = w[:, 0, :].rearrange("p (h c) -> p h c", h=8)[:, :, 64:128]
            for tt in range(TT):
                ready(mm(take("v_up", tt)[:, :].rearrange("p (h c) -> p h c", h=8), kvn[:, 128 * tt:128 * tt + 128], wv))
            full_bcast("sb")
            pe.wait_ge(sem("qcat"), 4)
            pe.wait_ge(sem("kcat"), 1)
            wait_emptied(pe, "k_up", 7)
            wait_emptied(pe, "v_up", 0)
            wait_emptied(pe, "v_up", 1)
            attention("mla")
            for tt in range(TT):
                pe.wait_ge(sem("mla.o"), tt + 1)
                dst = take("mla.oT", tt)
                for i in range(4):
                    last = transpose(dst[:, 128 * i:128 * i + 128], otok[:, tt, 128 * i:128 * i + 128])
                ready(last)
            pe.wait_ge(sem("o.act"), 2)
            linear("o", 0, KD, projected)
            folded_stat("postmix")
            full_bcast("postmix")
            w = block_ready("ple")
            for t in range(KD):
                dst = take("ple", t)
                for k in range(2):
                    last = mm(dst[:, 0:SEQ], w[:, k, 128 * t:128 * t + 128], pT[:, k, :], k == 0, k == 1)
                ready(last)
            mlp("ffn", "up", "down", "ffn.hidden", UP_CHUNKS, 2, projected)
            folded_stat("postffn")
            full_bcast("postffn")
            normed("plegate", "ple_gate", projected)
            linear("ple_gate", 3, KD - 3, projected)
            folded_stat("postple")
            full_bcast("postple")

        @block.scalar
        def _(act):
            own = [0]

            def settle(ins):
                own[0] += 1
                ins.then_inc(sem("scalar_step"), 1)
                act.wait_ge(sem("scalar_step"), own[0])

            def do(dst, src, func, bias=0.0, scale=1.0, **more):
                return nc.scalar.activation(dst, src, func, bias=bias, scale=scale, **more)

            def copy(dst, src, scale=1.0):
                return nc.scalar.activation(dst, src, ACT.Copy, scale=scale)

            def root(name, n, dim):
                wait_tile(act, f"{name}.stat", 0)
                c = RC[name]
                do(smalls[:, c:c + n], bank(f"{name}.stat", 0)[:, 0:n], ACT.Sqrt, const("eps6"), 1.0 / dim)\
                    .then_inc(emptied(f"{name}.stat", 0), 1)

            root_loads = [0]

            def load_root():
                do(unused_roots[:, root_loads[0]:root_loads[0] + 1], const("eps6"), ACT.Sqrt)
                root_loads[0] += 1

            def keep_bcast(name):
                wait_tile(act, f"{name}.bc", 0)
                copy(rb[:, :], bank(f"{name}.bc", 0)[:, 0:SEQ]).then_inc(emptied(f"{name}.bc", 0), 1)

            def empty(tile, dst, src, func=ACT.Copy):
                wait_tile(act, *tile)
                return copy(dst, src).then_inc(emptied(*tile), 1)

            def pump(stage, t):
                split_high(act, WEIGHTS_OF[stage, t] + SPLIT)

            def high(dst, src, signal):
                copy(dst, src).then_inc(sem(signal), 1)

            def high_of_x(t, dst, gname, name):
                copy(dst[:, t, :], x[:, t, :], const(gname, t, 1)).then_inc(sem(f"{name}.high"), 1)

            def squares_of_x(stage, first, norm, dst, gname):
                for t in range(KD):
                    if t == KD - 3:
                        load_root()
                    wait_emptied(act, stage, first + t)
                    high_of_x(t, dst, gname, norm)
                    do(sq[:, t, :], x[:, t, :], ACT.Square).then_inc(sem(f"{norm}.squares"), 1)
                    pump(stage, first + t)

            def exponentials(kind):
                for n, u in enumerate(UNITS[kind]):
                    slot = (FIRST_UNIT[kind] + n) % 2
                    act.wait_ge(sem("negmax"), FIRST_UNIT[kind] + n + 1)
                    if n >= 2:
                        wait_tile(act, kind, "T", n - 2)
                    ps = bank(kind, "S", n)
                    for i in range(len(u.heads)):
                        c = STAT_COL[kind, n] + i
                        last = do(probs[:, slot, u.keys * i:u.keys * (i + 1)], ps[:, u.keys * i:u.keys * (i + 1)],
                                  ACT.Exp, negmax[:, c:c + 1], MLA_SCALE if kind == "mla" else QK_SCALE,
                                  accum_out=rowsum[:, c:c + 1])
                    last.then_inc(emptied(kind, "S", n), 1)

            act.dma_start(flat(x[:, :, :]), x_in).then_inc(sem("x_in"), 16)
            act.dma_start(C[:, 0:FIRST_CONSTS], consts_in[:, 0:FIRST_CONSTS]).then_inc(sem("consts_in"), 16)
            act.dma_start(flat(y[:, :, :]), mem_in).then_inc(sem("mem_in"), 16)
            act.dma_start(C[:, FIRST_CONSTS:NCONST], consts_in[:, FIRST_CONSTS:NCONST]).then_inc(sem("more_consts_in"), 16)
            act.dma_start(flat(pT[:, :, :]), p_in).then_inc(sem("p_in"), 16)
            act.dma_start(pos[:, :], pos_in).then_inc(sem("positions_in"), 16)
            act.wait_ge(sem("x_in"), 16)
            act.wait_ge(sem("consts_in"), 16)
            for t in range(KD):
                high_of_x(t, act_hi, "g_mix0", "mix0")
                if t == 3:
                    split_high(act, 0)
            split_high(act, 1)
            do(flat(sq[:, :, :]), flat(x[:, :, :]), ACT.Square).then_inc(sem("mix0.squares"), KD)
            for w in (2, 3):
                split_high(act, w)
            root("mix0", 2, 1024)
            keep_bcast("mix0")

            for c in range(CONV_TILES):
                if c >= 2:
                    act.wait_ge(sem("glu.ready"), c - 1)
                for i in range(2):
                    pump("a_in", 2 * c + i)
                wait_emptied(act, "a_in", 2 * c + 1)
                do(tmp[:, c % 2, 256:512], tmp2[:, c % 2, 256:512], ACT.Sigmoid, const("b_glu", 6 + c, 1))\
                    .then_inc(sem("glu.sigmoid"), 1)
                if c == 1:
                    act.wait_ge(sem("mem_in"), 16)
                    do(flat(sq[:, :, :]), flat(y[:, :, :]), ACT.Square).then_inc(sem("mem.squares"), 1)
                if c == 2:
                    root("mem", 2, 1024)
                if c == 4:
                    wait_emptied(act, "mem.bc", 0)
                    high(flat(hidden_hi[:, 1, :, :]), flat(y[:, :, :]), "mem.high")
            for i in range(2):
                pump("a_in", 12 + i)
            wait_emptied(act, "a_in", 12)
            wait_emptied(act, "a_in", 13)
            do(flat(sq[:, 0:2, :]), flat(y[:, 0:2, :]), ACT.Square).then_inc(sem("qm0.squares"), 1)
            root("qm0", 8, 64)
            for l in range(2):
                for t in range(2):
                    empty((f"mem_kv{l}", t), y[:, 2 + 2 * l + t, :], bank(f"mem_kv{l}", t)[:, 0:SEQ])
                    pump(f"mem_kv{l}", t)
                for t in range(2):
                    wait_emptied(act, f"mem_kv{l}", t)
                do(flat(sq[:, 0:2, :]), flat(y[:, 2 + 2 * l:4 + 2 * l, :]), ACT.Square).then_inc(sem(f"mk{l}.squares"), 1)
                for t in range(2):
                    empty((f"mem_kv{l}", 2 + t), memv[:, l, :, 128 * t:128 * t + 128],
                          bank(f"mem_kv{l}", 2 + t)[:, 0:256].rearrange("p (a c) -> p a c", a=2))
                    pump(f"mem_kv{l}", 2 + t)
                root(f"mk{l}", 8, 64)
            exponentials("mem0")

            def mem_out(kind):
                for tt in range(TT):
                    wait_tile(act, f"{kind}.oT", tt)
                    copy(act_hi[:, 6:8, 128 * tt:128 * tt + 128],
                         bank(f"{kind}.oT", tt)[:, 0:256].rearrange("p (a t) -> p a t", a=2)).then_inc(sem(f"{kind}.high"), 1)

            mem_out("mem0")
            act.wait_ge(sem("ln.centered"), CONV_TILES)
            do(flat(sq[:, 0:6, :]), flat(conv2), ACT.Square).then_inc(sem("ln.squares"), 1)
            wait_tile(act, "ln.var", 0)
            do(tmp[:, 0, 0:256], bank("ln.var", 0)[:, 0:SEQ], ACT.Sqrt, const("eps5"), 1.0 / 768)\
                .then_inc(emptied("ln.var", 0), 1)
            for c in range(CONV_TILES):
                act.wait_ge(sem("ln.scaled"), c + 1)
                for dst in (mix, act_hi):
                    last = do(dst[:, c, :], conv2[:, c, :], ACT.Silu, const("ln_b", c, 1), const("ln_g", c, 1))
                last.then_inc(sem("mixed0.high"), 1)

            def mlp(l, norm, inputs, gname):
                squares_of_x(f"out{l}", 0, f"mlp{l}", mlp_hi, f"g_mlp{l}")
                root(f"mlp{l}", 2, 1024)
                keep_bcast(f"mlp{l}")
                into, back = f"mlp_in{l}", f"mlp_out{l}"
                for n in range(len(MLP_CHUNKS) + 1):
                    if n < len(MLP_CHUNKS):
                        for t in range(KD * n, KD * n + KD):
                            wait_emptied(act, into, t)
                            do(slots2[:, t % 4, :], slots[:, t % 4, :], ACT.Square)
                            do(hidden_hi[:, n % 2, t % KD, :], slots[:, t % 4, :], ACT.Square).then_inc(sem(f"mlp{l}.high_hidden"), 1)
                            pump(into, t)
                    if 1 <= n < len(MLP_CHUNKS):
                        for t in range(KD * (n - 1), KD * n):
                            pump(back, t)
                squares_of_x(back, KD * (len(MLP_CHUNKS) - 1), norm, inputs, gname)
                root(norm, 2, 1024)
                keep_bcast(norm)

            act.wait_ge(sem("more_consts_in"), 16)
            mlp(0, "mix1", hidden_hi[:, 0, :, :], "g_kv")
            for t in range(4):
                for k in (2 * t, 2 * t + 1):
                    high_of_x(k, act_hi, "g_mix1", "queries")
                pump("kv", t)
            for t in range(2):
                wait_emptied(act, "kv", 2 + t)
            do(flat(sq[:, 0:2, :]), flat(ksraw), ACT.Square).then_inc(sem("ks.squares"), 1)

            def token_tile(tile, dst, norm):
                wait_tile(act, *tile)
                for tt in range(TT):
                    c = RC[norm] + tt
                    last = copy(dst[:, tt, :], bank(*tile)[:, 128 * tt:128 * tt + 128], rc[:, c:c + 1])
                last.then_inc(emptied(*tile), 1)
                pump(*tile)

            for t in range(2):
                token_tile(("kv", 4 + t), vsw[:, :, 128 * t:128 * t + 128], "mix1")
            root("ks", 8, 64)
            def hidden_of_compression(a, n):
                for c in range(2):
                    wait_tile(act, f"cmp_{n}", c)
                    do(cmph[:, a, c, :], bank(f"cmp_{n}", c)[:, 0:32], ACT.Gelu_apprx_tanh)\
                        .then_inc(emptied(f"cmp_{n}", c), 1)

            for t in range(KD):
                if t == 4:
                    hidden_of_compression(0, "k")
                wait_emptied(act, "b_in", t)
                last = do(sq[:, t, :], y[:, t, :], ACT.Square)
                if t == KD - 1:
                    last.then_inc(sem("bq.squares"), 1)
                pump("b_in", t)
            hidden_of_compression(1, "v")
            empty(("kc", 0), kraw, bank("kc", 0)[:, 0:32])
            wait_emptied(act, "kc", 0)
            do(krms[:, 0:32], kraw, ACT.Square).then_inc(sem("kc.squares"), 1)
            wait_tile(act, "kc.norm", 0)
            do(krms[:, 32:64], bank("kc.norm", 0)[:, 0:32], ACT.Sqrt, const("eps6"), 1.0 / 64)\
                .then_inc(emptied("kc.norm", 0), 1)
            root("bq", 32, 64)
            act.wait_ge(sem("cmp.centered"), 1)
            do(flat(cmpp), flat(cmpp), ACT.Exp).then_inc(sem("cmp.probs"), 1)
            wait_emptied(act, "gates", 0)
            do(gates[0:36, :], gates[0:36, :], ACT.Sigmoid, const("b_gate")[0:36, :]).then_inc(sem("gates.sigmoid"), 1)
            exponentials("mem1")
            mem_out("mem1")
            exponentials("nsa")
            for n in range(4):
                tt, g = n // 2, n % 2
                wait_tile(act, "nsa.oT", n)
                copy(act_hi[:, 3 * g:3 * g + 3, 128 * tt:128 * tt + 128],
                     bank("nsa.oT", n)[:, 0:384].rearrange("p (a t) -> p a t", a=3)).then_inc(sem("nsa.high"), 1)
            mlp(1, "smix", act_hi, "g_smix")
            for t in range(8):
                pump("s_in", t)
            for t in range(4):
                token_tile(("s_in", 8 + t), sbv[:, :, 128 * t:128 * t + 128], "smix")
            act.wait_ge(sem("angles"), 1)
            do(sinT, tmp2[:, 0, 0:256], ACT.Sin)
            do(cosT, tmp2[:, 0, 256:512], ACT.Sin).then_inc(sem("rope.tables"), 1)
            for t in range(2):
                pump("s_in", 12 + t)
                wait_emptied(act, "s_in", 12 + t)
            do(flat(sq[:, 0:2, :]), flat(lat[:, 0:2, :]), ACT.Square).then_inc(sem("qlat.squares"), 1)
            for t in range(2):
                pump("s_lat", t)
            wait_emptied(act, "s_lat", 0)
            do(sq[:, 2, :], lat[:, 2, :], ACT.Square).then_inc(sem("kvlat.squares"), 1)
            root("qlat", 2, 256)
            root("kvlat", 2, 128)
            for w in range(9):
                if w < 8:
                    wait_tile(act, "sb.Z", w)
                    if w >= 2:
                        act.wait_ge(sem("sb.log_keep"), w - 1)
                    zs = zt[:, w % 2, :]
                    settle(do(zs, bank("sb.Z", w)[:, 0:384], ACT.Abs))
                    settle(do(zs, zs, ACT.Exp, scale=-1.0))
                    do(zs, zs, ACT.Ln, 1.0).then_inc(sem("sb.log"), 1)
                if w >= 1:
                    wait_tile(act, "sb.W", w - 1)
                    do(wt[:, (w - 1) % 2, :], bank("sb.W", w - 1)[:, 0:384], ACT.Exp).then_inc(emptied("sb.W", w - 1), 1)
                if w >= 3 and w % 2:
                    pair = (w - 3) // 2
                    wait_out_emptied(act, ("sb", pair))
                    do(sq[:, pair, :], osb[:, pair, :], ACT.Square).then_inc(sem("sb.squares"), 1)
            wait_out_emptied(act, ("sb", 3))
            do(sq[:, 3, :], osb[:, 3, :], ACT.Square).then_inc(sem("sb.squares"), 1)
            root("sb", 2, 512)
            for h in range(8):
                empty(("q_up", h), qcat[0:96, h, :], bank("q_up", h)[0:96, 0:SEQ])
            for h in range(8):
                empty(("k_up", h), kcat[0:64, h, :], bank("k_up", h)[0:64, 0:SEQ])
            wait_emptied(act, "sb.bc", 0)
            high(flat(act_hi[:, 0:4, :]), flat(mix[:, 0:4, :]), "sb.high")
            exponentials("mla")
            for tt in range(TT):
                c = RC["mla"] + tt
                wait_out_emptied(act, ("mla", "mla", tt, 0))
                settle(do(flat(sq[:, 0:2, :]), otok[:, tt, 0:512], ACT.Square, accum_out=smalls[:, c:c + 1]))
                do(smalls[:, c + 2:c + 3], smalls[:, c:c + 1], ACT.Sqrt, const("eps6"), 1.0 / 512)\
                    .then_inc(sem("mla.root"), 1)
            for tt in range(TT):
                wait_emptied(act, "mla.oT", tt)
            high(flat(act_hi[:, 4:8, :]), flat(mix[:, 4:8, :]), "mla.high")

            def raw_outputs(stage, norm):
                for t in range(KD):
                    if t == KD - 3:
                        load_root()
                    wait_tile(act, stage, t)
                    ps = bank(stage, t)[:, 0:SEQ]
                    do(sq[:, t, :], ps, ACT.Square).then_inc(sem(f"{norm}.squares"), 1)
                    copy(y[:, t, :], ps).then_inc(emptied(stage, t), 1)
                    pump(stage, t)
                root(norm, 2, 1024)

            def squares_after(norm, after, between=None):
                keep_bcast(after)
                for t in range(KD):
                    act.wait_ge(sem(f"{after}.x"), t + 1)
                    high_of_x(t, act_hi, f"g_{norm}", norm)
                    do(sq[:, t, :], x[:, t, :], ACT.Square).then_inc(sem(f"{norm}.squares"), 1)
                    if between is not None:
                        between(t)
                    if t == 2:
                        load_root()

            raw_outputs("o", "postmix")
            squares_after("ffn", "postmix", lambda t: empty(("ple", t), q[:, t, :], bank("ple", t)[:, 0:SEQ]))
            root("ffn", 2, 1024)
            keep_bcast("ffn")

            def first_taps(c):
                for i, col in enumerate((c, UP_PAIRS + c)):
                    wait_emptied(act, "up", 2 * c + i)
                    sl = (2 * c + i) % 4
                    do(slots[:, sl, :], padded[:, sl, 2:2 + SEQ], ACT.Identity, const("conv_b", col, 1), const("conv_w", 3 * col + 2, 1))\
                        .then_inc(sem("ffn.first_taps"), 1)

            def gelu(c):
                act.wait_ge(sem("ffn.gate"), c + 1)
                do(slots2[:, c % 4, :], slots[:, (2 * c) % 4, :], ACT.Gelu_apprx_tanh).then_inc(sem("ffn.gelu"), 1)

            def high_hidden(c):
                act.wait_ge(sem("ffn.product"), c + 1)
                high(hidden_hi[:, (c // KD) % 2, c % KD, :], slots2[:, c % 4, :], "ffn.high_hidden")

            for n in range(len(UP_CHUNKS) + 1):
                if n < len(UP_CHUNKS):
                    for c in range(KD * n, KD * n + UP_CHUNKS[n]):
                        first_taps(c)
                        for i in range(2):
                            pump("up", 2 * c + i)
                        if c > KD * n:
                            high_hidden(c - 1)
                        gelu(c)
                    high_hidden(c)
                if n >= 1:
                    for t in range(KD * (n - 1), KD * n):
                        if n == len(UP_CHUNKS):
                            if t % KD == KD - 3:
                                load_root()
                            wait_emptied(act, "down", t)
                            do(sq[:, t % KD, :], y[:, t % KD, :], ACT.Square).then_inc(sem("postffn.squares"), 1)
                        pump("down", t)
            root("postffn", 2, 1024)
            squares_after("plegate", "postffn")
            root("plegate", 2, 1024)
            keep_bcast("plegate")
            for t in range(KD + 1):
                if t < KD:
                    wait_emptied(act, "ple_gate", t)
                    do(slots2[:, t % 4, :], slots[:, t % 4, :], ACT.Sigmoid, const("b_plegate", t, 1))\
                        .then_inc(sem("ple.sigmoid"), 1)
                    pump("ple_gate", t)
                if t >= 1:
                    act.wait_ge(sem("ple.gated"), t)
                    do(sq[:, t - 1, :], y[:, t - 1, :], ACT.Square).then_inc(sem("postple.squares"), 1)
            root("postple", 2, 1024)
            keep_bcast("postple")

        @block.gpsimd
        def _(pool):
            def tt_(dst, a, b, op):
                return nc.gpsimd.tensor_tensor(dst, a, b, op)

            nc.gpsimd.memset(glu[:, :, 0:PAD], 0.0).then_inc(sem("glu.padded"), 1)
            done = [0]

            def low_parts(upto):
                while done[0] < min(upto, NTILES):
                    split_low(pool, "gpsimd", done[0])
                    done[0] += 1

            low_parts(3 * SPLIT)
            pool.wait_ge(sem("more_consts_in"), 16)
            nc.gpsimd.tensor_copy(ident_b[:, :], const("ident"))
            nc.gpsimd.tensor_copy(cbias_b[:, :], const("cbias"))
            nc.gpsimd.tensor_copy(sbias_b[:, :], const("sbias")).then_inc(sem("bf16_consts"), 1)
            low_parts(WEIGHTS_OF["kv", 5] + 1)
            wait_tile(pool, "kv", 0)
            nc.gpsimd.memset(tkv[:, :, 256:272], 0.0).then_inc(sem("tkv.padded"), 1)
            low_parts(WEIGHTS_OF["s_lat", 1] + SPLIT)
            pool.wait_ge(sem("krope.rotated"), 1)
            pool.wait_ge(sem("low_gpsimd"), LOW_ENGINE[:done[0]].count("gpsimd"))
            nc.gpsimd.tensor_copy(kcat[64:96, :, :], rows(tmp[64:96, 1, 256:512], 8)).then_inc(sem("kcat"), 1)
            pool.wait_ge(sem("kcat"), 1)
            low_parts(NTILES)

        @block.vector
        def _(dve):
            own = [0]

            def step(ins):
                own[0] += 1
                ins.then_inc(sem("vector_step"), 1)

            def settle(ins=None):
                if ins is not None:
                    step(ins)
                dve.wait_ge(sem("vector_step"), own[0])

            def tt_(dst, a, b, op):
                return nc.vector.tensor_tensor(dst, a, b, op)

            def ts(dst, a, s, op, s2=None, op2=None):
                if op2 is None:
                    return nc.vector.tensor_scalar(dst, a, s, None, op)
                return nc.vector.tensor_scalar(dst, a, s, s2, op, op2)

            def stt(dst, a, s, b, op0, op1):
                return nc.vector.scalar_tensor_tensor(out=dst, in0=a, scalar=s, in1=b, op0=op0, op1=op1)

            def invert(name, n):
                wait_emptied(dve, f"{name}.stat", 0)
                c = RC[name]
                nc.vector.reciprocal(rc[:, c:c + n], smalls[:, c:c + n]).then_inc(sem(f"{name}.rc"), 1)

            def scaled(tile, dst, src, factor):
                wait_tile(dve, *tile)
                tt_(dst, src, factor, ALU.mult).then_inc(emptied(*tile), 1)

            def pump(stage, t):
                split_low(dve, "vector", WEIGHTS_OF[stage, t] + SPLIT)

            def low(dst_, src, high_, signal):
                tt_(dst_, src, high_.bitcast(F32), ALU.subtract).then_inc(sem(signal), 1)

            def low_of_x(t, hi, lo, gname, name):
                dve.wait_ge(sem(f"{name}.high"), t + 1)
                stt(lo[:, t, :], x[:, t, :], const(gname, t, 1), hi[:, t, :].bitcast(F32), ALU.mult, ALU.subtract)\
                    .then_inc(sem(f"{name}.act"), 1)

            def add_output(stage, t):
                wait_tile(dve, stage, t)
                tt_(x[:, t % KD, :], x[:, t % KD, :], bank(stage, t)[:, 0:SEQ], ALU.add).then_inc(emptied(stage, t), 1)

            def fold(name, t):
                dve.wait_ge(sem(f"{name}.squares"), t + 1)
                if t == 0:
                    return
                if t >= 2:
                    dve.wait_ge(sem("square_sum"), folded[0])
                ins = tt_(square_sum[:, :], square_sum[:, :] if t >= 2 else sq[:, 0, :], sq[:, t, :], ALU.add)
                if t == KD - 1:
                    ins.then_inc(sem(f"{name}.folded"), 1)
                else:
                    ins.then_inc(sem("square_sum"), 1)
                    folded[0] += 1

            folded = [0]

            def residual(stage, first, hi, lo, gname, name):
                for t in range(KD):
                    add_output(stage, first + t)
                    if t >= 1:
                        low_of_x(t - 1, hi, lo, gname, name)
                        fold(name, t - 1)
                        pump(stage, first + t - 1)
                low_of_x(KD - 1, hi, lo, gname, name)
                fold(name, KD - 1)
                pump(stage, first + KD - 1)

            def normed_heads(name, srcs, dsts, gs):
                for pair in range(len(srcs) // 2):
                    wait_tile(dve, f"{name}.bc", pair)
                    for k in (2 * pair, 2 * pair + 1):
                        last = stt(dsts[k], srcs[k], gs[k], bank(f"{name}.bc", pair)[:, 256 * (k % 2):256 * (k % 2) + 256],
                                   ALU.mult, ALU.mult)
                    last.then_inc(emptied(f"{name}.bc", pair), 1)

            def heads_of(ap, outs):
                v = ap.rearrange("p (h d) -> p h d", d=64)
                s = outs[1] - outs[0] if len(outs) > 1 else 1
                return v[:, outs[0]:outs[-1] + 1:s, :]

            def attention(kind, finish, between=None):
                units = UNITS[kind]
                scale = MLA_SCALE if kind == "mla" else QK_SCALE
                for w in range(len(units) + 2):
                    if w < len(units):
                        u = units[w]
                        nh, c = len(u.heads), STAT_COL[kind, w]
                        wait_tile(dve, kind, "S", w)
                        s = bank(kind, "S", w)[:, 0:nh * u.keys].rearrange("p (h k) -> p h k", h=nh)
                        settle(nc.vector.reduce_max(rowmax[:, c:c + nh], s, X_AXIS))
                        ts(negmax[:, c:c + nh], rowmax[:, c:c + nh], -scale, ALU.mult).then_inc(sem("negmax"), 1)
                    if 1 <= w <= len(units):
                        slot = (FIRST_UNIT[kind] + w - 1) % 2
                        n = len(units[w - 1].heads) * units[w - 1].keys
                        wait_tile(dve, kind, "T", w - 1)
                        nc.vector.tensor_copy(probsT[:, slot, 0:n], bank(kind, "T", w - 1)[:, 0:n])\
                            .then_inc(emptied(kind, "T", w - 1), 1)
                    if between is not None:
                        between()
                    if w >= 2 and units[w - 2].last:
                        finish(kind, units[w - 2].group)

            def group_units(kind, group):
                return [(n, u) for n, u in enumerate(UNITS[kind]) if u.group == group]

            def inverse_sums(kind, group):
                us = group_units(kind, group)
                c0 = STAT_COL[kind, us[0][0]]
                total = sum(len(u.heads) for _, u in us)
                wait_emptied(dve, kind, "S", us[-1][0])
                settle(nc.vector.reciprocal(rowinv[:, 0:total], rowsum[:, c0:c0 + total]))
                return us

            def finish_plain(kind, group):
                us = inverse_sums(kind, group)
                wait_out(dve, group)
                _, _, tt, _ = group
                ps = obank(group)
                width = 512 if kind == "mla" else 256
                c = 0
                for _, u in us:
                    nh = len(u.heads)
                    last = tt_(heads_of(otok[:, tt, 0:width], u.outs), heads_of(ps[:, 0:width], u.outs),
                               bcast(rowinv[:, c:c + nh], 64), ALU.mult)
                    c += nh
                last.then_inc(out_emptied(group), 1)
                if kind != "mla":
                    own_ready(group, kind)

            def own_ready(group, kind):
                wait_out_emptied(dve, group)
                dve.sem_inc(sem(f"{kind}.o"), 1)

            def finish_gated(kind, group):
                us = inverse_sums(kind, group)
                _, branch, tt, base = group
                b = 1 if branch == "slc" else 2
                gview = gate_tok[:, tt, :].rearrange("p (h b) -> p h b", b=3)
                c = 0
                for _, u in us:
                    nh = len(u.heads)
                    s = u.heads[1] - u.heads[0] if nh > 1 else 1
                    step(tt_(rowinv[:, c:c + nh], rowinv[:, c:c + nh], gview[:, u.heads[0]:u.heads[-1] + 1:s, b], ALU.mult))
                    c += nh
                settle()
                wait_out(dve, group)
                ps = obank(group)
                c = 0
                part = tmp[:, 0, 0:384]
                for _, u in us:
                    nh = len(u.heads)
                    last = tt_(heads_of(part, u.outs), heads_of(ps[:, 0:384], u.outs), bcast(rowinv[:, c:c + nh], 64), ALU.mult)
                    c += nh
                last.then_inc(out_emptied(group), 1)
                wait_out_emptied(dve, group)
                o = otok[:, tt, 64 * base:64 * base + 384]
                ins = tt_(o, o, part, ALU.add)
                if branch == "win":
                    ins.then_inc(sem("nsa.o"), 1)
                else:
                    settle(ins)

            for w in range(SPLIT):
                split_low(dve, "vector", w)
            dve.wait_ge(sem("consts_in"), 16)
            dve.wait_ge(sem("x_in"), 16)
            for t in range(KD):
                low_of_x(t, act_hi, act_lo, "g_mix0", "mix0")
            for t in range(KD):
                fold("mix0", t)
            invert("mix0", 2)
            wait_emptied(dve, "mix0.bc", 0)

            conv_at, conv_ready, sum_step = [0], [0], [0, 0]

            def taps(n):
                for _ in range(n):
                    c, j = divmod(conv_at[0], TAPS + 1)
                    if c >= conv_ready[0]:
                        return
                    conv_at[0] += 1
                    sums = (conv[:, c, :], conv2[:, c, :])
                    if j == TAPS:
                        dve.wait_ge(sem("vector_step"), max(sum_step))
                        tt_(sums[0], sums[0], sums[1], ALU.add).then_inc(sem("conv.done"), 1)
                        continue
                    weight = const("dw", TAPS * c + j, 1)
                    if j == 0:
                        dve.wait_ge(sem("glu.ready"), c + 1)
                        step(ts(sums[0], glu[:, c, 0:SEQ], weight, ALU.mult, const("dw_b", c, 1), ALU.add))
                    elif j == 1:
                        step(ts(sums[1], glu[:, c, 1:1 + SEQ], weight, ALU.mult))
                    else:
                        dve.wait_ge(sem("vector_step"), sum_step[j % 2])
                        step(stt(sums[j % 2], glu[:, c, j:j + SEQ], weight, sums[j % 2], ALU.mult, ALU.add))
                    sum_step[j % 2] = own[0]

            def normalise_mem(t):
                if t == 0:
                    wait_tile(dve, "mem.bc", 0)
                last = stt(y[:, t, :], y[:, t, :], const("g_mem", t, 1), bank("mem.bc", 0)[:, 0:SEQ], ALU.mult, ALU.mult)
                if t == KD - 1:
                    last.then_inc(emptied("mem.bc", 0), 1)

            def low_of_mem(half):
                dve.wait_ge(sem("mem.high"), 1)
                part = slice(4 * half, 4 * half + 4)
                low(flat(hidden_lo[:, 1, part, :]), flat(y[:, part, :]), flat(hidden_hi[:, 1, part, :]), "mem.act")

            dve.wait_ge(sem("glu.padded"), 1)
            for c in range(CONV_TILES):
                s = c % 2
                for i in range(2):
                    t = 2 * c + i
                    scaled(("a_in", t), tmp2[:, s, 256 * i:256 * i + 256], bank("a_in", t)[:, 0:SEQ], rb[:, :])
                    if t == 6:
                        invert("mem", 2)
                    if t in (8, 9):
                        for k in range(4 * (t - 8), 4 * (t - 8) + 4):
                            normalise_mem(k)
                    taps(4 if t >= 8 else 7)
                dve.wait_ge(sem("glu.sigmoid"), c + 1)
                wait_emptied(dve, "a_in", 2 * c)
                stt(glu[:, c, PAD:PAD + SEQ], tmp2[:, s, 0:256], const("b_glu", c, 1), tmp[:, s, 256:512], ALU.add, ALU.mult)\
                    .then_inc(sem("glu.ready"), 1)
                conv_ready[0] += 1
            for half in range(2):
                low_of_mem(half)
            dve.wait_ge(sem("mem.act"), 2)
            for t in range(2):
                scaled(("a_in", 12 + t), y[:, t, :], bank("a_in", 12 + t)[:, 0:SEQ], rb[:, :])
                taps(6)
            invert("qm0", 8)
            taps(24)
            normed_heads("qm0", [y[:, t, :] for t in range(2)], [q[:, t, :] for t in range(2)], [const("g_memq0")] * 2)
            for l in range(2):
                invert(f"mk{l}", 8)
                taps(24 if l == 0 else 4)
                normed_heads(f"mk{l}", [y[:, 2 + 2 * l + t, :] for t in range(2)], [memk[:, l, t, :] for t in range(2)],
                             [const(f"g_memk{l}")] * 2)
            for stage in ("a_in", "mem_kv0", "mem_kv1"):
                for t in range(14 if stage == "a_in" else 4):
                    pump(stage, t)
            attention("mem0", finish_plain, lambda: taps(6))
            taps(CONV_TILES * (TAPS + 1))

            def mem_out(kind):
                for tt in range(TT):
                    dve.wait_ge(sem(f"{kind}.high"), tt + 1)
                    part = slice(128 * tt, 128 * tt + 128)
                    tt_(act_lo[:, 6:8, part], bank(f"{kind}.oT", tt)[:, 0:256].rearrange("p (a t) -> p a t", a=2),
                        act_hi[:, 6:8, part].bitcast(F32), ALU.subtract).then_inc(emptied(f"{kind}.oT", tt), 1)

            mem_out("mem0")
            dve.wait_ge(sem("conv.done"), CONV_TILES)
            wait_tile(dve, "ln.mean", 0)
            for c in range(CONV_TILES):
                ins = stt(conv2[:, c, :], bank("ln.mean", 0)[:, 0:SEQ], -1.0 / 768, conv[:, c, :], ALU.mult, ALU.add)
                ins.then_inc(sem("ln.centered"), 1)
            dve.wait_ge(sem("ln.centered"), CONV_TILES)
            dve.sem_inc(emptied("ln.mean", 0), 1)
            wait_emptied(dve, "ln.var", 0)
            settle(nc.vector.reciprocal(tmp2[:, 0, 0:256], tmp[:, 0, 0:256]))
            for c in range(CONV_TILES):
                tt_(conv2[:, c, :], conv2[:, c, :], tmp2[:, 0, 0:256], ALU.mult).then_inc(sem("ln.scaled"), 1)
            for c in range(CONV_TILES):
                dve.wait_ge(sem("mixed0.high"), c + 1)
                low(act_lo[:, c, :], mix[:, c, :], act_hi[:, c, :], "mixed0.act")

            def mlp(l, *after):
                residual(f"out{l}", 0, mlp_hi, mlp_lo, f"g_mlp{l}", f"mlp{l}")
                invert(f"mlp{l}", 2)
                wait_emptied(dve, f"mlp{l}.bc", 0)
                into, back = f"mlp_in{l}", f"mlp_out{l}"

                def low_hidden(t):
                    n = t // KD
                    dve.wait_ge(sem(f"mlp{l}.high_hidden"), t + 1)
                    low(hidden_lo[:, n % 2, t % KD, :], slots2[:, t % 4, :], hidden_hi[:, n % 2, t % KD, :], f"mlp{l}.hidden")

                for n in range(len(MLP_CHUNKS) + 1):
                    if n < len(MLP_CHUNKS):
                        for t in range(KD * n, KD * n + KD):
                            wait_tile(dve, into, t)
                            stt(slots[:, t % 4, :], bank(into, t)[:, 0:SEQ], 0.0, rb[:, :], ALU.max, ALU.mult)\
                                .then_inc(emptied(into, t), 1)
                            pump(into, t)
                            if t >= KD * n + 2:
                                low_hidden(t - 2)
                        low_hidden(t - 1)
                        low_hidden(t)
                    if 1 <= n < len(MLP_CHUNKS):
                        for t in range(KD * (n - 1), KD * n):
                            add_output(back, t)
                            pump(back, t)
                residual(back, KD * (len(MLP_CHUNKS) - 1), *after)

            dve.wait_ge(sem("more_consts_in"), 16)
            mlp(0, hidden_hi[:, 0, :, :], hidden_lo[:, 0, :, :], "g_kv", "mix1")
            invert("mix1", 2)
            wait_emptied(dve, "mix1.bc", 0)
            for t in range(4):
                dst = tkv[:, t, 0:SEQ] if t < 2 else ksraw[:, t - 2, :]
                scaled(("kv", t), dst, bank("kv", t)[:, 0:SEQ], rb[:, :])
                pump("kv", t)
                for k in (2 * t, 2 * t + 1):
                    low_of_x(k, act_hi, act_lo, "g_mix1", "queries")
                    ts(act32[:, k, :], x[:, k, :], const("g_mix1", k, 1), ALU.mult)
            wait_tile(dve, "kv", 5)
            for t in (4, 5):
                pump("kv", t)
            dve.wait_ge(sem("tkv.padded"), 1)
            for a, n in enumerate("kv"):
                wait_emptied(dve, "kv", a)
                for g in range(2):
                    src = tkv[64 * g:64 * g + 64, a, :].rearrange("p (n s) -> p s n", s=16)
                    for par in range(2):
                        for half in range(2):
                            pe_ = const(f"pe_{n}", 16 * par + 8 * half, 8)[64 * g:64 * g + 64, :]
                            last = tt_(windows[64 * par:64 * par + 64, a, 8 * half:8 * half + 8, 16 * g:16 * g + 16],
                                       src[:, par:16:2, half:half + 16], bcast(pe_, 16), ALU.add)
                last.then_inc(sem(f"windows_{n}"), 1)
            invert("ks", 8)
            for t in range(4):
                scaled(("b_in", t), y[:, t, :], bank("b_in", t)[:, 0:SEQ], rb[:, :])
                pump("b_in", t)
            wait_tile(dve, "ks.bc", 0)
            for br in range(2):
                for g in range(2):
                    rows_ = slice(64 * g, 64 * g + 64)
                    for d in range(2):
                        last = stt(kd[64 * d:64 * d + 64, br, g, :], ksraw[rows_, br, :], const("g_k", 1 + br, 1)[rows_, :],
                                   bank("ks.bc", 0)[rows_, 256 * br:256 * br + 256], ALU.mult, ALU.mult)
            last.then_inc(emptied("ks.bc", 0), 1)
            for t in range(4, KD):
                scaled(("b_in", t), y[:, t, :], bank("b_in", t)[:, 0:SEQ], rb[:, :])
                pump("b_in", t)
            for c in range(2):
                wait_emptied(dve, "cmp_v", c)
                for g in range(2):
                    last = nc.vector.tensor_copy(cmph6[:, c, g, :, :], rows(cmph[:, 1, c, 16 * g:16 * g + 16], 6))
            last.then_inc(sem("cmph6"), 1)
            for g in range(2):
                wait_tile(dve, "vc", g)
                tt_(vbd[0:96, g, :].rearrange("p (h d) -> p h d", h=6), rows(bank("vc", g)[0:96, 0:64], 6),
                    bcast(const("headblock")[0:96, :], 64), ALU.mult).then_inc(emptied("vc", g), 1)
            wait_emptied(dve, "kc.norm", 0)
            settle(nc.vector.reciprocal(krms[:, 64:96], krms[:, 32:64]))
            stt(kcmp, kraw, const("g_k", 0, 1), krms[:, 64:96], ALU.mult, ALU.mult).then_inc(sem("kcmp"), 1)
            invert("bq", 32)
            normed_heads("bq", [y[:, t, :] for t in range(KD)], [q[:, t, :] for t in range(KD)],
                         [const("g_bq")] * 6 + [const("g_memq1")] * 2)
            for n in range(4):
                tt = n // 2
                for odd in range(2):
                    tile = ("cmp.S", 2 * n + odd)
                    wait_tile(dve, *tile)
                    dst = cmps[:, n, :].rearrange("p (h k) -> p h k", h=6)[:, odd:6:2, :]
                    stt(dst, bank(*tile)[:, 0:48].rearrange("p (h k) -> p h k", h=3), QK_SCALE,
                        rows(const("cmpbias", 16 * tt, 16), 3), ALU.mult, ALU.add).then_inc(emptied(*tile), 1)
            for odd in range(2):
                wait_emptied(dve, "cmp.S", 6 + odd)
            for n in range(4):
                for odd in range(2):
                    wait_emptied(dve, "cmp.S", 2 * n + odd)
            cs = flat(cmps).rearrange("p (h k) -> p h k", k=16)
            cp = flat(cmpp).rearrange("p (h k) -> p h k", k=16)
            cmax, csum = smalls[:, 0:24], smalls[:, 32:56]
            settle(nc.vector.reduce_max(cmax, cs, X_AXIS))
            settle(ts(cmax, cmax, -1e29, ALU.max))
            tt_(cp, cs, bcast(cmax, 16), ALU.subtract).then_inc(sem("cmp.centered"), 1)
            scaled(("gates", 0), gates[0:36, :], bank("gates", 0)[0:36, 0:SEQ], rb[0:36, :])
            wait_tile(dve, "gatesT", 0)
            settle(nc.vector.tensor_copy(flat(gate_tok[:, :, :]), bank("gatesT", 0)[:, 0:72]))
            dve.sem_inc(emptied("gatesT", 0), 1)
            attention("mem1", finish_plain)
            mem_out("mem1")
            dve.wait_ge(sem("cmp.probs"), 1)
            settle(nc.vector.reduce_sum(csum, cp, X_AXIS))
            settle(ts(csum, csum, 1e-30, ALU.max))
            settle(nc.vector.reciprocal(csum, csum))
            gates_all = flat(gate_tok[:, :, :]).rearrange("p (h b) -> p h b", b=3)
            settle(tt_(csum, csum, gates_all[:, :, 0], ALU.mult))
            for n in range(4):
                wait_tile(dve, "cmp.T", n)
                nc.vector.tensor_copy(cmppT[0:96, n, :], bank("cmp.T", n)[0:96, 0:128]).then_inc(emptied("cmp.T", n), 1)
            for n in range(4):
                tt, g = n // 2, n % 2
                wait_out(dve, ("cmp", tt, g))
                tt_(otok[:, tt, 384 * g:384 * g + 384].rearrange("p (h d) -> p h d", h=6),
                    obank(("cmp", tt, g))[:, 0:384].rearrange("p (h d) -> p h d", h=6),
                    bcast(csum[:, 6 * n:6 * n + 6], 64), ALU.mult).then_inc(out_emptied(("cmp", tt, g)), 1)
            for n in range(4):
                wait_out_emptied(dve, ("cmp", n // 2, n % 2))
            attention("nsa", finish_gated)
            for n in range(4):
                tt, g = n // 2, n % 2
                dve.wait_ge(sem("nsa.high"), n + 1)
                part = slice(128 * tt, 128 * tt + 128)
                tt_(act_lo[:, 3 * g:3 * g + 3, part], bank("nsa.oT", n)[:, 0:384].rearrange("p (a t) -> p a t", a=3),
                    act_hi[:, 3 * g:3 * g + 3, part].bitcast(F32), ALU.subtract).then_inc(emptied("nsa.oT", n), 1)
            mlp(1, act_hi, act_lo, "g_smix", "smix")
            invert("smix", 2)
            wait_emptied(dve, "smix.bc", 0)
            for t in range(4):
                wait_tile(dve, "s_in", t)
                stt(q[:, t, :], bank("s_in", t)[:, 0:SEQ], QK_SCALE, rb[:, :], ALU.mult, ALU.mult)\
                    .then_inc(emptied("s_in", t), 1)
                pump("s_in", t)
            for t in range(4, 8):
                scaled(("s_in", t), q[:, t, :], bank("s_in", t)[:, 0:SEQ], rb[:, :])
                pump("s_in", t)
            dve.wait_ge(sem("positions_in"), 16)
            f, ang, turns = tmp[:, 0, 0:256], tmp[:, 0, 256:512], tmp[:, 1, 0:256]
            sin_arg, cos_arg = tmp2[:, 0, 0:256], tmp2[:, 0, 256:512]
            two_pi = 2 * math.pi
            parts = pi_parts(two_pi)
            settle(nc.vector.tensor_copy(f, pos[:, :]))
            settle(ts(ang, f, const("invf"), ALU.mult))
            settle(ts(turns, ang, 1.0 / two_pi, ALU.mult, ROUNDER, ALU.add))
            settle(ts(turns, turns, -ROUNDER, ALU.add))
            for part in parts:
                settle(stt(ang, turns, -part, ang, ALU.mult, ALU.add))
            settle(ts(cos_arg, ang, math.pi / 2, ALU.add))
            settle(ts(f, cos_arg, math.pi, ALU.is_gt, -two_pi, ALU.mult))
            settle(tt_(cos_arg, cos_arg, f, ALU.add))
            step(ts(cos_arg, cos_arg, SIN_LIMIT, ALU.min, -SIN_LIMIT, ALU.max))
            settle()
            ts(sin_arg, ang, SIN_LIMIT, ALU.min, -SIN_LIMIT, ALU.max).then_inc(sem("angles"), 1)
            for t in range(8, 12):
                pump("s_in", t)
            for t in range(2):
                scaled(("s_in", 12 + t), lat[:, t, :], bank("s_in", 12 + t)[:, 0:SEQ], rb[:, :])
                pump("s_in", 12 + t)
            scaled(("s_lat", 0), lat[:, 2, :], bank("s_lat", 0)[:, 0:SEQ], rb[:, :])
            scaled(("s_lat", 1), krope[64:96, :], bank("s_lat", 1)[64:96, 0:SEQ], rb[64:96, :])
            for t in range(2):
                pump("s_lat", t)
            invert("qlat", 2)
            invert("kvlat", 2)
            for t in range(2):
                wait_emptied(dve, "s_in", 12 + t)
            wait_tile(dve, "qlat.bc", 0)
            for t in range(2):
                last = stt(latn[:, t, :], lat[:, t, :], const("g_qlat", t, 1), bank("qlat.bc", 0)[:, 0:SEQ], ALU.mult, ALU.mult)
            last.then_inc(emptied("qlat.bc", 0), 1)
            wait_emptied(dve, "s_lat", 0)
            wait_tile(dve, "kvlat.bc", 0)
            stt(kvn, lat[:, 2, :], const("g_kvlat"), bank("kvlat.bc", 0)[:, 0:SEQ], ALU.mult, ALU.mult)\
                .then_inc(emptied("kvlat.bc", 0), 1)
            dve.wait_ge(sem("rope.tables"), 1)
            wait_emptied(dve, "s_lat", 1)
            wait_tile(dve, "krope.swap", 0)
            step(tt_(tmp[64:96, 0, 0:256], krope[64:96, :], cosT[64:96, :], ALU.mult))
            tt_(tmp[64:96, 0, 256:512], bank("krope.swap", 0)[64:96, 0:SEQ], sinT[64:96, :], ALU.mult)\
                .then_inc(emptied("krope.swap", 0), 1)
            settle()
            wait_emptied(dve, "krope.swap", 0)
            tt_(tmp[64:96, 1, 256:512], tmp[64:96, 0, 0:256], tmp[64:96, 0, 256:512], ALU.add).then_inc(sem("krope.rotated"), 1)
            for w in range(10):
                if w < 8:
                    zs = zt[:, w % 2, :]
                    dve.wait_ge(sem("sb.log"), w + 1)
                    stt(zs, bank("sb.Z", w)[:, 0:384], 0.0, zs, ALU.max, ALU.add).then_inc(emptied("sb.Z", w), 1)
                    wait_emptied(dve, "sb.Z", w)
                    tt_(sp[:, w % 2, :], zs, const("smask"), ALU.mult).then_inc(sem("sb.log_keep"), 1)
                if w >= 3 and w % 2:
                    pair = (w - 3) // 2
                    wait_out(dve, ("sb", pair))
                    nc.vector.tensor_copy(osb[:, pair, :], obank(("sb", pair))[:, 0:SEQ]).then_inc(out_emptied(("sb", pair)), 1)
            invert("sb", 2)
            for j in range(4):
                heads = slice(2 * j, 2 * j + 2)
                a, b = (tmp2[64:96, n, :].rearrange("p (h t) -> p h t", h=2) for n in range(2))
                for i in range(2):
                    wait_emptied(dve, "q_up", 2 * j + i)
                step(tt_(a, qcat[64:96, heads, :], rows(cosT[64:96, :], 2), ALU.mult))
                wait_tile(dve, "q.swap", j)
                tt_(b, bank("q.swap", j)[64:96, :].rearrange("p (h t) -> p h t", h=2), rows(sinT[64:96, :], 2), ALU.mult)\
                    .then_inc(emptied("q.swap", j), 1)
                settle()
                wait_emptied(dve, "q.swap", j)
                tt_(qcat[64:96, heads, :], a, b, ALU.add).then_inc(sem("qcat"), 1)
                dve.wait_ge(sem("qcat"), j + 1)
            for tt in range(TT):
                wait_tile(dve, "v_up", tt)
                nc.vector.tensor_copy(vmla[:, tt, :], bank("v_up", tt)[:, :]).then_inc(emptied("v_up", tt), 1)
            wait_tile(dve, "sb.bc", 0)
            for t in range(4):
                last = stt(mix[:, t, :], osb[:, t, :], const("g_sb", t, 1), bank("sb.bc", 0)[:, 0:SEQ], ALU.mult, ALU.mult)
            last.then_inc(emptied("sb.bc", 0), 1)
            dve.wait_ge(sem("sb.high"), 1)
            low(flat(act_lo[:, 0:4, :]), flat(mix[:, 0:4, :]), flat(act_hi[:, 0:4, :]), "o.act")
            attention("mla", finish_plain)
            for tt in range(TT):
                c = RC["mla"] + tt
                dve.wait_ge(sem("mla.root"), tt + 1)
                settle(nc.vector.reciprocal(rc[:, c:c + 1], smalls[:, c + 2:c + 3]))
                ts(otok[:, tt, 0:512], otok[:, tt, 0:512], rc[:, c:c + 1], ALU.mult).then_inc(sem("mla.o"), 1)
            for tt in range(TT):
                wait_tile(dve, "mla.oT", tt)
                tt_(mix[:, 4:8, 128 * tt:128 * tt + 128], bank("mla.oT", tt)[:, :].rearrange("p (a t) -> p a t", a=4),
                    bcast(const("g_mla"), 128), ALU.mult).then_inc(emptied("mla.oT", tt), 1)
            dve.wait_ge(sem("mla.high"), 1)
            low(flat(act_lo[:, 4:8, :]), flat(mix[:, 4:8, :]), flat(act_hi[:, 4:8, :]), "o.act")

            def post_norm(name, gname, stage, after=None):
                if stage:
                    for t in range(KD):
                        wait_emptied(dve, stage, t)
                        pump(stage, t)
                wait_emptied(dve, f"{name}.bc", 0)
                for t in range(KD):
                    settle(stt(y[:, t, :], y[:, t, :], const(gname, t, 1), rb[:, :], ALU.mult, ALU.mult))
                    tt_(x[:, t, :], x[:, t, :], y[:, t, :], ALU.add)\
                        .then_inc(sem("result" if after is None else f"{name}.x"), 1)
                    if after is not None and t >= 1:
                        low_of_x(t - 1, act_hi, act_lo, f"g_{after}", after)
                        fold(after, t - 1)
                if after is not None:
                    low_of_x(KD - 1, act_hi, act_lo, f"g_{after}", after)
                    fold(after, KD - 1)

            for t in range(KD):
                fold("postmix", t)
                pump("o", t)
            invert("postmix", 2)
            post_norm("postmix", "g_postmix", None, "ffn")
            invert("ffn", 2)
            wait_emptied(dve, "ffn.bc", 0)
            settle(nc.vector.memset(padded[:, :, 0:2], 0.0))

            def hidden_product(c):
                dve.wait_ge(sem("ffn.gelu"), c + 1)
                tt_(slots2[:, c % 4, :], slots2[:, c % 4, :], slots[:, (2 * c + 1) % 4, :], ALU.mult)\
                    .then_inc(sem("ffn.product"), 1)

            def low_hidden(c):
                n = (c // KD) % 2
                dve.wait_ge(sem("ffn.high_hidden"), c + 1)
                low(hidden_lo[:, n, c % KD, :], slots2[:, c % 4, :], hidden_hi[:, n, c % KD, :], "ffn.hidden")

            def taps(c):
                for k in (1, 0):
                    for i, col in enumerate((c, UP_PAIRS + c)):
                        sl = (2 * c + i) % 4
                        if k == 1:
                            dve.wait_ge(sem("ffn.first_taps"), 2 * c + i + 1)
                        else:
                            dve.wait_ge(sem("vector_step"), own[0] - (1 - i))
                        ins = stt(slots[:, sl, :], padded[:, sl, k:k + SEQ], const("conv_w", 3 * col + k, 1), slots[:, sl, :],
                                  ALU.mult, ALU.add)
                        if k == 0 and i == 0:
                            ins.then_inc(sem("ffn.gate"), 1)
                        else:
                            step(ins)

            for n in range(len(UP_CHUNKS) + 1):
                if n < len(UP_CHUNKS):
                    first = KD * n
                    for c in range(first, first + UP_CHUNKS[n]):
                        for i in range(2):
                            sl = (2 * c + i) % 4
                            scaled(("up", 2 * c + i), padded[:, sl, 2:2 + SEQ], bank("up", 2 * c + i)[:, 0:SEQ], rb[:, :])
                        for i in range(2):
                            pump("up", 2 * c + i)
                        if c > first:
                            settle()
                            hidden_product(c - 1)
                        taps(c)
                        if c > first:
                            low_hidden(c - 1)
                    settle()
                    hidden_product(c)
                    low_hidden(c)
                if n >= 1:
                    for t in range(KD * (n - 1), KD * n):
                        wait_tile(dve, "down", t)
                        ps = bank("down", t)[:, 0:SEQ]
                        dst = y[:, t % KD, :]
                        if n == 1:
                            ins = nc.vector.tensor_copy(dst, ps)
                        else:
                            ins = tt_(dst, dst, ps, ALU.add)
                        ins.then_inc(emptied("down", t), 1)
                        if n == len(UP_CHUNKS) and t % KD:
                            fold("postffn", t % KD - 1)
                        pump("down", t)
            fold("postffn", KD - 1)
            invert("postffn", 2)
            post_norm("postffn", "g_postffn", None, "plegate")
            invert("plegate", 2)
            wait_emptied(dve, "plegate.bc", 0)
            for t in range(KD):
                wait_emptied(dve, "ple", t)
            for t in range(KD + 1):
                if t < KD:
                    scaled(("ple_gate", t), slots[:, t % 4, :], bank("ple_gate", t)[:, 0:SEQ], rb[:, :])
                    pump("ple_gate", t)
                if t >= 1:
                    dve.wait_ge(sem("ple.sigmoid"), t)
                    tt_(y[:, t - 1, :], slots2[:, (t - 1) % 4, :], q[:, t - 1, :], ALU.mult).then_inc(sem("ple.gated"), 1)
                if t >= 2:
                    fold("postple", t - 2)
            fold("postple", KD - 1)
            invert("postple", 2)
            dve.wait_ge(sem("ple.gated"), KD)
            post_norm("postple", "g_postple", None)


def _rows(a, width):
    k = a.shape[0] // 128
    return a.reshape(k, 128, width).transpose(1, 0, 2).reshape(128, k * width)


def _pack_weights(i):
    import numpy as _np

    def cols(*parts):
        return _np.concatenate(parts, axis=1)

    u = i["a_w_in"][0]
    a_pairs = [cols(u[:, 128 * c:128 * c + 128], u[:, 768 + 128 * c:896 + 128 * c]) for c in range(6)]
    kv = i["w_kv"]
    part = [kv[:, 128 * n:128 * n + 128] for n in range(6)]
    b = i["b_w_in"][0]
    s = i["w_in_2"][0]
    up = i["w_up_2"][0]
    half = up.shape[1] // 2
    krope = cols(s[:, 1792:1920], _np.zeros((1024, 64), _np.float32), s[:, 1920:1952], _np.zeros((1024, 32), _np.float32))
    full = {
        "a_in": cols(*a_pairs, u[:, 1536:1792]),
        "mem_kv0": i["w_mem_kv"][0], "mem_kv1": i["w_mem_kv"][1],
        "out0": i["w_out"][0], "out1": i["w_out"][1],
        "mlp_in0": i["w_mlp_in"][0], "mlp_in1": i["w_mlp_in"][1],
        "mlp_out0": i["w_mlp_out"][0], "mlp_out1": i["w_mlp_out"][1],
        "kv": cols(part[0], part[1], part[2], part[4], part[3], part[5]),
        "cmp_k": i["cmp_w1_k"], "cmp_v": i["cmp_w1_v"],
        "b_in": b[:, 0:1024], "gates": b[:, 1024:1060],
        "s_in": s[:, 0:1792], "s_lat": krope,
        "q_up": i["w_q_up_2"][0], "kv_up": i["w_kv_up_2"][0],
        "o": i["w_o_2"][0],
        "up": cols(*[cols(up[:, 128 * c:128 * c + 128], up[:, half + 128 * c:half + 128 * c + 128])
                     for c in range(half // 128)]),
        "down": i["w_down_2"][0], "ple": i["w_ple_2"][0], "ple_gate": i["w_ple_gate_2"][0],
    }
    out = _np.zeros((NBLOCKS, 128, BLOCK_COLS), _np.float32)
    for n, (name, r0, kts, c0, width) in enumerate(WEIGHT_BLOCKS):
        block = full[name][128 * r0:128 * (r0 + kts), c0:c0 + width]
        step = width if name in DIRECT else 128
        for c in range(0, width, step):
            out[n, :, kts * c:kts * (c + step)] = _rows(block[:, c:c + step], step)
    return out


def _pack_consts(i):
    import numpy as _np

    out = _np.zeros((128, NCONST), _np.float32)

    def put(name, a):
        a = _np.asarray(a)
        at, width = CONST_AT[name]
        out[:a.shape[0], at:at + width] = a.reshape(a.shape[0], width)

    def vec(name, a):
        put(name, a.reshape(-1, 128).T)

    def twice(a):
        return _np.concatenate([a, a], axis=0)

    for l in range(2):
        vec(f"g_mix{l}", i["norm_mix_g"][l])
        vec(f"g_mlp{l}", i["norm_mlp_g"][l])
        put(f"g_memq{l}", twice(i["mem_q_norm_g"][l])[:, None])
        put(f"g_memk{l}", twice(i["mem_k_norm_g"][l])[:, None])
    vec("g_mem", i["mem_norm_g"])
    vec("b_glu", i["a_b_glu"][0])
    put("dw", i["a_dw"][0].reshape(31, 6, 128).transpose(2, 1, 0).reshape(128, 186))
    vec("dw_b", i["a_dw_b"][0])
    vec("ln_g", i["a_ln_g"][0])
    vec("ln_b", i["a_ln_b"][0])
    vec("g_kv", i["kv_norm_g"])
    put("b_gate", i["b_gate_b"][0][:, None])
    put("g_bq", twice(i["b_q_norm_g"][0])[:, None])
    put("g_k", _np.concatenate([i["k_norm_g"].T, i["k_norm_g"].T], axis=0))
    for n in "kv":
        put(f"pe_{n}", twice(i[f"cmp_pe_{n}"].reshape(16, 2, 64).transpose(2, 1, 0).reshape(64, 32)))
        w2 = i[f"cmp_w2_{n}"].reshape(2, 128, 64).transpose(1, 0, 2)
        put(f"w2_{n}", _np.concatenate([w2, w2], axis=2) if n == "k" else w2)
    for name, key in (("g_smix", "g_pre_mix_2"), ("g_qlat", "g_q_lat_2"), ("g_kvlat", "g_kv_lat_2"),
                      ("g_sb", "g_grp_sb_2"), ("g_mla", "g_grp_mla_2"), ("g_postmix", "g_post_mix_2"),
                      ("g_ffn", "g_pre_ffn_2"), ("g_postffn", "g_post_ffn_2"), ("g_plegate", "g_ple_gate_2"),
                      ("b_plegate", "b_ple_gate_2"), ("g_postple", "g_post_ple_2"), ("conv_b", "conv_b_2")):
        vec(name, i[key][0])
    put("conv_w", i["conv_w_2"][0].reshape(3, 44, 128).transpose(2, 1, 0).reshape(128, 132))

    p = _np.arange(128)
    put("ident", (p[:, None] == p[None, :]).astype(_np.float32))
    put("ones", _np.ones((128, 128), _np.float32))
    put("headsel", (p[:, None] // 64 == _np.arange(2)[None, :]).astype(_np.float32))
    put("halfones", (p[:, None] // 64 == p[None, :] // 64).astype(_np.float32))
    swap = _np.zeros((128, 96), _np.float32)
    for m in range(32):
        swap[64 + (m + 16) % 32, 64 + m] = -1.0 if m < 16 else 1.0
    put("swap", swap)
    inv = (1.0 / (_np.float32(10000.0) ** (_np.arange(0, 32, 2, dtype=_np.float32) / _np.float32(32)))).astype(_np.float32)
    put("invf", _np.tile(inv, 8)[:, None])
    put("eps6", _np.full((128, 1), 1e-6, _np.float32))
    put("eps5", _np.full((128, 1), 1e-5, _np.float32))
    put("cbias", _np.where(p[None, :] <= p[:, None], 0.0, -1e30).astype(_np.float32))
    put("sbias", _np.where(p[:, None] < p[None, :], 0.0, -1e30).astype(_np.float32))
    strict = (p[:, None] < p[None, :]).astype(_np.float32)
    put("smask", _np.concatenate([strict, _np.ones((128, 128), _np.float32), strict], axis=1))
    put("negtri", -(p[:, None] >= p[None, :]).astype(_np.float32))
    put("negones", -_np.ones((128, 128), _np.float32))
    t = p[:, None, None] + 128 * _np.arange(2)[None, :, None]
    n = _np.arange(16)[None, None, :]
    put("cmpbias", _np.where((16 * n + 31 <= t) & (n < 15), 0.0, -1e30).astype(_np.float32))
    put("headblock", (p[:96, None] // 16 == _np.arange(6)[None, :]).astype(_np.float32))
    return out


def _transposed(a):
    n = a.shape[1] // 128
    return a.T.reshape(n, 128, a.shape[0]).transpose(1, 0, 2).reshape(128, n * a.shape[0]).copy()


def kernel(**inputs):
    import numpy as _np
    import concourse.bacc as _bacc
    from concourse import mybir as _mybir
    from concourse.bass_utils import run_bass_kernel_spmd as _run

    i = {k: _np.asarray(v) for k, v in inputs.items()}
    arrays = {
        "in_x": _transposed(i["x"][0]), "in_mem": _transposed(i["mem"][0]), "in_p": _transposed(i["p_2"][0, 0]),
        "in_positions": _np.ascontiguousarray(_np.broadcast_to(i["positions_2"], (128, SEQ))),
        "in_consts": _pack_consts(i), "in_weights": _pack_weights(i),
    }
    nc = _bacc.Bacc("TRN2", target_bir_lowering=False, num_devices=1)
    args = [nc.dram_tensor(n, a.shape, _mybir.dt.from_np(a.dtype), kind="ExternalInput").ap() for n, a in arrays.items()]
    args.append(nc.dram_tensor("out_0", [128, KD * SEQ], _mybir.dt.float32, kind="ExternalOutput").ap())
    build(nc, *args)
    r = _run(nc, [arrays], core_ids=[0])
    y = r.results[0]["out_0"].reshape(128, KD, SEQ).transpose(2, 1, 0).reshape(1, SEQ, KD * 128)
    return _np.ascontiguousarray(y)
```
